# Optimizing a Trainium2 kernel written in Bass

```python
import math
import jax, jax.numpy as jnp
from jax import lax
import numpy as np

D_MODEL = 1024
BATCH = 1
SEQ = 2048
DEPTH = 1

POOL_WIDTH = 256
POOL_GROUPS = 4
POOL_WINDOWS = (2, 4, 8, 16)
POOL_GROUP_DIM = POOL_WIDTH // POOL_GROUPS
HGRN_HEADS = 4
HGRN_DK = 64
HGRN_DV = 64
HGRN_WIDTH = HGRN_HEADS * HGRN_DV
HGRN_CHUNK = 64
MIN_F = 1e-20
CONV_WIDTH = 256
CONV_K = 3
DIFF_HEADS = 4
DIFF_DH = 64
DIFF_WIDTH = DIFF_HEADS * 2 * DIFF_DH
Q_BLOCK = 128

N_BRANCH = 4
EPS = 1e-6
NEG = -1e30

IN_SPLITS = (
    POOL_WIDTH, POOL_WIDTH,
    HGRN_HEADS * HGRN_DK, HGRN_HEADS * HGRN_DK, HGRN_WIDTH, HGRN_WIDTH,
    CONV_WIDTH, CONV_WIDTH, CONV_WIDTH, CONV_WIDTH,
    DIFF_WIDTH, DIFF_WIDTH, DIFF_WIDTH, DIFF_WIDTH,
    N_BRANCH * D_MODEL,
)
D_IN = sum(IN_SPLITS)
IN_OFFSETS = tuple(int(v) for v in np.cumsum(IN_SPLITS)[:-1])

kernel_name = "hybrid_pool_hgrn2_conv_diffattn_block"

def rmsnorm(x, g):
    xf = x.astype(jnp.float32)
    y = xf * lax.rsqrt(jnp.mean(xf * xf, axis=-1, keepdims=True) + EPS)
    return (y * g.astype(jnp.float32)).astype(x.dtype)

def pool_mixer(a, pool_w, pool_scale):
    B_, T, _ = a.shape
    af = a.astype(jnp.float32).reshape(B_, T, POOL_GROUPS, POOL_GROUP_DIM)
    cs = jnp.concatenate([jnp.zeros_like(af[:, :1]), jnp.cumsum(af, axis=1)], axis=1)
    pos = jnp.arange(T)
    outs = []
    for gi, w in enumerate(POOL_WINDOWS):
        hi = cs[:, 1:, gi]
        lo = jnp.concatenate([jnp.zeros((B_, w - 1, POOL_GROUP_DIM), jnp.float32),
                              cs[:, :T - w + 1, gi]], axis=1)
        count = jnp.minimum(pos + 1, w).astype(jnp.float32)[None, :, None]
        outs.append((hi - lo) / count - af[:, :, gi])
    pooled = jnp.stack(outs, axis=2)
    mixed = jnp.einsum('btgc,gcd->btgd', pooled, pool_w.astype(jnp.float32))
    y = mixed.reshape(B_, T, POOL_WIDTH) * pool_scale.astype(jnp.float32)
    return y.astype(a.dtype)

def hgrn2_mixer(q, zf, v, lb, norm_g):
    B_, T, _ = q.shape
    f32 = jnp.float32
    nc = T // HGRN_CHUNK
    lbf = lb.astype(f32)
    z = zf.astype(f32)
    f = lbf + (1.0 - lbf) * jax.nn.sigmoid(z)
    log_f = jnp.log(jnp.maximum(f, MIN_F))
    k = (1.0 - lbf) * jax.nn.sigmoid(-z)
    qf = jax.nn.silu(q.astype(f32))

    def to_chunks(t, d):
        return t.reshape(B_, nc, HGRN_CHUNK, HGRN_HEADS, d).transpose(1, 0, 3, 2, 4)

    xs = (to_chunks(qf, HGRN_DK), to_chunks(k, HGRN_DK),
          to_chunks(v.astype(f32), HGRN_DV), to_chunks(log_f, HGRN_DK))
    causal = jnp.tril(jnp.ones((HGRN_CHUNK, HGRN_CHUNK), bool))[:, :, None]

    def step(S, inp):
        qc, kc, vc, gc = inp
        b = jnp.cumsum(gc, axis=2)
        o_inter = jnp.einsum('bhtk,bhkv->bhtv', qc * jnp.exp(b), S)
        diff = b[:, :, :, None, :] - b[:, :, None, :, :]
        decay = jnp.exp(jnp.where(causal, diff, NEG))
        scores = jnp.einsum('bhtk,bhtsk,bhsk->bhts', qc, decay, kc)
        o = o_inter + jnp.einsum('bhts,bhsv->bhtv', scores, vc)
        b_last = b[:, :, -1:, :]
        S_new = (jnp.exp(b_last[:, :, 0, :])[..., None] * S
                 + jnp.einsum('bhsk,bhsv->bhkv', kc * jnp.exp(b_last - b), vc))
        return S_new, o

    S0 = jnp.zeros((B_, HGRN_HEADS, HGRN_DK, HGRN_DV), f32)
    _, o = lax.scan(step, S0, xs)
    o = o.transpose(1, 0, 3, 2, 4).reshape(B_, T, HGRN_HEADS, HGRN_DV)
    o = rmsnorm(o, norm_g)
    return o.reshape(B_, T, HGRN_WIDTH).astype(q.dtype)

def short_conv_mixer(u, gate_b, gate_c, conv_w):
    z = gate_c * u
    y = lax.conv_general_dilated(z, conv_w[:, None, :], window_strides=(1,),
                                 padding=[(CONV_K - 1, 0)],
                                 dimension_numbers=('NWC', 'WIO', 'NWC'),
                                 feature_group_count=CONV_WIDTH)
    return gate_b * y

def diff_attention(q, k, v, lam, norm_g, layer_idx):
    B_, T, _ = q.shape
    f32 = jnp.float32
    q = q.reshape(B_, T, DIFF_HEADS, 2, DIFF_DH)
    k = k.reshape(B_, T, DIFF_HEADS, 2, DIFF_DH)
    v = v.reshape(B_, T, DIFF_HEADS, 2 * DIFF_DH)
    lam_init = 0.8 - 0.6 * math.exp(-0.3 * layer_idx)
    lf = lam.astype(f32)
    lam_full = jnp.exp(jnp.sum(lf[0] * lf[1])) - jnp.exp(jnp.sum(lf[2] * lf[3])) + lam_init
    scale = DIFF_DH ** -0.5
    qpos = jnp.arange(Q_BLOCK)
    outs = []
    for i in range(T // Q_BLOCK):
        L = (i + 1) * Q_BLOCK
        qb = q[:, i * Q_BLOCK:L]
        s = jnp.einsum('bqhmd,bkhmd->bhmqk', qb, k[:, :L]).astype(f32) * scale
        mask = jnp.arange(L)[None, :] <= (i * Q_BLOCK + qpos)[:, None]
        p = jax.nn.softmax(jnp.where(mask, s, NEG), axis=-1)
        a = p[:, :, 0] - lam_full * p[:, :, 1]
        outs.append(jnp.einsum('bhqk,bkhe->bqhe', a.astype(v.dtype), v[:, :L]))
    o = jnp.concatenate(outs, axis=1)
    o = rmsnorm(o, norm_g) * (1.0 - lam_init)
    return o.reshape(B_, T, DIFF_WIDTH)

def setup_inputs(seed: int = 0) -> dict:
    key = jax.random.key(seed)
    ks = jax.random.split(key, 20)

    def nrm(k, shape, s):
        return jax.random.normal(k, shape, jnp.float32) * s

    D = D_MODEL
    return {
        "x": nrm(ks[0], (BATCH, SEQ, D), 1.0),
        "c": nrm(ks[1], (BATCH, D), 1.0),
        "w_ada": nrm(ks[2], (DEPTH, D, 3 * D), 0.5 * D ** -0.5),
        "b_ada": nrm(ks[3], (DEPTH, 3 * D), 0.02),
        "g_pre": 1.0 + nrm(ks[4], (DEPTH, D), 0.1),
        "g_post": 1.0 + nrm(ks[5], (DEPTH, D), 0.1),
        "w_in": nrm(ks[6], (DEPTH, D, D_IN), D ** -0.5),
        "pool_w": nrm(ks[7], (DEPTH, POOL_GROUPS, POOL_GROUP_DIM, POOL_GROUP_DIM), POOL_GROUP_DIM ** -0.5),
        "pool_scale": 1.0 + nrm(ks[8], (DEPTH, POOL_WIDTH), 0.1),
        "hgrn_lb": nrm(ks[9], (DEPTH, HGRN_HEADS * HGRN_DK), 1.0),
        "hgrn_norm": 1.0 + nrm(ks[10], (DEPTH, HGRN_DV), 0.1),
        "conv_w": nrm(ks[11], (DEPTH, CONV_K, CONV_WIDTH), CONV_K ** -0.5),
        "diff_lam": nrm(ks[12], (DEPTH, 4, DIFF_DH), 0.1),
        "diff_norm": 1.0 + nrm(ks[13], (DEPTH, 2 * DIFF_DH), 0.1),
        "w_merge_pool": nrm(ks[14], (DEPTH, POOL_WIDTH, D), POOL_WIDTH ** -0.5),
        "w_merge_hgrn": nrm(ks[15], (DEPTH, HGRN_WIDTH, D), HGRN_WIDTH ** -0.5),
        "w_merge_conv": nrm(ks[16], (DEPTH, CONV_WIDTH, D), CONV_WIDTH ** -0.5),
        "w_merge_diff": nrm(ks[17], (DEPTH, DIFF_WIDTH, D), DIFF_WIDTH ** -0.5),
        "w_out": nrm(ks[18], (DEPTH, D, D), D ** -0.5),
    }

def reference(x, c, w_ada, b_ada, g_pre, g_post, w_in, pool_w, pool_scale, hgrn_lb,
              hgrn_norm, conv_w, diff_lam, diff_norm, w_merge_pool, w_merge_hgrn,
              w_merge_conv, w_merge_diff, w_out):
    B_, T, D = x.shape
    c_act = jax.nn.silu(c)
    lb_sm = jax.nn.softmax(hgrn_lb.astype(jnp.float32), axis=0)
    lower_bounds = jnp.cumsum(lb_sm, axis=0) - lb_sm[0]
    for l in range(DEPTH):
        mod = c_act @ w_ada[l] + b_ada[l]
        shift, scale, gate = jnp.split(mod, 3, axis=-1)
        h = rmsnorm(x, g_pre[l]) * (1.0 + scale[:, None]) + shift[:, None]
        p = h @ w_in[l]
        (a_in, a_g, b_q, b_f, b_i, b_g, c_x, c_b, c_c, c_g,
         d_q, d_k, d_v, d_g, m_g) = jnp.split(p, IN_OFFSETS, axis=-1)

        y_pool = pool_mixer(a_in, pool_w[l], pool_scale[l]) * jax.nn.silu(a_g)
        y_hgrn = hgrn2_mixer(b_q, b_f, b_i, lower_bounds[l], hgrn_norm[l]) * jax.nn.silu(b_g)
        y_conv = short_conv_mixer(c_x, c_b, c_c, conv_w[l]) * jax.nn.silu(c_g)
        y_diff = diff_attention(d_q, d_k, d_v, diff_lam[l], diff_norm[l], l) * jax.nn.silu(d_g)

        gates = jax.nn.sigmoid(m_g.reshape(B_, T, N_BRANCH, D))
        merged = (gates[:, :, 0] * (y_pool @ w_merge_pool[l])
                  + gates[:, :, 1] * (y_hgrn @ w_merge_hgrn[l])
                  + gates[:, :, 2] * (y_conv @ w_merge_conv[l])
                  + gates[:, :, 3] * (y_diff @ w_merge_diff[l]))
        out = merged @ w_out[l]
        x = x + gate[:, None] * rmsnorm(out, g_post[l])
    return x


_drawn_inputs = setup_inputs


def setup_inputs(seed=0):
    import zlib

    import numpy as np

    out = dict(_drawn_inputs(seed))
    spreads = {}
    factors = {'pool_scale': 4.326, 'hgrn_norm': 3.684, 'diff_lam': 8.0, 'diff_norm': 4.211}
    for name, (base, spread) in spreads.items():
        noise = np.random.default_rng([zlib.crc32(name.encode()), seed]).standard_normal(out[name].shape)
        drawn = base * np.exp(spread * noise) if base else spread * noise
        out[name] = __import__('jax').numpy.asarray(drawn.astype(out[name].dtype))
    for name, factor in factors.items():
        out[name] = (out[name] * factor).astype(out[name].dtype)
    return out
```

```python
import numpy as np
import concourse.bass as bass
from concourse import mybir
from contextlib import ExitStack

F32 = mybir.dt.float32
F32R = mybir.dt.float32r
ACT = mybir.ActivationFunctionType
ALU = mybir.AluOpType
AX = mybir.AxisListType

P = 128
D = 1024
T = 2048
KD = D // P
TG = 512
NG = T // TG
NT = T // P
D_IN = 8704
MIX_TILES = 36
GATE_TILES = D_IN // P - MIX_TILES
PAIRS = MIX_TILES // 2
EPS = 1e-6


def project_mixer_inputs(nc, x, c, w_ada, b_ada, g_pre, w_in, ident_d, h_hi, h_lo, pT):
    with ExitStack() as ctx:
        def sb(name, shape, dt=F32):
            return ctx.enter_context(nc.sbuf_tensor(name, shape, dt))

        def sem(name):
            return ctx.enter_context(nc.semaphore(name))

        w_stage = sb("w_stage", [P, KD, 2 * P])
        w_hi = [sb(f"w_hi{j}", [P, KD, P], F32R) for j in range(2)]
        w_lo = [sb(f"w_lo{j}", [P, KD, P], F32R) for j in range(2)]
        p_out = [sb(f"p_out{j}", [P, T]) for j in range(2)]
        x_tile = [sb(f"x_tile{j}", [P, D]) for j in range(2)]
        xn_all = sb("xn_all", [P, 4, D])
        xn = [xn_all[:, j, :] for j in range(4)]
        h_tmp = [sb(f"h_tmp{j}", [P, TG]) for j in range(4)]
        ada_acc = [xn_all[:, 2 * j:2 * j + 2, :].rearrange("p a n -> p (a n)") for j in range(2)]
        square = sb("square", [P, D])
        ident = sb("ident", [P, P])
        ones = sb("ones", [P, 1])
        epsb = sb("epsb", [P, 1])
        c_col = sb("c_col", [P, KD])
        c_act = sb("c_act", [P, KD])
        c_sig = sb("c_sig", [P, KD])
        g_col = sb("g_col", [P, KD])
        b_col = sb("b_col", [P, 2 * KD])
        mod = sb("mod", [P, 2 * KD])
        sc1 = sb("sc1", [P, KD])
        gs = sb("gs", [P, KD])
        ss = sb("ss", [P, NT])
        rt = sb("rt", [P, NT])
        rstd = sb("rstd", [P, NT])
        bank = [ctx.enter_context(nc.psum_tensor(f"bankA{i}", [P, TG], F32)) for i in range(8)]

        consts_in = sem("A_consts_in")
        ones_set = sem("A_ones_set")
        ada_in = [sem(f"A_ada_in{j}") for j in range(2)]
        ada_used = sem("A_ada_used")
        c_ready = sem("A_c_ready")
        mod_summed = sem("A_mod_summed")
        mod_ready = sem("A_mod_ready")
        x_in = [sem(f"A_x_in{j}") for j in range(2)]
        squared = sem("A_squared")
        rooted = sem("A_rooted")
        inverted = sem("A_inverted")
        xn_ready = sem("A_xn_ready")
        turned = sem("A_turned")
        h_ready = sem("A_h_ready")
        hi_ready = sem("A_hi_ready")
        lo_ready = sem("A_lo_ready")
        dchain = sem("A_dchain")
        w_in_sem = sem("A_w_loaded")
        whi = sem("A_w_hi_ready")
        wlo = sem("A_w_lo_ready")
        ps_ready = sem("A_ps_ready")
        evac = sem("A_evacuated")
        stored = [sem(f"A_stored{j}") for j in range(2)]

        block = ctx.enter_context(nc.Block())
        w_v = w_in.rearrange("a (k p) n -> p (a k) n", p=P)
        ada_v = w_ada.rearrange("a (k p) n -> p (a k) n", p=P)

        @block.sync
        def _(sp):
            sp.dma_start(c_col[:, :], c.rearrange("a (k p) -> p (a k)", p=P), allow_slow_non_contiguous=True).then_inc(consts_in, 16)
            sp.dma_start(b_col[:, :], b_ada[:, 0:2 * D].rearrange("a (k p) -> p (a k)", p=P), allow_slow_non_contiguous=True).then_inc(consts_in, 16)
            sp.dma_start(g_col[:, :], g_pre.rearrange("a (k p) -> p (a k)", p=P), allow_slow_non_contiguous=True).then_inc(consts_in, 16)
            sp.dma_start(ident[:, :], ident_d).then_inc(consts_in, 16)
            for k in range(KD):
                if k >= 2:
                    sp.wait_ge(ada_used, k - 1)
                sp.dma_start(p_out[k % 2][:, :], ada_v[:, k, 0:2 * D]).then_inc(ada_in[k % 2], 16)
            for t in range(NT):
                if t >= 2:
                    sp.wait_ge(xn_ready, t - 1)
                sp.dma_start(x_tile[t % 2][:, :], x[0, t * P:(t + 1) * P, :]).then_inc(x_in[t % 2], 16)

            def load(q):
                sp.dma_start(w_stage[:, :, :], w_v[:, :, bass.ds(q * 2 * P, 2 * P)]).then_inc(w_in_sem, 16)

            def store(q, j):
                sp.wait_ge(evac, 8 * q + 4 * j + 4)
                sp.dma_start(pT[bass.ds(2 * q + j, 1), :, :].rearrange("a p t -> (a p) t"), p_out[j][:, :]).then_inc(stored[j], 16)

            load(0)
            with sp.Fori(1, PAIRS) as q:
                sp.wait_ge(whi, 2 * q)
                sp.wait_ge(wlo, 2 * q)
                load(q)
                store(q - 1, 0)
                store(q - 1, 1)
            store(PAIRS - 1, 0)
            store(PAIRS - 1, 1)
            for j in range(2):
                sp.wait_ge(stored[j], 16 * PAIRS)

        @block.gpsimd
        def _(pool):
            nc.gpsimd.memset(ones[:, :], 1.0).then_inc(ones_set, 1)
            nc.gpsimd.memset(epsb[:, :], EPS).then_inc(ones_set, 1)
            for n in range(NG * KD):
                g, k = divmod(n, KD)
                pool.wait_ge(hi_ready, n + 1)
                nc.gpsimd.tensor_tensor(h_lo[:, k, g * TG:(g + 1) * TG], h_tmp[n % 4][:, :],
                                        h_hi[:, k, g * TG:(g + 1) * TG].bitcast(F32), ALU.subtract).then_inc(lo_ready, 1)

        @block.vector
        def _(dve):
            chain = [0]

            def link(ins):
                chain[0] += 1
                ins.then_inc(dchain, 1)
                dve.wait_ge(dchain, chain[0])

            dve.wait_ge(c_ready, 1)
            link(nc.vector.tensor_tensor(c_act[:, :], c_col[:, :], c_sig[:, :], ALU.mult))
            for k in range(KD):
                dve.wait_ge(ada_in[k % 2], 16 * (k // 2 + 1))
                if k == 0:
                    ins = nc.vector.tensor_scalar(ada_acc[0], p_out[0][:, :], c_act[:, 0:1], None, ALU.mult)
                else:
                    ins = nc.vector.scalar_tensor_tensor(ada_acc[k % 2], p_out[k % 2][:, :], c_act[:, k:k + 1],
                                                         ada_acc[(k - 1) % 2], ALU.mult, ALU.add)
                ins.then_inc(ada_used, 1)
                dve.wait_ge(ada_used, k + 1)
            dve.wait_ge(mod_summed, 1)
            link(nc.vector.tensor_tensor(mod[:, :], bank[0][:, 0:2 * KD], b_col[:, :], ALU.add))
            link(nc.vector.tensor_scalar(sc1[:, :], mod[:, KD:2 * KD], 1.0, None, ALU.add))
            nc.vector.tensor_tensor(gs[:, :], sc1[:, :], g_col[:, :], ALU.mult).then_inc(mod_ready, 1)
            dve.wait_ge(mod_ready, 1)

            def norm(t):
                dve.wait_ge(rooted, t + 1)
                nc.vector.reciprocal(rstd[:, t:t + 1], rt[:, t:t + 1]).then_inc(inverted, 1)
                dve.wait_ge(inverted, t + 1)
                if t >= 4:
                    dve.wait_ge(turned, (t // 4) * KD)
                nc.vector.tensor_scalar(xn[t % 4], x_tile[t % 2][:, :], rstd[:, t:t + 1], None,
                                        ALU.mult).then_inc(xn_ready, 1)

            for t in range(4):
                norm(t)
            for g in range(NG):
                for k in range(KD):
                    n = g * KD + k
                    dve.wait_ge(turned, n + 1)
                    if n >= 4:
                        dve.wait_ge(lo_ready, n - 3)
                    nc.vector.tensor_scalar(h_tmp[n % 4][:, :], bank[k][:, :], gs[:, k:k + 1], mod[:, k:k + 1],
                                            ALU.mult, ALU.add).then_inc(h_ready, 1)
                if g + 1 < NG:
                    for t in range(4 * g + 4, 4 * g + 8):
                        norm(t)

            def split(q, j, first):
                dve.wait_ge(whi, 2 * q + j + 1)
                nc.vector.tensor_tensor(w_lo[j][:, :, :], w_stage[:, :, j * P:(j + 1) * P],
                                        w_hi[j][:, :, :].bitcast(F32), ALU.subtract).then_inc(wlo, 1)

            with dve.Fori(0, PAIRS) as q:
                for j in range(2):
                    split(q, j, False)

        @block.scalar
        def _(act):
            act.wait_ge(consts_in, 64)
            nc.scalar.activation(c_sig[:, :], c_col[:, :], ACT.Sigmoid).then_inc(c_ready, 1)
            act.wait_ge(ones_set, 2)

            def root(t):
                act.wait_ge(x_in[t % 2], 16 * (t // 2 + 1))
                nc.scalar.activation(square[:, :], x_tile[t % 2][:, :], ACT.Square,
                                     accum_out=ss[:, t:t + 1]).then_inc(squared, 1)
                act.wait_ge(squared, t + 1)
                nc.scalar.activation(rt[:, t:t + 1], ss[:, t:t + 1], ACT.Sqrt, bias=epsb[:, :],
                                     scale=1.0 / D).then_inc(rooted, 1)

            for t in range(4):
                root(t)
            for g in range(NG):
                for k in range(KD):
                    n = g * KD + k
                    act.wait_ge(h_ready, n + 1)
                    nc.scalar.activation(h_hi[:, k, g * TG:(g + 1) * TG], h_tmp[n % 4][:, :], ACT.Copy).then_inc(hi_ready, 1)
                if g + 1 < NG:
                    for t in range(4 * g + 4, 4 * g + 8):
                        root(t)

            def split(q, j, first):
                act.wait_ge(w_in_sem, 16 * (q + 1))
                if not first:
                    act.wait_ge(ps_ready, 4 * (2 * q + j - 1))
                nc.scalar.activation(w_hi[j][:, :, :], w_stage[:, :, j * P:(j + 1) * P], ACT.Copy).then_inc(whi, 1)

            def evacuate(q, j, first):
                for g in range(NG):
                    act.wait_ge(ps_ready, 8 * q + 4 * j + g + 1)
                    if not first and g == 0:
                        act.wait_ge(stored[j], 16 * q)
                    nc.scalar.activation(p_out[j][:, g * TG:(g + 1) * TG], bank[4 * j + g][:, :], ACT.Copy).then_inc(evac, 1)

            def body(q, first, last=False):
                evacuate(q, 0, first)
                if not last:
                    split(q + 1, 0, False)
                evacuate(q, 1, first)
                if not last:
                    split(q + 1, 1, False)

            split(0, 0, True)
            split(0, 1, True)
            body(0, True)
            with act.Fori(1, PAIRS - 1) as q:
                body(q, False)
            body(PAIRS - 1, False, last=True)

        @block.tensor
        def _(pe):
            pe.wait_ge(ones_set, 2)
            pe.wait_ge(ada_used, KD)
            for j in range(2 * KD):
                last = nc.tensor.matmul(bank[0][:, j:j + 1], ada_acc[(KD - 1) % 2][:, j * P:(j + 1) * P], ones[:, :],
                                        start=True, stop=True)
            last.then_inc(mod_summed, 1)
            pe.wait_ge(mod_ready, 1)
            for g in range(NG):
                pe.wait_ge(xn_ready, 4 * (g + 1))
                for k in range(KD):
                    if g:
                        pe.wait_ge(h_ready, (g - 1) * KD + k + 1)
                    for i in range(4):
                        last = nc.tensor.transpose(bank[k][:, i * P:(i + 1) * P], xn[i][:, k * P:(k + 1) * P], ident[:, :])
                    last.then_inc(turned, 1)
            pe.wait_ge(h_ready, NG * KD)
            pe.wait_ge(hi_ready, NG * KD)
            pe.wait_ge(lo_ready, NG * KD)

            def tile(q, j, first):
                pe.wait_ge(wlo, 2 * q + j + 1)
                for g in range(NG):
                    if not first:
                        pe.wait_ge(evac, 8 * (q - 1) + 4 * j + g + 1)
                    cols = slice(g * TG, (g + 1) * TG)
                    for k in range(KD):
                        nc.tensor.matmul(bank[4 * j + g][:, :], w_hi[j][:, k, :], h_hi[:, k, cols], start=(k == 0), stop=False)
                        nc.tensor.matmul(bank[4 * j + g][:, :], w_hi[j][:, k, :], h_lo[:, k, cols], start=False, stop=False)
                        last = nc.tensor.matmul(bank[4 * j + g][:, :], w_lo[j][:, k, :], h_hi[:, k, cols], start=False,
                                                stop=(k == KD - 1))
                    last.then_inc(ps_ready, 1)

            tile(0, 0, True)
            tile(0, 1, True)
            with pe.Fori(1, PAIRS) as q:
                for j in range(2):
                    tile(q, j, False)


LEVELS = (64, 32, 16, 8, 4, 2, 1)
NL = len(LEVELS) + 1
SPLIT = 2.0 ** -30
MIN_F = 1e-20
HALO_P, HALO_C = 16, 2


def gates_and_local_mixers(nc, w_in, h_hi, h_lo, pT, gT, yT, consts, hgrn_lb, hgrn_norm, conv_w, pool_w, pool_scale):
    with ExitStack() as ctx:
        def sb(name, shape, dt=F32):
            return ctx.enter_context(nc.sbuf_tensor("B_" + name, shape, dt))

        def sem(name):
            return ctx.enter_context(nc.semaphore("B_" + name))

        w_stage = sb("w_stage", [P, KD, P])
        w_hi = [sb(f"w_hi{j}", [P, KD, P], F32R) for j in range(2)]
        w_lo = [sb(f"w_lo{j}", [P, KD, P], F32R) for j in range(2)]
        g_out = [sb(f"g_out{j}", [P, TG]) for j in range(4)]
        ident = sb("ident", [P, P])
        mean_w = sb("mean_w", [P, P])
        head_m = sb("head_m", [P, P])
        masks = sb("masks", [P, NL, P], mybir.dt.uint8)
        scan_m = sb("scan_m", [P, 2 * P])
        inv_first = sb("inv_first", [P, 2, P])
        inv_count = sb("inv_count", [P, 2])
        pool_bd = sb("pool_bd", [P, 2, P])
        pool_sc = sb("pool_sc", [P, 2])
        conv_c = sb("conv_c", [P, 3, 2])
        lb_x = sb("lb_x", [P, 2])
        lb_e = sb("lb_e", [P, 2])
        lb = sb("lb", [P, 2])
        omlb = sb("omlb", [P, 2])
        norm_c = sb("norm_c", [P, 1])
        epsb = sb("epsb", [P, 1])
        in3 = sb("in3", [P, 6, P])
        g_in = sb("g_in", [P, 2, P])
        f_s = sb("f_s", [P, 2, P])
        k_s = sb("k_s", [P, 2, P])
        q_s = sb("q_s", [P, 2, P])
        f_ab = sb("f_ab", [P, 2, 2, P])
        b_s = sb("b_s", [P, 2, P])
        eb = sb("eb", [P, 2, P])
        qe = sb("qe", [P, 2, P])
        kt = sb("kt", [P, 2, P])
        X = sb("X", [P, NL, 2, P])
        QX = sb("QX", [P, NL, 2, P])
        tok = sb("tok", [P, 4, P])
        AT = sb("AT", [P, 2, 2, P])
        picks = sb("picks", [P, 2, 4, P])
        part = sb("part", [P, 2, P])
        S = sb("S", [P, 2, P])
        kvm = sb("kvm", [P, 2, P])
        osq = sb("osq", [P, 2, P])
        rs = sb("rs", [P, 2, P])
        sgate = sb("sgate", [P, 2, P])
        yh = sb("yh", [P, 2, P])
        a_in = sb("a_in", [P, 2, HALO_P + P])
        ag_in = sb("ag_in", [P, 2, P])
        s_ag = sb("s_ag", [P, 2, P])
        sum2 = sb("sum2", [P, 2, HALO_P + P])
        sum4 = sb("sum4", [P, 2, HALO_P + P])
        sum8 = sb("sum8", [P, HALO_P + P])
        win = sb("win", [P, 2, P])
        yp = sb("yp", [P, 2, P])
        c_in = sb("c_in", [P, 8, HALO_C + P])
        s_cg = sb("s_cg", [P, 2, P])
        z_s = sb("z_s", [P, 2, HALO_C + P])
        tap = sb("tap", [P, 2, P])
        acc = sb("acc", [P, 2, P])
        yc = sb("yc", [P, 2, P])
        bank = [ctx.enter_context(nc.psum_tensor(f"bankB{i}", [P, TG], F32)) for i in range(4)]
        score = ctx.enter_context(nc.psum_tensor("B_score", [P, 2, 4, P], F32))
        b6 = ctx.enter_context(nc.psum_tensor("B_b6", [P, 4, P], F32))
        b7 = ctx.enter_context(nc.psum_tensor("B_b7", [P, 4, P], F32))

        consts_in = sem("consts_in")
        zeroed = sem("zeroed")
        zeroed_v = sem("zeroed_v")
        lb_exp = sem("lb_exp")
        w_loaded = sem("w_loaded")
        whi, wlo = sem("w_hi_ready"), sem("w_lo_ready")
        ps_ready, evac = sem("ps_ready"), sem("evacuated")
        stored = [sem(f"stored{j}") for j in range(4)]
        in3_loaded, g_loaded, a_loaded, c_loaded = sem("in3_loaded"), sem("g_loaded"), sem("a_loaded"), sem("c_loaded")
        sig_ready, sigg_ready, sigac_ready = sem("sig_ready"), sem("sigg_ready"), sem("sigac_ready")
        clipped, logged, scanned, decayed, spread, xready = (sem(n) for n in ("clipped", "logged", "scanned", "decayed", "spread", "x_ready"))
        kt_ready, prep_ready = sem("kt_ready"), sem("prep_ready")
        t_done, r_done, o_done, n_done = sem("t_done"), sem("r_done"), sem("o_done"), sem("n_done")
        tok_ready, picked = sem("tok_ready"), sem("picked")
        attn_ready = sem("attn_ready")
        state_done, osq_ready, rstd_ready, fin_done = sem("state_done"), sem("osq_ready"), sem("rstd_ready"), sem("fin_done")
        pooled, sag_ready, yp_ready, yc_ready = sem("pooled"), sem("sag_ready"), sem("yp_ready"), sem("yc_ready")
        yh_stored, yp_stored, yc_stored = sem("yh_stored"), sem("yp_stored"), sem("yc_stored")
        dchain, pchain, achain = sem("dchain"), sem("pchain"), sem("achain")

        block = ctx.enter_context(nc.Block())
        w_v = w_in.rearrange("a (k p) n -> p (a k) n", p=P)
        STEPS = NT
        assert GATE_TILES == 2 * STEPS

        def loop(eng, body):
            body(0, True, False)
            with eng.Fori(1, STEPS - 1) as i:
                body(i, False, False)
            body(STEPS - 1, False, True)

        @block.sync
        def _(sp):
            n = 0
            for dst, src in ((ident, consts["ident"]), (mean_w, consts["mean_w"]), (head_m, consts["head_m"]),
                             (scan_m, consts["scan_m"])):
                sp.dma_start(dst[:, :], src).then_inc(consts_in, 16)
                n += 1
            sp.dma_start(QX[:, :, 0, :], consts["masks"]).then_inc(consts_in, 16)
            sp.dma_start(inv_first[:, :, :], consts["inv_first"]).then_inc(consts_in, 16)
            sp.dma_start(inv_count[:, :], consts["inv_count"]).then_inc(consts_in, 16)
            sp.dma_start(pool_sc[:, :], pool_scale.rearrange("a (n p) -> p (a n)", p=P), allow_slow_non_contiguous=True).then_inc(consts_in, 16)
            for k in range(3):
                sp.dma_start(conv_c[:, k, :], conv_w[0, k:k + 1, :].rearrange("a (n p) -> p (a n)", p=P),
                             allow_slow_non_contiguous=True).then_inc(consts_in, 16)
            sp.dma_start(lb_x[:, :], hgrn_lb.rearrange("a (n p) -> p (a n)", p=P), allow_slow_non_contiguous=True).then_inc(consts_in, 16)
            for h in range(2):
                sp.dma_start(norm_c[64 * h:64 * h + 64, :], hgrn_norm.rearrange("a p -> p a"), allow_slow_non_contiguous=True).then_inc(consts_in, 16)
            sp.wait_ge(zeroed, 1)
            for g in range(4):
                sp.dma_start(pool_bd[64 * (g % 2):64 * (g % 2) + 64, g // 2, 64 * (g % 2):64 * (g % 2) + 64],
                             pool_w[0, g, :, :]).then_inc(consts_in, 16)

            def fixed(value):
                return value if isinstance(value, int) else sp.snap(value)

            def load_w(col):
                sp.dma_start(w_stage[:, :, :], w_v[:, :, bass.ds(col, P)]).then_inc(w_loaded, 16)

            def load_hgrn(at):
                sp.dma_start(in3[:, :, :], pT[4:10, :, bass.ds(at, P)].rearrange("n p t -> p n t")).then_inc(in3_loaded, 16)

            def load_gate(at):
                sp.dma_start(g_in[:, :, :], pT[10:12, :, bass.ds(at, P)].rearrange("n p t -> p n t")).then_inc(g_loaded, 16)

            def load_pool_conv(at, at_p, at_c):
                if at_p is None:
                    sp.wait_ge(zeroed, 3)
                    sp.dma_start(a_in[:, :, HALO_P:], pT[0:2, :, 0:P].rearrange("n p t -> p n t")).then_inc(a_loaded, 16)
                    sp.dma_start(c_in[:, :, HALO_C:], pT[12:20, :, 0:P].rearrange("n p t -> p n t")).then_inc(c_loaded, 16)
                else:
                    sp.dma_start(a_in[:, :, :], pT[0:2, :, bass.ds(at_p, HALO_P + P)].rearrange("n p t -> p n t")).then_inc(a_loaded, 16)
                    sp.dma_start(c_in[:, :, :], pT[12:20, :, bass.ds(at_c, HALO_C + P)].rearrange("n p t -> p n t")).then_inc(c_loaded, 16)
                sp.dma_start(ag_in[:, :, :], pT[2:4, :, bass.ds(at, P)].rearrange("n p t -> p n t")).then_inc(a_loaded, 16)

            def store_gate(i, s, tile):
                sp.wait_ge(evac, 8 * i + s + 1)
                sp.dma_start(gT[bass.ds(tile, 1), :, (s % 4) * TG:(s % 4 + 1) * TG].rearrange("a p t -> (a p) t"),
                             g_out[s % 4][:, :]).then_inc(stored[s % 4], 16)

            def store_y(at, first_chunk, src, done):
                sp.dma_start(yT[first_chunk:first_chunk + 2, :, bass.ds(at, P)].rearrange("n p t -> p n t"),
                             src[:, :, :]).then_inc(done, 16)

            load_w(MIX_TILES * P)
            load_hgrn(0)
            load_pool_conv(0, None, None)
            sp.wait_ge(whi, 1)
            sp.wait_ge(wlo, 1)
            load_w((MIX_TILES + 1) * P)

            def finish_last(i, at):
                sp.wait_ge(fin_done, i)
                store_y(at, 2, yh, yh_stored)
                sp.wait_ge(yp_ready, i)
                store_y(at, 0, yp, yp_stored)

            def body(i, first, last):
                here = fixed(i * P)
                before = None if first else fixed(i * P - P)
                tiles = [fixed(2 * i), fixed(2 * i + 1)]
                if not last:
                    cols = [fixed(i * (2 * P) + (MIX_TILES + 2 + j) * P) for j in range(2)]
                    after, after_p, after_c = (fixed(i * P + (P - halo)) for halo in (0, HALO_P, HALO_C))
                    sp.wait_ge(whi, 2 * i + 2)
                    sp.wait_ge(wlo, 2 * i + 2)
                    load_w(cols[0])
                store_gate(i, 0, tiles[0])
                store_gate(i, 1, tiles[0])
                if not first:
                    finish_last(i, before)
                load_gate(here)
                store_gate(i, 2, tiles[0])
                store_gate(i, 3, tiles[0])
                if not last:
                    sp.wait_ge(whi, 2 * i + 3)
                    sp.wait_ge(wlo, 2 * i + 3)
                    load_w(cols[1])
                    sp.wait_ge(prep_ready, i + 1)
                    sp.wait_ge(t_done, i + 1)
                    load_hgrn(after)
                store_gate(i, 4, tiles[1])
                store_gate(i, 5, tiles[1])
                store_gate(i, 6, tiles[1])
                sp.wait_ge(yc_ready, i + 1)
                store_y(here, 4, yc, yc_stored)
                if not last:
                    load_pool_conv(after, after_p, after_c)
                store_gate(i, 7, tiles[1])

            loop(sp, body)
            finish_last(STEPS, (STEPS - 1) * P)
            for j in range(4):
                sp.wait_ge(stored[j], 16 * 2 * STEPS)
            sp.wait_ge(yh_stored, 16 * STEPS)
            sp.wait_ge(yp_stored, 16 * STEPS)
            sp.wait_ge(yc_stored, 16 * STEPS)

        @block.gpsimd
        def _(pool):
            chain = [0]
            base = [0]
            PER = 13

            def link(ins):
                chain[0] += 1
                ins.then_inc(pchain, 1)
                pool.wait_ge(pchain, base[0] + chain[0])

            tt = nc.gpsimd.tensor_tensor
            nc.gpsimd.memset(pool_bd[:, :, :], 0.0).then_inc(zeroed, 1)
            nc.gpsimd.memset(a_in[:, :, 0:HALO_P], 0.0).then_inc(zeroed, 1)
            nc.gpsimd.memset(c_in[:, :, 0:HALO_C], 0.0).then_inc(zeroed, 1)
            pool.wait_ge(consts_in, 16 * 18)

            def body(i, first, last):
                base[0] = PER * i
                chain[0] = 0
                pool.wait_ge(a_loaded, 32 * (i + 1))
                link(tt(sum2[:, :, 1:], a_in[:, :, 1:], a_in[:, :, :-1], ALU.add))
                link(tt(sum4[:, :, 3:], sum2[:, :, 3:], sum2[:, :, 1:-2], ALU.add))
                link(tt(sum8[:, 7:], sum4[:, 1, 7:], sum4[:, 1, 3:-4], ALU.add))
                if not first:
                    pool.wait_ge(o_done, i)
                tt(win[64:128, 1, :], sum8[64:128, HALO_P:], sum8[64:128, 8:-8], ALU.add)
                nc.gpsimd.tensor_copy(win[0:64, 0, :], sum2[0:64, 0, HALO_P:])
                nc.gpsimd.tensor_copy(win[64:128, 0, :], sum4[64:128, 0, HALO_P:])
                link(nc.gpsimd.tensor_copy(win[0:64, 1, :], sum8[0:64, HALO_P:]))
                inv = inv_first[:, :, :] if first else inv_count[:, :].unsqueeze(2).to_broadcast([P, 2, P])
                link(tt(win[:, :, :], win[:, :, :], inv, ALU.mult))
                tt(win[:, :, :], win[:, :, :], a_in[:, :, HALO_P:], ALU.subtract).then_inc(pooled, 1)
                pool.wait_ge(sigac_ready, i + 1)
                tt(s_ag[:, :, :], s_ag[:, :, :], ag_in[:, :, :], ALU.mult).then_inc(sag_ready, 1)
                pool.wait_ge(c_loaded, 16 * (i + 1))
                link(tt(z_s[:, :, :], c_in[:, 0:2, :], c_in[:, 4:6, :], ALU.mult))
                w = [conv_c[:, k, :].unsqueeze(2).to_broadcast([P, 2, P]) for k in range(3)]
                link(tt(acc[:, :, :], z_s[:, :, 2:], w[2], ALU.mult))
                link(tt(tap[:, :, :], z_s[:, :, 1:-1], w[1], ALU.mult))
                link(tt(acc[:, :, :], acc[:, :, :], tap[:, :, :], ALU.add))
                link(tt(tap[:, :, :], z_s[:, :, :-2], w[0], ALU.mult))
                link(tt(acc[:, :, :], acc[:, :, :], tap[:, :, :], ALU.add))
                link(tt(acc[:, :, :], acc[:, :, :], c_in[:, 2:4, HALO_C:], ALU.mult))
                link(tt(s_cg[:, :, :], s_cg[:, :, :], c_in[:, 6:8, HALO_C:], ALU.mult))
                if not first:
                    pool.wait_ge(yc_stored, 16 * i)
                tt(yc[:, :, :], acc[:, :, :], s_cg[:, :, :], ALU.mult).then_inc(yc_ready, 1)
                assert chain[0] == PER, chain[0]

            loop(pool, body)

        @block.vector
        def _(dve):
            chain = [0]
            base = [0]
            START, PER = 5, 13

            def link(ins):
                chain[0] += 1
                ins.then_inc(dchain, 1)
                dve.wait_ge(dchain, base[0] + chain[0])

            tt, ts, stt = nc.vector.tensor_tensor, nc.vector.tensor_scalar, nc.vector.scalar_tensor_tensor
            nc.vector.memset(S[:, :, :], 0.0).then_inc(zeroed_v, 1)
            nc.vector.memset(epsb[:, :], EPS).then_inc(zeroed_v, 1)
            nc.vector.memset(AT[:, :, :, :], 0.0).then_inc(zeroed_v, 1)
            dve.wait_ge(zeroed_v, 3)
            dve.wait_ge(consts_in, 16 * 18)
            nc.vector.tensor_copy(masks[:, :, :], QX[:, :, 0, :])
            link(tt(lb_x[:, :], lb_x[:, :], lb_x[:, :], ALU.subtract))
            dve.wait_ge(lb_exp, 1)
            link(nc.vector.reciprocal(lb[:, :], lb_e[:, :]))
            link(tt(lb[:, :], lb[:, :], lb_e[:, :], ALU.mult))
            link(tt(lb[:, :], lb[:, :], lb[:, :], ALU.subtract))
            link(ts(omlb[:, :], lb[:, :], -1.0, 1.0, ALU.mult, ALU.add))
            assert chain[0] == START

            def lo(tile, j):
                dve.wait_ge(whi, tile + 1)
                tt(w_lo[j][:, :, :], w_stage[:, :, :], w_hi[j][:, :, :].bitcast(F32), ALU.subtract).then_inc(wlo, 1)

            lo(0, 0)
            lo(1, 1)

            def advance_state(i):
                dve.wait_ge(o_done, i)
                tt(kvm[:, :, :], b7[:, 0:2, :], head_m[:, :].unsqueeze(1).to_broadcast([P, 2, P]), ALU.mult).then_inc(dchain, 1)
                chain[0] += 1
                dve.wait_ge(dchain, base[0] + chain[0])
                for t in range(2):
                    last = stt(S[:, t, :], S[:, t, :], eb[:, t, P - 1:P], kvm[:, t, :], ALU.mult, ALU.add)
                last.then_inc(state_done, 1)
                dve.wait_ge(sag_ready, i)

            def pool_out(i, second):
                dve.wait_ge(osq_ready, i)
                if not second:
                    dve.wait_ge(yp_stored, 16 * (i - 1))
                for t in range(2):
                    last = stt(yp[:, t, :], b6[:, 2 + t, :], pool_sc[:, t:t + 1], s_ag[:, t, :], ALU.mult, ALU.mult)
                last.then_inc(yp_ready, 1)

            def finish(i, second):
                dve.wait_ge(sigg_ready, i)
                link(tt(sgate[:, :, :], sgate[:, :, :], g_in[:, :, :], ALU.mult))
                dve.wait_ge(rstd_ready, i)
                link(tt(rs[:, :, :], b6[:, 0:2, :], rs[:, :, :], ALU.mult))
                if not second:
                    dve.wait_ge(yh_stored, 16 * (i - 1))
                stt(yh[:, :, :], rs[:, :, :], norm_c[:, :], sgate[:, :, :], ALU.mult, ALU.mult).then_inc(fin_done, 1)

            def body(i, first, last, second=False):
                base[0] = START + PER * i
                chain[0] = 0
                if first:
                    for _ in range(3):
                        link(nc.vector.memset(kvm[:, 0, 0:1], 0.0))
                else:
                    advance_state(i)
                    pool_out(i, second)
                dve.wait_ge(sig_ready, i + 1)
                for t in range(2):
                    ts(k_s[:, t, :], k_s[:, t, :], omlb[:, t:t + 1], None, ALU.mult)
                for t in range(2):
                    ins = ts(f_s[:, t, :], f_s[:, t, :], omlb[:, t:t + 1], lb[:, t:t + 1], ALU.mult, ALU.add)
                link(ins)
                ts(f_ab[:, 0, :, :], f_s[:, :, :], SPLIT, None, ALU.max)
                ts(f_ab[:, 1, :, :], f_s[:, :, :], MIN_F, SPLIT, ALU.max, ALU.min).then_inc(clipped, 1)
                link(tt(q_s[:, :, :], q_s[:, :, :], in3[:, 0:2, :], ALU.mult))
                dve.wait_ge(logged, i + 1)
                link(tt(f_s[:, :, :], f_ab[:, 0, :, :], f_ab[:, 1, :, :], ALU.add))
                link(nc.vector.tensor_tensor_scan(b_s[:, :, :].rearrange("p n t -> p (n t)"), scan_m[:, :],
                                                  f_s[:, :, :].rearrange("p n t -> p (n t)"), 0.0, ALU.mult, ALU.add))
                nc.vector.tensor_copy(f_s[:, 0, 0:1], b_s[:, 0, 0:1]).then_inc(scanned, 1)
                if not first:
                    dve.wait_ge(r_done, 4 * i)
                for n, m in enumerate(LEVELS):
                    v = b_s[:, :, :].rearrange("p n t -> p (n t)").rearrange("p (n u) -> p n u", u=2 * m)
                    o = X[:, n, :, :].rearrange("p n t -> p (n t)").rearrange("p (n u) -> p n u", u=2 * m)
                    ref = v[:, :, m - 1:m].to_broadcast([P, P // m, 2 * m])
                    ins = tt(o, v, ref, ALU.subtract)
                link(ins)
                flat = X[:, 0:NL - 1, :, :].rearrange("p l n t -> p (l n t)")
                stt(flat, flat, -1.0, flat, ALU.mult, ALU.min).then_inc(spread, 1)
                dve.wait_ge(decayed, i + 1)
                tt(kt[:, :, :], kt[:, :, :], k_s[:, :, :], ALU.mult).then_inc(kt_ready, 1)
                tt(qe[:, :, :], q_s[:, :, :], eb[:, :, :], ALU.mult)
                nc.vector.tensor_copy(QX[:, NL - 1, :, :], q_s[:, :, :])
                nc.vector.tensor_copy(X[:, NL - 1, :, :], k_s[:, :, :])
                dve.wait_ge(xready, i + 1)
                link(tt(QX[:, 0:NL - 1, :, :], X[:, 0:NL - 1, :, :],
                        q_s[:, :, :].unsqueeze(1).to_broadcast([P, NL - 1, 2, P]), ALU.mult))
                tt(X[:, 0:NL - 1, :, :], X[:, 0:NL - 1, :, :],
                   k_s[:, :, :].unsqueeze(1).to_broadcast([P, NL - 1, 2, P]), ALU.mult).then_inc(prep_ready, 1)
                if not first:
                    finish(i, second)
                for r in range(4):
                    dve.wait_ge(r_done, 4 * i + r + 1)
                    m = masks[:, 4 * (r % 2):4 * (r % 2) + 4, :]
                    for h in range(2):
                        ins = tt(picks[:, h, :, :], score[:, h, :, :], m, ALU.mult)
                    ins.then_inc(picked, 1)
                    dve.wait_ge(picked, 4 * i + r + 1)
                    out = AT if r % 2 == 0 else part
                    link(nc.vector.tensor_reduce(out[:, r // 2, :, :].rearrange("p h t -> p (h t)") if r % 2 == 0 else out[:, :, :].rearrange("p h t -> p (h t)"),
                                                 picks[:, :, :, :].rearrange("p h n t -> p h t n"), AX.X, ALU.add))
                    if r % 2:
                        tt(AT[:, r // 2, :, :], AT[:, r // 2, :, :], part[:, :, :], ALU.add).then_inc(attn_ready, 1)
                    if r == 0 and not last:
                        lo(2 * i + 2, 0)
                if not last:
                    lo(2 * i + 3, 1)

            body(0, True, False)
            assert chain[0] == PER
            body(1, False, False, second=True)
            assert chain[0] == PER
            with dve.Fori(2, STEPS - 1) as i:
                body(i, False, False)
            body(STEPS - 1, False, True)
            base[0] = START + PER * STEPS
            chain[0] = 0
            advance_state(STEPS)
            pool_out(STEPS, False)
            finish(STEPS, False)

        @block.scalar
        def _(act):
            chain = [0]
            base = [0]

            def link(ins):
                chain[0] += 1
                ins.then_inc(achain, 1)
                act.wait_ge(achain, base[0] + chain[0])

            a = nc.scalar.activation
            act.wait_ge(dchain, 1)
            a(lb_e[:, :], lb_x[:, :], ACT.Exp).then_inc(lb_exp, 1)

            def hi(tile, j, fresh):
                act.wait_ge(w_loaded, 16 * (tile + 1))
                if not fresh:
                    act.wait_ge(ps_ready, 4 * (tile - 1))
                a(w_hi[j][:, :, :], w_stage[:, :, :], ACT.Copy).then_inc(whi, 1)

            hi(0, 0, True)
            hi(1, 1, True)

            def evacuate(i, s, first):
                act.wait_ge(ps_ready, 8 * i + s + 1)
                if not (first and s < 4):
                    act.wait_ge(stored[s % 4], 16 * (2 * i + s // 4))
                a(g_out[s % 4][:, :], bank[s % 4][:, :], ACT.Copy).then_inc(evac, 1)

            def squares(i):
                act.wait_ge(o_done, i)
                a(osq[:, :, :], b6[:, 0:2, :], ACT.Square).then_inc(osq_ready, 1)

            def gate_sigmoid(i, second):
                act.wait_ge(g_loaded, 16 * i)
                a(sgate[:, :, :], g_in[:, :, :], ACT.Sigmoid).then_inc(sigg_ready, 1)

            def root(i):
                act.wait_ge(n_done, i)
                link(a(rs[:, :, :], b7[:, 2:4, :], ACT.Ln, bias=epsb[:, :]))
                a(rs[:, :, :], rs[:, :, :], ACT.Exp, scale=-0.5).then_inc(rstd_ready, 1)

            def body(i, first, last):
                base[0] = i - 1 if not first else 0
                chain[0] = 0
                if not first:
                    squares(i)
                act.wait_ge(in3_loaded, 16 * (i + 1))
                if not first:
                    act.wait_ge(prep_ready, i)
                a(f_s[:, :, :], in3[:, 2:4, :], ACT.Sigmoid)
                a(k_s[:, :, :], in3[:, 2:4, :], ACT.Sigmoid, scale=-1.0)
                a(q_s[:, :, :], in3[:, 0:2, :], ACT.Sigmoid).then_inc(sig_ready, 1)
                if not first:
                    act.wait_ge(yp_ready, i)
                    gate_sigmoid(i, False)
                act.wait_ge(a_loaded, 32 * (i + 1))
                a(s_ag[:, :, :], ag_in[:, :, :], ACT.Sigmoid)
                act.wait_ge(c_loaded, 16 * (i + 1))
                a(s_cg[:, :, :], c_in[:, 6:8, HALO_C:], ACT.Sigmoid).then_inc(sigac_ready, 1)
                act.preload_act_table_set("natural_log_exp_and_others")
                act.wait_ge(clipped, i + 1)
                a(f_ab[:, 0, :, :], f_ab[:, 0, :, :], ACT.Ln)
                a(f_ab[:, 1, :, :], f_ab[:, 1, :, :], ACT.Ln, scale=1.0 / SPLIT).then_inc(logged, 1)
                evacuate(i, 0, first)
                if not first:
                    root(i)
                act.wait_ge(scanned, i + 1)
                if not first:
                    act.wait_ge(state_done, i)
                a(eb[:, :, :], b_s[:, :, :], ACT.Exp)
                if not first:
                    act.wait_ge(t_done, i)
                for t in range(2):
                    ins = a(kt[:, t, :], b_s[:, t, :], ACT.Exp, bias=b_s[:, t, P - 1:P], scale=-1.0)
                ins.then_inc(decayed, 1)
                evacuate(i, 1, first)
                act.wait_ge(spread, i + 1)
                a(X[:, 0:NL - 1, :, :], X[:, 0:NL - 1, :, :], ACT.Exp).then_inc(xready, 1)
                evacuate(i, 2, first)
                evacuate(i, 3, first)
                if not last:
                    hi(2 * i + 2, 0, False)
                act.wait_ge(t_done, i + 1)
                if not first:
                    act.wait_ge(o_done, i)
                a(tok[:, :, :], b6[:, :, :], ACT.Copy).then_inc(tok_ready, 1)
                for s in range(4, 8):
                    evacuate(i, s, first)
                if not last:
                    hi(2 * i + 3, 1, False)

            loop(act, body)
            base[0] = STEPS - 1
            chain[0] = 0
            squares(STEPS)
            gate_sigmoid(STEPS, False)
            root(STEPS)

        @block.tensor
        def _(pe):
            mm = nc.tensor.matmul
            pe.wait_ge(zeroed_v, 3)
            pe.wait_ge(consts_in, 16 * 18)

            def segment(i, s, first):
                j, g = divmod(s, 4)
                if g == 0:
                    pe.wait_ge(wlo, 2 * i + j + 1)
                if not (first and j == 0):
                    pe.wait_ge(evac, 8 * i + s - 3)
                cols = slice(g * TG, (g + 1) * TG)
                for k in range(KD):
                    mm(bank[g][:, :], w_hi[j][:, k, :], h_hi[:, k, cols], start=(k == 0), stop=False)
                    mm(bank[g][:, :], w_hi[j][:, k, :], h_lo[:, k, cols], start=False, stop=False)
                    last = mm(bank[g][:, :], w_lo[j][:, k, :], h_hi[:, k, cols], start=False, stop=(k == KD - 1))
                last.then_inc(ps_ready, 1)

            def norms(i):
                pe.wait_ge(osq_ready, i)
                pe.wait_ge(state_done, i)
                mm(b7[:, 2:4, :], mean_w[:, :], osq[:, :, :], start=True, stop=True).then_inc(n_done, 1)

            def transposes(i, first):
                pe.wait_ge(kt_ready, i + 1)
                if not first:
                    pe.wait_ge(fin_done, i)
                    pe.wait_ge(yp_ready, i)
                for t in range(2):
                    nc.tensor.transpose(b6[:, t, :], in3[:, 4 + t, :], ident[:, :])
                    last = nc.tensor.transpose(b6[:, 2 + t, :], kt[:, t, :], ident[:, :])
                last.then_inc(t_done, 1)

            def scores(i, r, first):
                if r == 0:
                    pe.wait_ge(prep_ready, i + 1)
                if not (first and r == 0):
                    pe.wait_ge(picked, 4 * i + r)
                t = r // 2
                for n in range(4):
                    for h in range(2):
                        rows = slice(64 * h, 64 * h + 64)
                        last = mm(score[:, h, n, :], X[rows, 4 * (r % 2) + n, t, :], QX[rows, 4 * (r % 2) + n, t, :],
                                  start=True, stop=True)
                last.then_inc(r_done, 1)

            def outputs(i, first):
                pe.wait_ge(attn_ready, 2 * i + 2)
                pe.wait_ge(tok_ready, i + 1)
                pe.wait_ge(pooled, i + 1)
                if not first:
                    pe.wait_ge(state_done, i)
                for t in range(2):
                    mm(b6[:, t, :], S[:, t, :], qe[:, t, :], start=True, stop=False, skip_group_check=True)
                    for h in range(2):
                        mm(b6[64 * h:64 * h + 64, t, :], tok[:, t, 64 * h:64 * h + 64], AT[:, t, h, :], start=False, stop=True,
                           skip_group_check=True)
                for t in range(2):
                    mm(b6[:, 2 + t, :], pool_bd[:, t, :], win[:, t, :], start=True, stop=True, skip_group_check=True)
                for t in range(2):
                    last = mm(b7[:, t, :], tok[:, 2 + t, :], tok[:, t, :], start=True, stop=True)
                last.then_inc(o_done, 1)

            def body(i, first, last):
                segment(i, 0, first)
                if not first:
                    norms(i)
                segment(i, 1, first)
                segment(i, 2, first)
                segment(i, 3, first)
                transposes(i, first)
                scores(i, 0, first)
                segment(i, 4, first)
                scores(i, 1, first)
                segment(i, 5, first)
                scores(i, 2, first)
                segment(i, 6, first)
                scores(i, 3, first)
                segment(i, 7, first)
                outputs(i, first)

            loop(pe, body)
            norms(STEPS)


HEADS = 4
DH = 64
LAM_INIT = 0.8 - 0.6 * float(np.exp(-0.3 * 0))
NEG = -1e30


def differential_attention(nc, pT, yT, consts, diff_lam, diff_norm, c, w_ada, b_ada, g_post, post):
    with ExitStack() as ctx:
        def sb(name, shape, dt=F32):
            return ctx.enter_context(nc.sbuf_tensor("C_" + name, shape, dt))

        def sem(name):
            return ctx.enter_context(nc.semaphore("C_" + name))

        q_in = sb("q_in", [P, 2, T])
        k_in = sb("k_in", [P, 2, T])
        v_in = sb("v_in", [P, T])
        g_in = sb("g_in", [P, T])
        g_sig = sb("g_sig", [P, T])
        ks = sb("ks", [P, 2, T], F32R)
        q_hi = sb("q_hi", [P, 2, T], F32R)
        q_lo = sb("q_lo", [P, 2, T], F32R)
        v_tok = sb("v_tok", [P, NT, P])
        prob = [sb(f"prob{j}", [P, 2, T]) for j in range(3)]
        at = [sb(f"at{j}", [P, NT, P]) for j in range(2)]
        on = sb("on", [P, P])
        junk = sb("junk", [P, P])
        y_out = sb("y_out", [P, 2, P])
        ident = sb("ident", [P, P])
        ident_r = sb("ident_r", [P, P], F32R)
        causal = sb("causal", [P, P])
        causal_r = sb("causal_r", [P, P], F32R)
        lam_in = sb("lam_in", [P, 4, DH])
        lam_p = sb("lam_p", [P, 2, DH])
        lam_s = sb("lam_s", [P, 2])
        nlam = sb("nlam", [P, 1])
        norm_c = sb("norm_c", [P, 1])
        epsb = sb("epsb", [P, 1])
        negm = [sb(f"negm{j}", [P, 2, 4]) for j in range(2)]
        sums = [sb(f"sums{j}", [P, 2, 4]) for j in range(2)]
        nm = sb("nm", [P, 2])
        dist = sb("dist", [P, 2, 4])
        wts = sb("wts", [P, 2, 4])
        wsum = sb("wsum", [P, 2, 4])
        tot = sb("tot", [P, 2])
        inv = sb("inv", [P, 2])
        cf = sb("cf", [P, 2, 4])
        ssq = sb("ssq", [P, 1])
        rstd = sb("rstd", [P, 1])
        c_col = sb("c_col", [P, KD])
        c_act = sb("c_act", [P, KD])
        ada_in = [sb(f"ada_in{j}", [P, D]) for j in range(2)]
        ada_p = sb("ada_p", [P, D])
        ada_sum = sb("ada_sum", [P, D])
        ada_b = sb("ada_b", [P, D])
        g_row = sb("g_row", [P, D])
        ones = sb("ones", [P, P])
        sc = [ctx.enter_context(nc.psum_tensor(f"C_sc{j}", [P, 2, TG], F32)) for j in range(2)]
        tb = [ctx.enter_context(nc.psum_tensor(f"C_tb{j}", [P, 4, P], F32)) for j in range(2)]
        ob = ctx.enter_context(nc.psum_tensor("C_ob", [P, TG], F32))
        otb = ctx.enter_context(nc.psum_tensor("C_otb", [P, TG], F32))

        consts_in, setup, setup_v = sem("consts_in"), sem("setup"), sem("setup_v")
        qk_loaded, v_loaded, g_loaded = sem("qk_loaded"), sem("v_loaded"), sem("g_loaded")
        hi_ready, lo_ready, vt_ready, v_ready = sem("hi_ready"), sem("lo_ready"), sem("vt_ready"), sem("v_ready")
        gsig_ready, gs_ready = sem("gsig_ready"), sem("gs_ready")
        s_ready, max_ready, exp_done = sem("s_ready"), sem("max_ready"), sem("exp_done")
        d_ready, w_ready, a_ready = sem("d_ready"), sem("w_ready"), sem("a_ready")
        t_ready, at_ready = sem("t_ready"), sem("at_ready")
        pv_done, rstd_ready, on_ready, ot_ready, y_ready = (sem(n) for n in ("pv_done", "rstd_ready", "on_ready", "ot_ready", "y_ready"))
        y_stored = [sem(f"y_stored{j}") for j in range(2)]
        dchain, achain, c_done = sem("dchain"), sem("achain"), sem("c_done")
        c_sig, ones_set, pchain = sem("c_sig"), sem("ones_set"), sem("pchain")
        ada_loaded, rows_loaded, ada_used = [sem(f"ada_loaded{j}") for j in range(2)], sem("rows_loaded"), sem("ada_used")
        gate_ready, post_ready = sem("gate_ready"), sem("post_ready")

        block = ctx.enter_context(nc.Block())
        U = NT
        pieces = [(u + 4) // 4 for u in range(U)]
        before = [sum(pieces[:u]) for u in range(U + 1)]
        NP = before[U]
        multi_before = [sum(p > 1 for p in pieces[:u]) for u in range(U + 1)]
        multi = multi_before[U]

        def width(u, p):
            return min(TG, (u + 1) * P - p * TG)

        @block.sync
        def _(sp):
            sp.dma_start(ident[:, :], consts["ident"]).then_inc(consts_in, 16)
            sp.dma_start(causal[:, :], consts["causal"]).then_inc(consts_in, 16)
            sp.dma_start(c_col[:, :], c.rearrange("a (k p) -> p (a k)", p=P), allow_slow_non_contiguous=True).then_inc(consts_in, 16)
            sp.dma_start(lam_in[:, :, :].rearrange("p a d -> p (a d)"),
                         diff_lam.rearrange("a l d -> a (l d)").to_broadcast([P, 4 * DH])).then_inc(consts_in, 16)
            sp.dma_start(norm_c[:, :], diff_norm.rearrange("a p -> p a"), allow_slow_non_contiguous=True).then_inc(consts_in, 16)

            def load(h):
                tiles = [h + 20, h + 24, h + 28, h + 32] if isinstance(h, int) else [sp.snap(h + n) for n in (20, 24, 28, 32)]
                if not isinstance(h, int):
                    sp.wait_ge(lo_ready, 4 * h)
                for m in range(2):
                    for half in range(2):
                        rows = slice(DH * half, DH * half + DH)
                        sp.dma_start(k_in[rows, m, :], pT[bass.ds(tiles[1], 1), DH * m:DH * m + DH, :].rearrange("a p t -> (a p) t")).then_inc(qk_loaded, 16)
                        sp.dma_start(q_in[rows, m, :], pT[bass.ds(tiles[0], 1), DH * m:DH * m + DH, :].rearrange("a p t -> (a p) t")).then_inc(qk_loaded, 16)
                if not isinstance(h, int):
                    sp.wait_ge(vt_ready, 4 * h)
                sp.dma_start(v_in[:, :], pT[bass.ds(tiles[2], 1), :, :].rearrange("a p t -> (a p) t")).then_inc(v_loaded, 16)
                if not isinstance(h, int):
                    sp.wait_ge(gs_ready, h)
                sp.dma_start(g_in[:, :], pT[bass.ds(tiles[3], 1), :, :].rearrange("a p t -> (a p) t")).then_inc(g_loaded, 16)

            def store(h, u, tile):
                sp.wait_ge(y_ready, U * h + u + 1)
                sp.dma_start(yT[bass.ds(tile, 1), :, u * P:(u + 1) * P].rearrange("a p t -> (a p) t"),
                             y_out[:, u % 2, :]).then_inc(y_stored[u % 2], 16)

            load(0)
            sp.dma_start(ada_b[:, :], b_ada[:, 2 * D:3 * D].to_broadcast([P, D])).then_inc(rows_loaded, 16)
            sp.dma_start(g_row[:, :], g_post.to_broadcast([P, D])).then_inc(rows_loaded, 16)
            ada_v = w_ada.rearrange("a (k p) n -> p (a k) n", p=P)
            for k in range(2):
                sp.dma_start(ada_in[k][:, :], ada_v[:, k, 2 * D:3 * D]).then_inc(ada_loaded[k], 16)
            with sp.Fori(0, HEADS - 1) as h:
                tile = sp.snap(h + 6)
                load(sp.snap(h + 1))
                for u in range(U):
                    store(h, u, tile)
            for u in range(U):
                store(HEADS - 1, u, HEADS + 5)
                if 2 <= u + 2 < KD:
                    sp.wait_ge(ada_used, u + 1)
                    sp.dma_start(ada_in[u % 2][:, :], ada_v[:, u + 2, 2 * D:3 * D]).then_inc(ada_loaded[u % 2], 16)
            for j in range(2):
                sp.wait_ge(y_stored[j], 16 * HEADS * U // 2)

        @block.gpsimd
        def _(pool):
            with pool.Fori(0, HEADS) as h:
                pool.wait_ge(gsig_ready, h + 1)
                nc.gpsimd.tensor_tensor(g_sig[:, :], g_sig[:, :], g_in[:, :], ALU.mult).then_inc(gs_ready, 1)
            chain = [0]

            def link(ins):
                chain[0] += 1
                ins.then_inc(pchain, 1)
                pool.wait_ge(pchain, chain[0])

            pool.wait_ge(c_sig, 1)
            link(nc.gpsimd.tensor_tensor(c_act[:, :], c_act[:, :], c_col[:, :], ALU.mult))
            link(nc.gpsimd.memset(ada_sum[:, :], 0.0))
            nc.gpsimd.memset(ones[:, :], 1.0).then_inc(ones_set, 1)
            for k in range(KD):
                pool.wait_ge(ada_loaded[k % 2], 16 * (k // 2 + 1))
                nc.gpsimd.tensor_scalar(ada_p[:, :], ada_in[k % 2][:, :], c_act[:, k:k + 1], None, ALU.mult).then_inc(ada_used, 1)
                pool.wait_ge(ada_used, k + 1)
                link(nc.gpsimd.tensor_tensor(ada_sum[:, :], ada_sum[:, :], ada_p[:, :], ALU.add))

        @block.vector
        def _(dve):
            chain = [0]
            base = [0]
            START = 5
            PER = 5 * sum(p > 1 for p in pieces) + NP

            def link(ins):
                chain[0] += 1
                ins.then_inc(dchain, 1)
                dve.wait_ge(dchain, base[0] + chain[0])

            tt, ts, stt = nc.vector.tensor_tensor, nc.vector.tensor_scalar, nc.vector.scalar_tensor_tensor
            nc.vector.memset(epsb[:, :], EPS).then_inc(setup_v, 1)
            dve.wait_ge(consts_in, 80)
            nc.vector.tensor_copy(ident_r[:, :], ident[:, :]).then_inc(setup_v, 1)
            nc.vector.tensor_copy(causal_r[:, :], causal[:, :]).then_inc(setup_v, 1)
            lv = lam_in[:, :, :].rearrange("p (a b) d -> p a b d", b=2)
            link(tt(lam_p[:, :, :], lv[:, :, 0, :], lv[:, :, 1, :], ALU.mult))
            nc.vector.tensor_reduce(lam_s[:, :], lam_p[:, :, :], AX.X, ALU.add).then_inc(setup_v, 1)
            dve.wait_ge(setup, 1)
            link(tt(nlam[:, :], lam_s[:, 1:2], lam_s[:, 0:1], ALU.subtract))
            link(ts(nlam[:, :], nlam[:, :], -LAM_INIT, None, ALU.add))
            link(ts(norm_c[:, :], norm_c[:, :], 1.0 - LAM_INIT, None, ALU.mult))
            link(nc.vector.memset(junk[:, 0:1], 0.0))
            assert chain[0] == START

            def maximum(h, u, p):
                n = before[u] + p
                w = width(u, p)
                dve.wait_ge(s_ready, NP * h + n + 1)
                nc.vector.tensor_reduce(negm[u % 2][:, :, p:p + 1], sc[n % 2][:, :, 0:w], AX.X, ALU.max,
                                        negate=True).then_inc(max_ready, 1)

            def weights(h, u):
                np_ = pieces[u]
                dve.wait_ge(a_ready, U * h + u)
                sm, ng = sums[u % 2], negm[u % 2]
                if np_ > 1:
                    link(nc.vector.tensor_reduce(nm[:, :], ng[:, :, 0:np_], AX.X, ALU.min))
                    tt(dist[:, :, 0:np_], ng[:, :, 0:np_], nm[:, :].unsqueeze(2).to_broadcast([P, 2, np_]),
                       ALU.subtract).then_inc(d_ready, 1)
                    dve.wait_ge(exp_done, NP * h + before[u] + np_)
                    dve.wait_ge(w_ready, multi * h + multi_before[u] + 1)
                    link(tt(wsum[:, :, 0:np_], wts[:, :, 0:np_], sm[:, :, 0:np_], ALU.mult))
                    link(nc.vector.tensor_reduce(tot[:, :], wsum[:, :, 0:np_], AX.X, ALU.add))
                    link(nc.vector.reciprocal(inv[:, :], tot[:, :]))
                    link(tt(cf[:, :, 0:np_], wts[:, :, 0:np_], inv[:, :].unsqueeze(2).to_broadcast([P, 2, np_]), ALU.mult))
                else:
                    dve.wait_ge(exp_done, NP * h + before[u] + 1)
                    nc.vector.reciprocal(cf[:, :, 0:1], sm[:, :, 0:1]).then_inc(c_done, 1)
                    dve.wait_ge(c_done, 4 * h + u + 1)

            def combine(h, u, p):
                keys = slice(p * TG, p * TG + width(u, p))
                pr = prob[u % 3]
                link(ts(pr[:, 1, keys], pr[:, 1, keys], cf[:, 1, p:p + 1], nlam[:, :], ALU.mult, ALU.mult))
                ins = stt(pr[:, 0, keys], pr[:, 0, keys], cf[:, 0, p:p + 1], pr[:, 1, keys], ALU.mult, ALU.add)
                if p == pieces[u] - 1:
                    ins.then_inc(a_ready, 1)

            def normalise(h, u):
                dve.wait_ge(rstd_ready, U * h + u + 1)
                dve.wait_ge(ot_ready, U * h + u)
                ts(on[:, :], ob[:, 0:P], rstd[:, :], None, ALU.mult).then_inc(on_ready, 1)

            def gate(h, u, wait_store):
                dve.wait_ge(ot_ready, U * h + u + 1)
                if u == 0:
                    dve.wait_ge(gs_ready, h + 1)
                dve.wait_ge(y_stored[u % 2], 16 * (U // 2 * h + u // 2))
                stt(y_out[:, u % 2, :], otb[:, 0:P], norm_c[:, :], g_sig[:, u * P:(u + 1) * P], ALU.mult,
                    ALU.mult).then_inc(y_ready, 1)

            with dve.Fori(0, HEADS) as h:
                base[0] = START + PER * h
                chain[0] = 0
                dve.wait_ge(qk_loaded, 128 * (h + 1))
                for m in range(2):
                    dve.wait_ge(hi_ready, 4 * h + 2 * m + 1)
                    tt(ks[DH:P, m, :], k_in[DH:P, m, :], ks[DH:P, m, :].bitcast(F32), ALU.subtract).then_inc(lo_ready, 1)
                    dve.wait_ge(hi_ready, 4 * h + 2 * m + 2)
                    stt(q_lo[:, m, :], q_in[:, m, :], DH ** -0.5, q_hi[:, m, :].bitcast(F32), ALU.mult,
                        ALU.subtract).then_inc(lo_ready, 1)
                for u in range(U + 5):
                    top = [(maximum, u, p) for p in range(pieces[u])] if u < U else []
                    rest = []
                    if 0 <= u - 1 < U:
                        rest += [(lambda h, u, p: weights(h, u), u - 1, 0)]
                        rest += [(combine, u - 1, p) for p in range(pieces[u - 1])]
                    for step in merged(top, rest):
                        step[0](h, step[1], step[2])
                    if 0 <= u - 3 < U:
                        normalise(h, u - 3)
                    if 0 <= u - 4 < U:
                        gate(h, u - 4, True)
                assert chain[0] == PER, (chain[0], PER)
            dve.wait_ge(gate_ready, 1)
            dve.wait_ge(rows_loaded, 32)
            tt(post[:, :], sc[0][:, :, :].rearrange("p a n -> p (a n)"), ada_b[:, :], ALU.add).then_inc(post_ready, 1)
            dve.wait_ge(post_ready, 1)
            tt(post[:, :], post[:, :], g_row[:, :], ALU.mult).then_inc(post_ready, 1)

        @block.scalar
        def _(act):
            a = nc.scalar.activation
            act.wait_ge(setup_v, 4)
            a(lam_s[:, :], lam_s[:, :], ACT.Exp).then_inc(setup, 1)
            act.wait_ge(consts_in, 80)
            a(c_act[:, :], c_col[:, :], ACT.Sigmoid).then_inc(c_sig, 1)

            def exps(h, u, p):
                n = before[u] + p
                w = width(u, p)
                act.wait_ge(max_ready, NP * h + n + 1)
                if p == 0 and u >= 3:
                    act.wait_ge(t_ready, NP * h + before[u - 2])
                for m in range(2):
                    ins = a(prob[u % 3][:, m, p * TG:p * TG + w], sc[n % 2][:, m, 0:w], ACT.Exp,
                            bias=negm[u % 2][:, m, p:p + 1], accum_out=sums[u % 2][:, m, p:p + 1])
                ins.then_inc(exp_done, 1)

            def wexp(h, u):
                if pieces[u] > 1:
                    act.wait_ge(d_ready, multi * h + multi_before[u] + 1)
                    a(wts[:, :, 0:pieces[u]], dist[:, :, 0:pieces[u]], ACT.Exp, scale=-1.0).then_inc(w_ready, 1)

            def evacuate(h, u, p):
                n = before[u] + p
                nb = width(u, p) // P
                act.wait_ge(t_ready, NP * h + n + 1)
                if p == 0:
                    if u >= 2:
                        act.wait_ge(pv_done, U * h + u - 1)
                a(at[u % 2][:, 4 * p:4 * p + nb, :], tb[n % 2][:, 0:nb, :], ACT.Copy).then_inc(at_ready, 1)

            def root(h, u):
                act.wait_ge(pv_done, U * h + u + 1)
                act.wait_ge(on_ready, U * h + u)
                a(junk[:, :], ob[:, 0:P], ACT.Square, accum_out=ssq[:, :]).then_inc(achain, 1)
                act.wait_ge(achain, 2 * (U * h + u) + 1)
                a(ssq[:, :], ssq[:, :], ACT.Ln, bias=epsb[:, :], scale=1.0 / P).then_inc(achain, 1)
                act.wait_ge(achain, 2 * (U * h + u) + 2)
                a(rstd[:, :], ssq[:, :], ACT.Exp, scale=-0.5).then_inc(rstd_ready, 1)

            with act.Fori(0, HEADS) as h:
                act.wait_ge(qk_loaded, 128 * (h + 1))
                act.wait_ge(s_ready, NP * h)
                for m in range(2):
                    a(ks[:, m, :], k_in[:, m, :], ACT.Copy).then_inc(hi_ready, 1)
                    a(q_hi[:, m, :], q_in[:, m, :], ACT.Copy, scale=DH ** -0.5).then_inc(hi_ready, 1)
                act.wait_ge(g_loaded, 16 * (h + 1))
                act.wait_ge(y_ready, U * h)
                a(g_sig[:, :], g_in[:, :], ACT.Sigmoid).then_inc(gsig_ready, 1)
                act.preload_act_table_set("natural_log_exp_and_others")
                for n in range(4):
                    act.wait_ge(vt_ready, 4 * h + n + 1)
                    a(v_tok[:, 4 * n:4 * n + 4, :], tb[n % 2][:, :, :], ACT.Copy).then_inc(v_ready, 1)
                for u in range(U + 5):
                    top = [(exps, u, p) for p in range(pieces[u])] if u < U else []
                    rest = []
                    if 0 <= u - 1 < U:
                        wexp(h, u - 1)
                    if 0 <= u - 2 < U:
                        rest += [(evacuate, u - 2, p) for p in range(pieces[u - 2])]
                    for step in merged(top, rest):
                        step[0](h, step[1], step[2])
                    if 0 <= u - 3 < U:
                        root(h, u - 3)

        @block.tensor
        def _(pe):
            mm = nc.tensor.matmul
            pe.wait_ge(setup_v, 4)

            def scores(h, u, p):
                n = before[u] + p
                w = width(u, p)
                if n >= 2:
                    pe.wait_ge(exp_done, NP * h + n - 1)
                q = slice(u * P, (u + 1) * P)
                keys = slice(p * TG, p * TG + w)
                last_piece = p == pieces[u] - 1
                for m in range(2):
                    mm(sc[n % 2][:, m, 0:w], q_hi[:, m, q], ks[:, m, keys], start=True, stop=False)
                    last = mm(sc[n % 2][:, m, 0:w], q_lo[:, m, q], ks[:, m, keys], start=False, stop=True)
                    if last_piece:
                        last = mm(sc[n % 2][:, m, w - P:w], ident_r[:, :], causal_r[:, :], start=False, stop=True,
                                  skip_group_check=True)
                last.then_inc(s_ready, 1)

            def turn(h, u, p):
                n = before[u] + p
                if p == 0:
                    pe.wait_ge(a_ready, U * h + u + 1)
                if n >= 2:
                    pe.wait_ge(at_ready, NP * h + n - 1)
                else:
                    pe.wait_ge(v_ready, 4 * h + 4)
                    pe.wait_ge(at_ready, NP * h)
                for b in range(width(u, p) // P):
                    last = nc.tensor.transpose(tb[n % 2][:, b, :], prob[u % 3][:, 0, p * TG + b * P:p * TG + (b + 1) * P],
                                               ident[:, :])
                last.then_inc(t_ready, 1)

            def values(h, u, p):
                if p == 0:
                    pe.wait_ge(on_ready, U * h + u)
                pe.wait_ge(at_ready, NP * h + before[u] + p + 1)
                for b in range(4 * p, min(4 * p + 4, u + 1)):
                    last = mm(ob[:, 0:P], at[u % 2][:, b, :], v_tok[:, b, :], start=(b == 0), stop=(b == u))
                if p == pieces[u] - 1:
                    last.then_inc(pv_done, 1)

            def turn_back(h, u):
                pe.wait_ge(on_ready, U * h + u + 1)
                pe.wait_ge(y_ready, U * h + u)
                nc.tensor.transpose(otb[:, 0:P], on[:, :], ident[:, :]).then_inc(ot_ready, 1)

            with pe.Fori(0, HEADS) as h:
                pe.wait_ge(v_loaded, 16 * (h + 1))
                pe.wait_ge(pv_done, U * h)
                for n in range(4):
                    if n < 2:
                        pe.wait_ge(at_ready, NP * h)
                    else:
                        pe.wait_ge(v_ready, 4 * h + n - 1)
                    for b in range(4):
                        last = nc.tensor.transpose(tb[n % 2][:, b, :], v_in[:, (4 * n + b) * P:(4 * n + b + 1) * P], ident[:, :])
                    last.then_inc(vt_ready, 1)
                pe.wait_ge(lo_ready, 4 * h + 4)
                pe.wait_ge(exp_done, NP * h)
                for u in range(U + 5):
                    top = [(scores, u, p) for p in range(pieces[u])] if u < U else []
                    rest = []
                    if 0 <= u - 2 < U:
                        rest += [(turn, u - 2, p) for p in range(pieces[u - 2])]
                    if 0 <= u - 3 < U:
                        rest += [(values, u - 3, p) for p in range(pieces[u - 3])]
                    for step in merged(top, rest):
                        step[0](h, step[1], step[2])
                    if 0 <= u - 4 < U:
                        turn_back(h, u - 4)
            pe.wait_ge(ones_set, 1)
            pe.wait_ge(pchain, 2 + KD)
            pe.wait_ge(exp_done, NP * HEADS)
            for m in range(2):
                last = mm(sc[0][:, m, :], ones[:, :], ada_sum[:, m * TG:(m + 1) * TG], start=True, stop=True)
            last.then_inc(gate_ready, 1)


def merged(top, rest):
    out, done = [], 0
    for n, step in enumerate(top):
        out.append(step)
        until = len(rest) * (n + 1) // len(top)
        out += rest[done:until]
        done = until
    return out + rest[done:]


BRANCH_CHUNKS = ((0, 2), (2, 4), (4, 6), (6, 10))
YC = 10


def merge_and_output(nc, x, w_merge, w_out, gT, yT, post, out):
    with ExitStack() as ctx:
        def sb(name, shape, dt=F32):
            return ctx.enter_context(nc.sbuf_tensor("D_" + name, shape, dt))

        def sem(name):
            return ctx.enter_context(nc.semaphore("D_" + name))

        wo_stage = [sb(f"wo_stage{j}", [P, D]) for j in range(2)]
        wo_hi = sb("wo_hi", [P, KD, D], F32R)
        wo_lo = sb("wo_lo", [P, KD, D], F32R)
        wm_stage = sb("wm_stage", [P, YC, P])
        wm_hi = [sb(f"wm_hi{j}", [P, YC, P], F32R) for j in range(2)]
        wm_lo = [sb(f"wm_lo{j}", [P, YC, P], F32R) for j in range(2)]
        y_stage = [sb(f"y_stage{j}", [P, 2, TG]) for j in range(2)]
        y_hi = sb("y_hi", [P, YC, TG], F32R)
        y_lo = sb("y_lo", [P, YC, TG], F32R)
        m_hi = sb("m_hi", [P, KD, TG], F32R)
        m_lo = sb("m_lo", [P, KD, TG], F32R)
        g_in = sb("g_in", [P, 4, TG])
        prods = [sb(f"prods{j}", [P, 4, TG]) for j in range(1)]
        x_in = [sb(f"x_in{j}", [P, D]) for j in range(2)]
        o_buf = [sb(f"o_buf{j}", [P, D]) for j in range(2)]
        ss = sb("ss", [P, 1])
        rstd = sb("rstd", [P, 1])
        epsb = sb("epsb", [P, 1])
        mb = [ctx.enter_context(nc.psum_tensor(f"D_mb{b}", [P, TG], F32)) for b in range(4)]
        pb = [ctx.enter_context(nc.psum_tensor(f"D_pb{j}", [P, D], F32)) for j in range(2)]

        eps_set, wo_loaded, wo_hi_ready, wo_lo_ready = sem("eps_set"), [sem(f"wo_loaded{j}") for j in range(2)], sem("wo_hi_ready"), sem("wo_lo_ready")
        wm_loaded, wm_hi_ready, wm_lo_ready = sem("wm_loaded"), sem("wm_hi_ready"), sem("wm_lo_ready")
        y_loaded, y_hi_ready, y_lo_ready = [sem(f"y_loaded{j}") for j in range(2)], sem("y_hi_ready"), sem("y_lo_ready")
        g_loaded, g_ready, merged_done, gated, added = sem("g_loaded"), sem("g_ready"), sem("merged_done"), sem("gated"), sem("added")
        m_hi_ready, m_lo_ready, p_done, squared, logged, rstd_ready, scaled, out_ready = (
            sem(n) for n in ("m_hi_ready", "m_lo_ready", "p_done", "squared", "logged", "rstd_ready", "scaled", "out_ready"))
        x_loaded, out_stored = [sem(f"x_loaded{j}") for j in range(2)], [sem(f"out_stored{j}") for j in range(2)]
        pchain, mul_done, sq_out = sem("pchain"), sem("mul_done"), sb("sq_out", [P, D])
        block = ctx.enter_context(nc.Block())
        wo_v = w_out.rearrange("a (k p) n -> p (a k) n", p=P)
        TB = TG // P
        YP = YC // 2

        def load_wm(eng, g, d):
            if not (isinstance(g, int) and g == 0 and d == 0):
                eng.wait_ge(wm_hi_ready, KD * g + d)
                eng.wait_ge(wm_lo_ready, KD * g + d)
            for w, (c0, c1) in zip(w_merge, BRANCH_CHUNKS):
                eng.dma_start(wm_stage[:, c0:c1, :], w[0, :, d * P:(d + 1) * P].rearrange("(k p) n -> p k n", p=P)).then_inc(wm_loaded, 16)

        @block.sync
        def _(sp):
            def load_y(at, g, n):
                sp.wait_ge(y_hi_ready, YP * g + n - 1) if n >= 2 else None
                sp.wait_ge(y_lo_ready, YP * g + n - 1) if n >= 2 else None
                sp.dma_start(y_stage[n % 2][:, :, :], yT[2 * n:2 * n + 2, :, bass.ds(at, TG)].rearrange("n p t -> p n t")).then_inc(y_loaded[n % 2], 16)

            with sp.Fori(0, NG) as g:
                at = sp.snap(g * TG)
                rows = [sp.snap(g * TG + b * P) for b in range(TB)]
                sp.wait_ge(y_hi_ready, YP * g)
                sp.wait_ge(y_lo_ready, YP * g)
                for n in range(YP):
                    load_y(at, g, n)
                load_wm(sp, g, 0)
                for d in range(KD):
                    sp.wait_ge(gated, KD * g + d)
                    sp.dma_start(g_in[:, :, :], gT[d:d + 3 * KD + 1:KD, :, bass.ds(at, TG)].rearrange("n p t -> p n t")).then_inc(g_loaded, 16)
                    if d + 1 < KD:
                        load_wm(sp, g, d + 1)
                for b in range(TB):
                    sp.wait_ge(out_ready, TB * g + b)
                    sp.dma_start(x_in[b % 2][:, :], x[0, bass.ds(rows[b], P), :]).then_inc(x_loaded[b % 2], 16)
                    if b:
                        sp.dma_start(out[0, bass.ds(rows[b - 1], P), :], o_buf[(b - 1) % 2][:, :]).then_inc(out_stored[(b - 1) % 2], 16)
                sp.wait_ge(out_ready, TB * g + TB)
                sp.dma_start(out[0, bass.ds(rows[TB - 1], P), :], o_buf[(TB - 1) % 2][:, :]).then_inc(out_stored[(TB - 1) % 2], 16)
            for j in range(2):
                sp.wait_ge(out_stored[j], 16 * NT // 2)

        @block.gpsimd
        def _(pool):
            tt = nc.gpsimd.tensor_tensor
            for k in range(KD):
                pool.wait_ge(wo_hi_ready, k + 1)
                tt(wo_lo[:, k, :], wo_stage[k % 2][:, :], wo_hi[:, k, :].bitcast(F32), ALU.subtract).then_inc(wo_lo_ready, 1)
            with pool.Fori(0, NG) as g:
                for d in range(KD):
                    pool.wait_ge(gated, KD * g + d + 1)
                    pr = prods[0]
                    tt(pr[:, 0:2, :], pr[:, 0:2, :], pr[:, 2:4, :], ALU.add).then_inc(pchain, 1)
                    pool.wait_ge(pchain, KD * g + d + 1)
                    tt(pr[:, 0, :], pr[:, 0, :], pr[:, 1, :], ALU.add).then_inc(added, 1)
                for b in range(TB):
                    pool.wait_ge(scaled, TB * g + b + 1)
                    pool.wait_ge(x_loaded[b % 2], 16 * (TB // 2 * g + b // 2 + 1))
                    tt(o_buf[b % 2][:, :], o_buf[b % 2][:, :], x_in[b % 2][:, :], ALU.add).then_inc(out_ready, 1)

        @block.vector
        def _(dve):
            tt, stt = nc.vector.tensor_tensor, nc.vector.scalar_tensor_tensor
            nc.vector.memset(epsb[:, :], EPS).then_inc(eps_set, 1)

            def split_wm(g, d):
                dve.wait_ge(wm_hi_ready, KD * g + d + 1)
                tt(wm_lo[d % 2][:, :, :], wm_stage[:, :, :], wm_hi[d % 2][:, :, :].bitcast(F32), ALU.subtract).then_inc(wm_lo_ready, 1)

            def split_y(g):
                for n in range(YP):
                    dve.wait_ge(y_hi_ready, YP * g + n + 1)
                    tt(y_lo[:, 2 * n:2 * n + 2, :], y_stage[n % 2][:, :, :], y_hi[:, 2 * n:2 * n + 2, :].bitcast(F32), ALU.subtract).then_inc(y_lo_ready, 1)

            def low(g, d):
                dve.wait_ge(m_hi_ready, KD * g + d + 1)
                tt(m_lo[:, d, :], prods[0][:, 0, :], m_hi[:, d, :].bitcast(F32), ALU.subtract).then_inc(m_lo_ready, 1)

            with dve.Fori(0, NG) as g:
                split_y(g)
                split_wm(g, 0)
                for d in range(KD):
                    if d + 1 < KD:
                        split_wm(g, d + 1)
                    dve.wait_ge(g_ready, KD * g + d + 1)
                    for b in range(4):
                        dve.wait_ge(merged_done, 4 * (KD * g + d) + b + 1)
                        if b == 0:
                            dve.wait_ge(m_lo_ready, KD * g + d)
                        ins = tt(prods[0][:, b, :], mb[b][:, :], g_in[:, b, :], ALU.mult)
                        if b < 3:
                            ins.then_inc(mul_done, 1)
                    ins.then_inc(gated, 1)
                    low(g, d)
                for b in range(TB):
                    dve.wait_ge(rstd_ready, TB * g + b + 1)
                    dve.wait_ge(out_stored[b % 2], 16 * (TB // 2 * g + b // 2))
                    stt(o_buf[b % 2][:, :], pb[b % 2][:, :], rstd[:, :], post[:, :], ALU.mult, ALU.mult).then_inc(scaled, 1)

        @block.scalar
        def _(act):
            a = nc.scalar.activation
            for k in range(KD):
                if k >= 2:
                    act.wait_ge(wo_hi_ready, k - 1)
                    act.wait_ge(wo_lo_ready, k - 1)
                act.dma_start(wo_stage[k % 2][:, :], wo_v[:, k, :]).then_inc(wo_loaded[k % 2], 16)
                if k >= 1:
                    act.wait_ge(wo_loaded[(k - 1) % 2], 16 * ((k - 1) // 2 + 1))
                    a(wo_hi[:, k - 1, :], wo_stage[(k - 1) % 2][:, :], ACT.Copy).then_inc(wo_hi_ready, 1)
            act.wait_ge(wo_loaded[(KD - 1) % 2], 16 * (KD // 2))
            a(wo_hi[:, KD - 1, :], wo_stage[(KD - 1) % 2][:, :], ACT.Copy).then_inc(wo_hi_ready, 1)
            act.wait_ge(eps_set, 1)

            def split_wm(g, d):
                act.wait_ge(wm_loaded, 64 * (KD * g + d + 1))
                if d >= 2:
                    act.wait_ge(merged_done, 4 * (KD * g + d - 1))
                else:
                    act.wait_ge(merged_done, 4 * KD * g)
                a(wm_hi[d % 2][:, :, :], wm_stage[:, :, :], ACT.Copy).then_inc(wm_hi_ready, 1)

            def split_y(g):
                act.wait_ge(merged_done, 4 * KD * g)
                for n in range(YP):
                    act.wait_ge(y_loaded[n % 2], 16 * (g * ((YP + 1 - n % 2) // 2) + n // 2 + 1))
                    a(y_hi[:, 2 * n:2 * n + 2, :], y_stage[n % 2][:, :, :], ACT.Copy).then_inc(y_hi_ready, 1)

            def sigmoids(g, d):
                act.wait_ge(g_loaded, 16 * (KD * g + d + 1))
                a(g_in[:, :, :], g_in[:, :, :], ACT.Sigmoid).then_inc(g_ready, 1)

            def high(g, d):
                act.wait_ge(added, KD * g + d + 1)
                act.wait_ge(p_done, TB * g)
                a(m_hi[:, d, :], prods[0][:, 0, :], ACT.Copy).then_inc(m_hi_ready, 1)

            with act.Fori(0, NG) as g:
                split_y(g)
                split_wm(g, 0)
                sigmoids(g, 0)
                for d in range(KD):
                    if d + 1 < KD:
                        split_wm(g, d + 1)
                    high(g, d)
                    if d + 1 < KD:
                        sigmoids(g, d + 1)
                act.preload_act_table_set("natural_log_exp_and_others")
                for b in range(TB):
                    n = TB * g + b
                    act.wait_ge(p_done, n + 1)
                    act.wait_ge(scaled, n)
                    a(sq_out[:, :], pb[b % 2][:, :], ACT.Square, accum_out=ss[:, :]).then_inc(squared, 1)
                    act.wait_ge(squared, n + 1)
                    a(ss[:, :], ss[:, :], ACT.Ln, bias=epsb[:, :], scale=1.0 / D).then_inc(logged, 1)
                    act.wait_ge(logged, n + 1)
                    a(rstd[:, :], ss[:, :], ACT.Exp, scale=-0.5).then_inc(rstd_ready, 1)

        @block.tensor
        def _(pe):
            mm = nc.tensor.matmul
            with pe.Fori(0, NG) as g:
                pe.wait_ge(y_lo_ready, YP * g + YP)
                for d in range(KD):
                    pe.wait_ge(wm_lo_ready, KD * g + d + 1)
                    for b, (c0, c1) in enumerate(BRANCH_CHUNKS):
                        if b == 0:
                            pe.wait_ge(mul_done, 3 * (KD * g + d))
                            pe.wait_ge(gated, KD * g + d)
                        for k in range(c0, c1):
                            mm(mb[b][:, :], wm_hi[d % 2][:, k, :], y_hi[:, k, :], start=(k == c0), stop=False)
                            mm(mb[b][:, :], wm_hi[d % 2][:, k, :], y_lo[:, k, :], start=False, stop=False)
                            last = mm(mb[b][:, :], wm_lo[d % 2][:, k, :], y_hi[:, k, :], start=False, stop=(k == c1 - 1))
                        last.then_inc(merged_done, 1)
                pe.wait_ge(wo_lo_ready, KD)
                pe.wait_ge(m_lo_ready, KD * g + KD)
                for b in range(TB):
                    n = TB * g + b
                    if b >= 2:
                        pe.wait_ge(scaled, n - 1)
                    else:
                        pe.wait_ge(scaled, TB * g)
                    tok = slice(b * P, (b + 1) * P)
                    for half in range(2):
                        cols = slice(half * TG, (half + 1) * TG)
                        for k in range(KD):
                            mm(pb[b % 2][:, cols], m_hi[:, k, tok], wo_hi[:, k, cols], start=(k == 0), stop=False)
                            mm(pb[b % 2][:, cols], m_hi[:, k, tok], wo_lo[:, k, cols], start=False, stop=False)
                            last = mm(pb[b % 2][:, cols], m_lo[:, k, tok], wo_hi[:, k, cols], start=False, stop=(k == KD - 1))
                    last.then_inc(p_done, 1)


def constants():
    i = np.arange(P)
    same_head = (i[:, None] // 64 == i[None, :] // 64).astype(np.float32)
    masks = np.zeros((P, NL, P), np.float32)
    for n, m in enumerate(LEVELS):
        s, t = i[:, None], i[None, :]
        masks[:, n, :] = (s // (2 * m) == t // (2 * m)) & (s % (2 * m) < m) & (t % (2 * m) >= m)
    masks[:, NL - 1, :] = np.eye(P)
    scan = np.ones((P, 2, P), np.float32)
    scan[:, :, 0] = 0
    windows = np.array([[2, 8], [4, 16]])[i // 64]
    inv_first = 1.0 / np.minimum(i[None, None, :] + 1, windows[:, :, None])
    return {
        "causal": np.where(i[None, :] <= i[:, None], 0.0, NEG).astype(np.float32),
        "ident": np.eye(P, dtype=np.float32),
        "mean_w": same_head / 64,
        "head_m": same_head,
        "masks": masks,
        "scan_m": scan.reshape(P, 2 * P),
        "inv_first": inv_first.astype(np.float32),
        "inv_count": (1.0 / windows).astype(np.float32),
    }


def hybrid_trunk(nc, A, consts, out):
    pT = nc.dram_tensor("pT_scratch", [MIX_TILES, P, T], F32).ap()
    gT = nc.dram_tensor("gT_scratch", [GATE_TILES, P, T], F32).ap()
    yT = nc.dram_tensor("yT_scratch", [YC, P, T], F32).ap()
    with ExitStack() as ctx:
        h_hi = ctx.enter_context(nc.sbuf_tensor("h_hi", [P, KD, T], F32R))
        h_lo = ctx.enter_context(nc.sbuf_tensor("h_lo", [P, KD, T], F32R))
        project_mixer_inputs(nc, A["x"], A["c"], A["w_ada"], A["b_ada"], A["g_pre"], A["w_in"], consts["ident"], h_hi, h_lo, pT)
        gates_and_local_mixers(nc, A["w_in"], h_hi, h_lo, pT, gT, yT, consts, A["hgrn_lb"], A["hgrn_norm"], A["conv_w"],
                               A["pool_w"], A["pool_scale"])
    with ExitStack() as ctx:
        post = ctx.enter_context(nc.sbuf_tensor("post", [P, D], F32))
        differential_attention(nc, pT, yT, consts, A["diff_lam"], A["diff_norm"], A["c"], A["w_ada"], A["b_ada"], A["g_post"], post)
        merge_and_output(nc, A["x"], [A[f"w_merge_{b}"] for b in ("pool", "hgrn", "conv", "diff")], A["w_out"], gT, yT, post, out)


NAMES = ["x", "c", "w_ada", "b_ada", "g_pre", "g_post", "w_in", "pool_w", "pool_scale", "hgrn_lb", "hgrn_norm", "conv_w",
         "diff_lam", "diff_norm", "w_merge_pool", "w_merge_hgrn", "w_merge_conv", "w_merge_diff", "w_out"]


def kernel(**inputs):
    import concourse.bacc as bacc
    from concourse.bass_utils import run_bass_kernel_spmd

    nc = bacc.Bacc("TRN2", target_bir_lowering=False, num_devices=1, dynamic_dma_scratch_size=1024)
    arrays = {}

    def declare(name, array):
        array = np.ascontiguousarray(array)
        arrays[name + "_dram"] = array
        return nc.dram_tensor(name + "_dram", array.shape, mybir.dt.from_np(array.dtype), kind="ExternalInput").ap()

    inputs_ap = {n: declare("in_" + n, np.asarray(inputs[n])) for n in NAMES}
    consts_ap = {n: declare("const_" + n, a) for n, a in constants().items()}
    out = nc.dram_tensor("out_dram", (1, T, D), F32, kind="ExternalOutput").ap()
    hybrid_trunk(nc, inputs_ap, consts_ap, out)
    result = run_bass_kernel_spmd(nc, [arrays], core_ids=[0])
    return result.results[0]["out_dram"]
```

```python
import numpy as np
import concourse.bass as bass
from concourse import mybir
from contextlib import ExitStack

F32 = mybir.dt.float32
F32R = mybir.dt.float32r
ACT = mybir.ActivationFunctionType
ALU = mybir.AluOpType
AX = mybir.AxisListType

P = 128
D = 1024
T = 2048
KD = D // P
TG = 512
NG = T // TG
NT = T // P
D_IN = 8704
MIX_TILES = 36
GATE_TILES = D_IN // P - MIX_TILES
PAIRS = MIX_TILES // 2
EPS = 1e-6


def project_mixer_inputs(nc, x, c, w_ada, b_ada, g_pre, w_in, ident_d, h_hi, h_lo, pT):
    with ExitStack() as ctx:
        def sb(name, shape, dt=F32):
            return ctx.enter_context(nc.sbuf_tensor(name, shape, dt))

        def sem(name):
            return ctx.enter_context(nc.semaphore(name))

        w_stage = sb("w_stage", [P, KD, 2 * P])
        w_hi = [sb(f"w_hi{j}", [P, KD, P], F32R) for j in range(2)]
        w_lo = [sb(f"w_lo{j}", [P, KD, P], F32R) for j in range(2)]
        p_out = [sb(f"p_out{j}", [P, T]) for j in range(2)]
        x_tile = [sb(f"x_tile{j}", [P, D]) for j in range(2)]
        xn_all = sb("xn_all", [P, 4, D])
        xn = [xn_all[:, j, :] for j in range(4)]
        h_tmp = [sb(f"h_tmp{j}", [P, TG]) for j in range(4)]
        ada_acc = [xn_all[:, 2 * j:2 * j + 2, :].rearrange("p a n -> p (a n)") for j in range(2)]
        square = sb("square", [P, D])
        ident = sb("ident", [P, P])
        ones = sb("ones", [P, 1])
        epsb = sb("epsb", [P, 1])
        c_col = sb("c_col", [P, KD])
        c_act = sb("c_act", [P, KD])
        c_sig = sb("c_sig", [P, KD])
        g_col = sb("g_col", [P, KD])
        b_col = sb("b_col", [P, 2 * KD])
        mod = sb("mod", [P, 2 * KD])
        sc1 = sb("sc1", [P, KD])
        gs = sb("gs", [P, KD])
        ss = sb("ss", [P, NT])
        rt = sb("rt", [P, NT])
        rstd = sb("rstd", [P, NT])
        bank = [ctx.enter_context(nc.psum_tensor(f"bankA{i}", [P, TG], F32)) for i in range(8)]

        consts_in = sem("A_consts_in")
        ones_set = sem("A_ones_set")
        ada_in = [sem(f"A_ada_in{j}") for j in range(2)]
        ada_used = sem("A_ada_used")
        c_ready = sem("A_c_ready")
        mod_summed = sem("A_mod_summed")
        mod_ready = sem("A_mod_ready")
        x_in = [sem(f"A_x_in{j}") for j in range(2)]
        squared = sem("A_squared")
        rooted = sem("A_rooted")
        inverted = sem("A_inverted")
        xn_ready = sem("A_xn_ready")
        turned = sem("A_turned")
        h_ready = sem("A_h_ready")
        hi_ready = sem("A_hi_ready")
        lo_ready = sem("A_lo_ready")
        dchain = sem("A_dchain")
        w_in_sem = sem("A_w_loaded")
        whi = sem("A_w_hi_ready")
        wlo = sem("A_w_lo_ready")
        ps_ready = sem("A_ps_ready")
        evac = sem("A_evacuated")
        stored = [sem(f"A_stored{j}") for j in range(2)]

        block = ctx.enter_context(nc.Block())
        w_v = w_in.rearrange("a (k p) n -> p (a k) n", p=P)
        ada_v = w_ada.rearrange("a (k p) n -> p (a k) n", p=P)

        @block.sync
        def _(sp):
            sp.dma_start(c_col[:, :], c.rearrange("a (k p) -> p (a k)", p=P), allow_slow_non_contiguous=True).then_inc(consts_in, 16)
            sp.dma_start(b_col[:, :], b_ada[:, 0:2 * D].rearrange("a (k p) -> p (a k)", p=P), allow_slow_non_contiguous=True).then_inc(consts_in, 16)
            sp.dma_start(g_col[:, :], g_pre.rearrange("a (k p) -> p (a k)", p=P), allow_slow_non_contiguous=True).then_inc(consts_in, 16)
            sp.dma_start(ident[:, :], ident_d).then_inc(consts_in, 16)
            for k in range(KD):
                if k >= 2:
                    sp.wait_ge(ada_used, k - 1)
                sp.dma_start(p_out[k % 2][:, :], ada_v[:, k, 0:2 * D]).then_inc(ada_in[k % 2], 16)
            for t in range(NT):
                if t >= 2:
                    sp.wait_ge(xn_ready, t - 1)
                sp.dma_start(x_tile[t % 2][:, :], x[0, t * P:(t + 1) * P, :]).then_inc(x_in[t % 2], 16)

            def load(q):
                sp.dma_start(w_stage[:, :, :], w_v[:, :, bass.ds(q * 2 * P, 2 * P)]).then_inc(w_in_sem, 16)

            def store(q, j):
                sp.wait_ge(evac, 8 * q + 4 * j + 4)
                sp.dma_start(pT[bass.ds(2 * q + j, 1), :, :].rearrange("a p t -> (a p) t"), p_out[j][:, :]).then_inc(stored[j], 16)

            load(0)
            with sp.Fori(1, PAIRS) as q:
                sp.wait_ge(whi, 2 * q)
                sp.wait_ge(wlo, 2 * q)
                load(q)
                store(q - 1, 0)
                store(q - 1, 1)
            store(PAIRS - 1, 0)
            store(PAIRS - 1, 1)
            for j in range(2):
                sp.wait_ge(stored[j], 16 * PAIRS)

        @block.gpsimd
        def _(pool):
            nc.gpsimd.memset(ones[:, :], 1.0).then_inc(ones_set, 1)
            nc.gpsimd.memset(epsb[:, :], EPS).then_inc(ones_set, 1)
            for n in range(NG * KD):
                g, k = divmod(n, KD)
                pool.wait_ge(hi_ready, n + 1)
                nc.gpsimd.tensor_tensor(h_lo[:, k, g * TG:(g + 1) * TG], h_tmp[n % 4][:, :],
                                        h_hi[:, k, g * TG:(g + 1) * TG].bitcast(F32), ALU.subtract).then_inc(lo_ready, 1)

        @block.vector
        def _(dve):
            chain = [0]

            def link(ins):
                chain[0] += 1
                ins.then_inc(dchain, 1)
                dve.wait_ge(dchain, chain[0])

            dve.wait_ge(c_ready, 1)
            link(nc.vector.tensor_tensor(c_act[:, :], c_col[:, :], c_sig[:, :], ALU.mult))
            for k in range(KD):
                dve.wait_ge(ada_in[k % 2], 16 * (k // 2 + 1))
                if k == 0:
                    ins = nc.vector.tensor_scalar(ada_acc[0], p_out[0][:, :], c_act[:, 0:1], None, ALU.mult)
                else:
                    ins = nc.vector.scalar_tensor_tensor(ada_acc[k % 2], p_out[k % 2][:, :], c_act[:, k:k + 1],
                                                         ada_acc[(k - 1) % 2], ALU.mult, ALU.add)
                ins.then_inc(ada_used, 1)
                dve.wait_ge(ada_used, k + 1)
            dve.wait_ge(mod_summed, 1)
            link(nc.vector.tensor_tensor(mod[:, :], bank[0][:, 0:2 * KD], b_col[:, :], ALU.add))
            link(nc.vector.tensor_scalar(sc1[:, :], mod[:, KD:2 * KD], 1.0, None, ALU.add))
            nc.vector.tensor_tensor(gs[:, :], sc1[:, :], g_col[:, :], ALU.mult).then_inc(mod_ready, 1)
            dve.wait_ge(mod_ready, 1)

            def norm(t):
                dve.wait_ge(rooted, t + 1)
                nc.vector.reciprocal(rstd[:, t:t + 1], rt[:, t:t + 1]).then_inc(inverted, 1)
                dve.wait_ge(inverted, t + 1)
                if t >= 4:
                    dve.wait_ge(turned, (t // 4) * KD)
                nc.vector.tensor_scalar(xn[t % 4], x_tile[t % 2][:, :], rstd[:, t:t + 1], None,
                                        ALU.mult).then_inc(xn_ready, 1)

            for t in range(4):
                norm(t)
            for g in range(NG):
                for k in range(KD):
                    n = g * KD + k
                    dve.wait_ge(turned, n + 1)
                    if n >= 4:
                        dve.wait_ge(lo_ready, n - 3)
                    nc.vector.tensor_scalar(h_tmp[n % 4][:, :], bank[k][:, :], gs[:, k:k + 1], mod[:, k:k + 1],
                                            ALU.mult, ALU.add).then_inc(h_ready, 1)
                if g + 1 < NG:
                    for t in range(4 * g + 4, 4 * g + 8):
                        norm(t)

            def split(q, j, first):
                dve.wait_ge(whi, 2 * q + j + 1)
                nc.vector.tensor_tensor(w_lo[j][:, :, :], w_stage[:, :, j * P:(j + 1) * P],
                                        w_hi[j][:, :, :].bitcast(F32), ALU.subtract).then_inc(wlo, 1)

            with dve.Fori(0, PAIRS) as q:
                for j in range(2):
                    split(q, j, False)

        @block.scalar
        def _(act):
            act.wait_ge(consts_in, 64)
            nc.scalar.activation(c_sig[:, :], c_col[:, :], ACT.Sigmoid).then_inc(c_ready, 1)
            act.wait_ge(ones_set, 2)

            def root(t):
                act.wait_ge(x_in[t % 2], 16 * (t // 2 + 1))
                nc.scalar.activation(square[:, :], x_tile[t % 2][:, :], ACT.Square,
                                     accum_out=ss[:, t:t + 1]).then_inc(squared, 1)
                act.wait_ge(squared, t + 1)
                nc.scalar.activation(rt[:, t:t + 1], ss[:, t:t + 1], ACT.Sqrt, bias=epsb[:, :],
                                     scale=1.0 / D).then_inc(rooted, 1)

            for t in range(4):
                root(t)
            for g in range(NG):
                for k in range(KD):
                    n = g * KD + k
                    act.wait_ge(h_ready, n + 1)
                    nc.scalar.activation(h_hi[:, k, g * TG:(g + 1) * TG], h_tmp[n % 4][:, :], ACT.Copy).then_inc(hi_ready, 1)
                if g + 1 < NG:
                    for t in range(4 * g + 4, 4 * g + 8):
                        root(t)

            def split(q, j, first):
                act.wait_ge(w_in_sem, 16 * (q + 1))
                if not first:
                    act.wait_ge(ps_ready, 4 * (2 * q + j - 1))
                nc.scalar.activation(w_hi[j][:, :, :], w_stage[:, :, j * P:(j + 1) * P], ACT.Copy).then_inc(whi, 1)

            def evacuate(q, j, first):
                for g in range(NG):
                    act.wait_ge(ps_ready, 8 * q + 4 * j + g + 1)
                    if not first and g == 0:
                        act.wait_ge(stored[j], 16 * q)
                    nc.scalar.activation(p_out[j][:, g * TG:(g + 1) * TG], bank[4 * j + g][:, :], ACT.Copy).then_inc(evac, 1)

            def body(q, first, last=False):
                evacuate(q, 0, first)
                if not last:
                    split(q + 1, 0, False)
                evacuate(q, 1, first)
                if not last:
                    split(q + 1, 1, False)

            split(0, 0, True)
            split(0, 1, True)
            body(0, True)
            with act.Fori(1, PAIRS - 1) as q:
                body(q, False)
            body(PAIRS - 1, False, last=True)

        @block.tensor
        def _(pe):
            pe.wait_ge(ones_set, 2)
            pe.wait_ge(ada_used, KD)
            for j in range(2 * KD):
                last = nc.tensor.matmul(bank[0][:, j:j + 1], ada_acc[(KD - 1) % 2][:, j * P:(j + 1) * P], ones[:, :],
                                        start=True, stop=True)
            last.then_inc(mod_summed, 1)
            pe.wait_ge(mod_ready, 1)
            for g in range(NG):
                pe.wait_ge(xn_ready, 4 * (g + 1))
                for k in range(KD):
                    if g:
                        pe.wait_ge(h_ready, (g - 1) * KD + k + 1)
                    for i in range(4):
                        last = nc.tensor.transpose(bank[k][:, i * P:(i + 1) * P], xn[i][:, k * P:(k + 1) * P], ident[:, :])
                    last.then_inc(turned, 1)
            pe.wait_ge(h_ready, NG * KD)
            pe.wait_ge(hi_ready, NG * KD)
            pe.wait_ge(lo_ready, NG * KD)

            def tile(q, j, first):
                pe.wait_ge(wlo, 2 * q + j + 1)
                for g in range(NG):
                    if not first:
                        pe.wait_ge(evac, 8 * (q - 1) + 4 * j + g + 1)
                    cols = slice(g * TG, (g + 1) * TG)
                    for k in range(KD):
                        nc.tensor.matmul(bank[4 * j + g][:, :], w_hi[j][:, k, :], h_hi[:, k, cols], start=(k == 0), stop=False)
                        nc.tensor.matmul(bank[4 * j + g][:, :], w_hi[j][:, k, :], h_lo[:, k, cols], start=False, stop=False)
                        last = nc.tensor.matmul(bank[4 * j + g][:, :], w_lo[j][:, k, :], h_hi[:, k, cols], start=False,
                                                stop=(k == KD - 1))
                    last.then_inc(ps_ready, 1)

            tile(0, 0, True)
            tile(0, 1, True)
            with pe.Fori(1, PAIRS) as q:
                for j in range(2):
                    tile(q, j, False)


LEVELS = (64, 32, 16, 8, 4, 2, 1)
NL = len(LEVELS) + 1
SPLIT = 2.0 ** -30
MIN_F = 1e-20
HALO_P, HALO_C = 16, 2


def gates_and_local_mixers(nc, w_in, h_hi, h_lo, pT, gT, yT, consts, hgrn_lb, hgrn_norm, conv_w, pool_w, pool_scale):
    with ExitStack() as ctx:
        def sb(name, shape, dt=F32):
            return ctx.enter_context(nc.sbuf_tensor("B_" + name, shape, dt))

        def sem(name):
            return ctx.enter_context(nc.semaphore("B_" + name))

        w_stage = sb("w_stage", [P, KD, P])
        w_hi = [sb(f"w_hi{j}", [P, KD, P], F32R) for j in range(2)]
        w_lo = [sb(f"w_lo{j}", [P, KD, P], F32R) for j in range(2)]
        g_out = [sb(f"g_out{j}", [P, TG]) for j in range(4)]
        ident = sb("ident", [P, P])
        mean_w = sb("mean_w", [P, P])
        head_m = sb("head_m", [P, P])
        masks = sb("masks", [P, NL, P], mybir.dt.uint8)
        scan_m = sb("scan_m", [P, 2 * P])
        inv_first = sb("inv_first", [P, 2, P])
        inv_count = sb("inv_count", [P, 2])
        pool_bd = sb("pool_bd", [P, 2, P])
        pool_sc = sb("pool_sc", [P, 2])
        conv_c = sb("conv_c", [P, 3, 2])
        lb_x = sb("lb_x", [P, 2])
        lb_e = sb("lb_e", [P, 2])
        lb = sb("lb", [P, 2])
        omlb = sb("omlb", [P, 2])
        norm_c = sb("norm_c", [P, 1])
        epsb = sb("epsb", [P, 1])
        in3 = sb("in3", [P, 6, P])
        g_in = sb("g_in", [P, 2, P])
        f_s = sb("f_s", [P, 2, P])
        k_s = sb("k_s", [P, 2, P])
        q_s = sb("q_s", [P, 2, P])
        f_ab = sb("f_ab", [P, 2, 2, P])
        b_s = sb("b_s", [P, 2, P])
        eb = sb("eb", [P, 2, P])
        qe = sb("qe", [P, 2, P])
        kt = sb("kt", [P, 2, P])
        X = sb("X", [P, NL, 2, P])
        QX = sb("QX", [P, NL, 2, P])
        tok = sb("tok", [P, 4, P])
        AT = sb("AT", [P, 2, 2, P])
        picks = sb("picks", [P, 2, 4, P])
        part = sb("part", [P, 2, P])
        S = sb("S", [P, 2, P])
        kvm = sb("kvm", [P, 2, P])
        osq = sb("osq", [P, 2, P])
        rs = sb("rs", [P, 2, P])
        sgate = sb("sgate", [P, 2, P])
        yh = sb("yh", [P, 2, P])
        a_in = sb("a_in", [P, 2, HALO_P + P])
        ag_in = sb("ag_in", [P, 2, P])
        s_ag = sb("s_ag", [P, 2, P])
        sum2 = sb("sum2", [P, 2, HALO_P + P])
        sum4 = sb("sum4", [P, 2, HALO_P + P])
        sum8 = sb("sum8", [P, HALO_P + P])
        win = sb("win", [P, 2, P])
        yp = sb("yp", [P, 2, P])
        c_in = sb("c_in", [P, 8, HALO_C + P])
        s_cg = sb("s_cg", [P, 2, P])
        z_s = sb("z_s", [P, 2, HALO_C + P])
        tap = sb("tap", [P, 2, P])
        acc = sb("acc", [P, 2, P])
        yc = sb("yc", [P, 2, P])
        bank = [ctx.enter_context(nc.psum_tensor(f"bankB{i}", [P, TG], F32)) for i in range(4)]
        score = ctx.enter_context(nc.psum_tensor("B_score", [P, 2, 4, P], F32))
        b6 = ctx.enter_context(nc.psum_tensor("B_b6", [P, 4, P], F32))
        b7 = ctx.enter_context(nc.psum_tensor("B_b7", [P, 4, P], F32))

        consts_in = sem("consts_in")
        zeroed = sem("zeroed")
        zeroed_v = sem("zeroed_v")
        lb_exp = sem("lb_exp")
        w_loaded = sem("w_loaded")
        whi, wlo = sem("w_hi_ready"), sem("w_lo_ready")
        ps_ready, evac = sem("ps_ready"), sem("evacuated")
        stored = [sem(f"stored{j}") for j in range(4)]
        in3_loaded, g_loaded, a_loaded, c_loaded = sem("in3_loaded"), sem("g_loaded"), sem("a_loaded"), sem("c_loaded")
        sig_ready, sigg_ready, sigac_ready = sem("sig_ready"), sem("sigg_ready"), sem("sigac_ready")
        clipped, logged, scanned, decayed, spread, xready = (sem(n) for n in ("clipped", "logged", "scanned", "decayed", "spread", "x_ready"))
        kt_ready, prep_ready = sem("kt_ready"), sem("prep_ready")
        t_done, r_done, o_done, n_done = sem("t_done"), sem("r_done"), sem("o_done"), sem("n_done")
        tok_ready, picked = sem("tok_ready"), sem("picked")
        attn_ready = sem("attn_ready")
        state_done, osq_ready, rstd_ready, fin_done = sem("state_done"), sem("osq_ready"), sem("rstd_ready"), sem("fin_done")
        pooled, sag_ready, yp_ready, yc_ready = sem("pooled"), sem("sag_ready"), sem("yp_ready"), sem("yc_ready")
        yh_stored, yp_stored, yc_stored = sem("yh_stored"), sem("yp_stored"), sem("yc_stored")
        dchain, pchain, achain = sem("dchain"), sem("pchain"), sem("achain")

        block = ctx.enter_context(nc.Block())
        w_v = w_in.rearrange("a (k p) n -> p (a k) n", p=P)
        STEPS = NT
        assert GATE_TILES == 2 * STEPS

        def loop(eng, body):
            body(0, True, False)
            with eng.Fori(1, STEPS - 1) as i:
                body(i, False, False)
            body(STEPS - 1, False, True)

        @block.sync
        def _(sp):
            n = 0
            for dst, src in ((ident, consts["ident"]), (mean_w, consts["mean_w"]), (head_m, consts["head_m"]),
                             (scan_m, consts["scan_m"])):
                sp.dma_start(dst[:, :], src).then_inc(consts_in, 16)
                n += 1
            sp.dma_start(QX[:, :, 0, :], consts["masks"]).then_inc(consts_in, 16)
            sp.dma_start(inv_first[:, :, :], consts["inv_first"]).then_inc(consts_in, 16)
            sp.dma_start(inv_count[:, :], consts["inv_count"]).then_inc(consts_in, 16)
            sp.dma_start(pool_sc[:, :], pool_scale.rearrange("a (n p) -> p (a n)", p=P), allow_slow_non_contiguous=True).then_inc(consts_in, 16)
            for k in range(3):
                sp.dma_start(conv_c[:, k, :], conv_w[0, k:k + 1, :].rearrange("a (n p) -> p (a n)", p=P),
                             allow_slow_non_contiguous=True).then_inc(consts_in, 16)
            sp.dma_start(lb_x[:, :], hgrn_lb.rearrange("a (n p) -> p (a n)", p=P), allow_slow_non_contiguous=True).then_inc(consts_in, 16)
            for h in range(2):
                sp.dma_start(norm_c[64 * h:64 * h + 64, :], hgrn_norm.rearrange("a p -> p a"), allow_slow_non_contiguous=True).then_inc(consts_in, 16)
            sp.wait_ge(zeroed, 1)
            for g in range(4):
                sp.dma_start(pool_bd[64 * (g % 2):64 * (g % 2) + 64, g // 2, 64 * (g % 2):64 * (g % 2) + 64],
                             pool_w[0, g, :, :]).then_inc(consts_in, 16)

            def fixed(value):
                return value if isinstance(value, int) else sp.snap(value)

            def load_w(col):
                sp.dma_start(w_stage[:, :, :], w_v[:, :, bass.ds(col, P)]).then_inc(w_loaded, 16)

            def load_hgrn(at):
                sp.dma_start(in3[:, :, :], pT[4:10, :, bass.ds(at, P)].rearrange("n p t -> p n t")).then_inc(in3_loaded, 16)

            def load_gate(at):
                sp.dma_start(g_in[:, :, :], pT[10:12, :, bass.ds(at, P)].rearrange("n p t -> p n t")).then_inc(g_loaded, 16)

            def load_pool_conv(at, at_p, at_c):
                if at_p is None:
                    sp.wait_ge(zeroed, 3)
                    sp.dma_start(a_in[:, :, HALO_P:], pT[0:2, :, 0:P].rearrange("n p t -> p n t")).then_inc(a_loaded, 16)
                    sp.dma_start(c_in[:, :, HALO_C:], pT[12:20, :, 0:P].rearrange("n p t -> p n t")).then_inc(c_loaded, 16)
                else:
                    sp.dma_start(a_in[:, :, :], pT[0:2, :, bass.ds(at_p, HALO_P + P)].rearrange("n p t -> p n t")).then_inc(a_loaded, 16)
                    sp.dma_start(c_in[:, :, :], pT[12:20, :, bass.ds(at_c, HALO_C + P)].rearrange("n p t -> p n t")).then_inc(c_loaded, 16)
                sp.dma_start(ag_in[:, :, :], pT[2:4, :, bass.ds(at, P)].rearrange("n p t -> p n t")).then_inc(a_loaded, 16)

            def store_gate(i, s, tile):
                sp.wait_ge(evac, 8 * i + s + 1)
                sp.dma_start(gT[bass.ds(tile, 1), :, (s % 4) * TG:(s % 4 + 1) * TG].rearrange("a p t -> (a p) t"),
                             g_out[s % 4][:, :]).then_inc(stored[s % 4], 16)

            def store_y(at, first_chunk, src, done):
                sp.dma_start(yT[first_chunk:first_chunk + 2, :, bass.ds(at, P)].rearrange("n p t -> p n t"),
                             src[:, :, :]).then_inc(done, 16)

            load_w(MIX_TILES * P)
            load_hgrn(0)
            load_pool_conv(0, None, None)
            sp.wait_ge(whi, 1)
            sp.wait_ge(wlo, 1)
            load_w((MIX_TILES + 1) * P)

            def finish_last(i, at):
                sp.wait_ge(fin_done, i)
                store_y(at, 2, yh, yh_stored)
                sp.wait_ge(yp_ready, i)
                store_y(at, 0, yp, yp_stored)

            def body(i, first, last):
                here = fixed(i * P)
                before = None if first else fixed(i * P - P)
                tiles = [fixed(2 * i), fixed(2 * i + 1)]
                if not last:
                    cols = [fixed(i * (2 * P) + (MIX_TILES + 2 + j) * P) for j in range(2)]
                    after, after_p, after_c = (fixed(i * P + (P - halo)) for halo in (0, HALO_P, HALO_C))
                    sp.wait_ge(whi, 2 * i + 2)
                    sp.wait_ge(wlo, 2 * i + 2)
                    load_w(cols[0])
                store_gate(i, 0, tiles[0])
                store_gate(i, 1, tiles[0])
                if not first:
                    finish_last(i, before)
                load_gate(here)
                store_gate(i, 2, tiles[0])
                store_gate(i, 3, tiles[0])
                if not last:
                    sp.wait_ge(whi, 2 * i + 3)
                    sp.wait_ge(wlo, 2 * i + 3)
                    load_w(cols[1])
                    sp.wait_ge(prep_ready, i + 1)
                    sp.wait_ge(t_done, i + 1)
                    load_hgrn(after)
                store_gate(i, 4, tiles[1])
                store_gate(i, 5, tiles[1])
                store_gate(i, 6, tiles[1])
                sp.wait_ge(yc_ready, i + 1)
                store_y(here, 4, yc, yc_stored)
                if not last:
                    load_pool_conv(after, after_p, after_c)
                store_gate(i, 7, tiles[1])

            loop(sp, body)
            finish_last(STEPS, (STEPS - 1) * P)
            for j in range(4):
                sp.wait_ge(stored[j], 16 * 2 * STEPS)
            sp.wait_ge(yh_stored, 16 * STEPS)
            sp.wait_ge(yp_stored, 16 * STEPS)
            sp.wait_ge(yc_stored, 16 * STEPS)

        @block.gpsimd
        def _(pool):
            chain = [0]
            base = [0]
            PER = 13

            def link(ins):
                chain[0] += 1
                ins.then_inc(pchain, 1)
                pool.wait_ge(pchain, base[0] + chain[0])

            tt = nc.gpsimd.tensor_tensor
            nc.gpsimd.memset(pool_bd[:, :, :], 0.0).then_inc(zeroed, 1)
            nc.gpsimd.memset(a_in[:, :, 0:HALO_P], 0.0).then_inc(zeroed, 1)
            nc.gpsimd.memset(c_in[:, :, 0:HALO_C], 0.0).then_inc(zeroed, 1)
            pool.wait_ge(consts_in, 16 * 18)

            def body(i, first, last):
                base[0] = PER * i
                chain[0] = 0
                pool.wait_ge(a_loaded, 32 * (i + 1))
                link(tt(sum2[:, :, 1:], a_in[:, :, 1:], a_in[:, :, :-1], ALU.add))
                link(tt(sum4[:, :, 3:], sum2[:, :, 3:], sum2[:, :, 1:-2], ALU.add))
                link(tt(sum8[:, 7:], sum4[:, 1, 7:], sum4[:, 1, 3:-4], ALU.add))
                if not first:
                    pool.wait_ge(o_done, i)
                tt(win[64:128, 1, :], sum8[64:128, HALO_P:], sum8[64:128, 8:-8], ALU.add)
                nc.gpsimd.tensor_copy(win[0:64, 0, :], sum2[0:64, 0, HALO_P:])
                nc.gpsimd.tensor_copy(win[64:128, 0, :], sum4[64:128, 0, HALO_P:])
                link(nc.gpsimd.tensor_copy(win[0:64, 1, :], sum8[0:64, HALO_P:]))
                inv = inv_first[:, :, :] if first else inv_count[:, :].unsqueeze(2).to_broadcast([P, 2, P])
                link(tt(win[:, :, :], win[:, :, :], inv, ALU.mult))
                tt(win[:, :, :], win[:, :, :], a_in[:, :, HALO_P:], ALU.subtract).then_inc(pooled, 1)
                pool.wait_ge(sigac_ready, i + 1)
                tt(s_ag[:, :, :], s_ag[:, :, :], ag_in[:, :, :], ALU.mult).then_inc(sag_ready, 1)
                pool.wait_ge(c_loaded, 16 * (i + 1))
                link(tt(z_s[:, :, :], c_in[:, 0:2, :], c_in[:, 4:6, :], ALU.mult))
                w = [conv_c[:, k, :].unsqueeze(2).to_broadcast([P, 2, P]) for k in range(3)]
                link(tt(acc[:, :, :], z_s[:, :, 2:], w[2], ALU.mult))
                link(tt(tap[:, :, :], z_s[:, :, 1:-1], w[1], ALU.mult))
                link(tt(acc[:, :, :], acc[:, :, :], tap[:, :, :], ALU.add))
                link(tt(tap[:, :, :], z_s[:, :, :-2], w[0], ALU.mult))
                link(tt(acc[:, :, :], acc[:, :, :], tap[:, :, :], ALU.add))
                link(tt(acc[:, :, :], acc[:, :, :], c_in[:, 2:4, HALO_C:], ALU.mult))
                link(tt(s_cg[:, :, :], s_cg[:, :, :], c_in[:, 6:8, HALO_C:], ALU.mult))
                if not first:
                    pool.wait_ge(yc_stored, 16 * i)
                tt(yc[:, :, :], acc[:, :, :], s_cg[:, :, :], ALU.mult).then_inc(yc_ready, 1)
                assert chain[0] == PER, chain[0]

            loop(pool, body)

        @block.vector
        def _(dve):
            chain = [0]
            base = [0]
            START, PER = 5, 13

            def link(ins):
                chain[0] += 1
                ins.then_inc(dchain, 1)
                dve.wait_ge(dchain, base[0] + chain[0])

            tt, ts, stt = nc.vector.tensor_tensor, nc.vector.tensor_scalar, nc.vector.scalar_tensor_tensor
            nc.vector.memset(S[:, :, :], 0.0).then_inc(zeroed_v, 1)
            nc.vector.memset(epsb[:, :], EPS).then_inc(zeroed_v, 1)
            nc.vector.memset(AT[:, :, :, :], 0.0).then_inc(zeroed_v, 1)
            dve.wait_ge(zeroed_v, 3)
            dve.wait_ge(consts_in, 16 * 18)
            nc.vector.tensor_copy(masks[:, :, :], QX[:, :, 0, :])
            link(tt(lb_x[:, :], lb_x[:, :], lb_x[:, :], ALU.subtract))
            dve.wait_ge(lb_exp, 1)
            link(nc.vector.reciprocal(lb[:, :], lb_e[:, :]))
            link(tt(lb[:, :], lb[:, :], lb_e[:, :], ALU.mult))
            link(tt(lb[:, :], lb[:, :], lb[:, :], ALU.subtract))
            link(ts(omlb[:, :], lb[:, :], -1.0, 1.0, ALU.mult, ALU.add))
            assert chain[0] == START

            def lo(tile, j):
                dve.wait_ge(whi, tile + 1)
                tt(w_lo[j][:, :, :], w_stage[:, :, :], w_hi[j][:, :, :].bitcast(F32), ALU.subtract).then_inc(wlo, 1)

            lo(0, 0)
            lo(1, 1)

            def advance_state(i):
                dve.wait_ge(o_done, i)
                tt(kvm[:, :, :], b7[:, 0:2, :], head_m[:, :].unsqueeze(1).to_broadcast([P, 2, P]), ALU.mult).then_inc(dchain, 1)
                chain[0] += 1
                dve.wait_ge(dchain, base[0] + chain[0])
                for t in range(2):
                    last = stt(S[:, t, :], S[:, t, :], eb[:, t, P - 1:P], kvm[:, t, :], ALU.mult, ALU.add)
                last.then_inc(state_done, 1)
                dve.wait_ge(sag_ready, i)

            def pool_out(i, second):
                dve.wait_ge(osq_ready, i)
                if not second:
                    dve.wait_ge(yp_stored, 16 * (i - 1))
                for t in range(2):
                    last = stt(yp[:, t, :], b6[:, 2 + t, :], pool_sc[:, t:t + 1], s_ag[:, t, :], ALU.mult, ALU.mult)
                last.then_inc(yp_ready, 1)

            def finish(i, second):
                dve.wait_ge(sigg_ready, i)
                link(tt(sgate[:, :, :], sgate[:, :, :], g_in[:, :, :], ALU.mult))
                dve.wait_ge(rstd_ready, i)
                link(tt(rs[:, :, :], b6[:, 0:2, :], rs[:, :, :], ALU.mult))
                if not second:
                    dve.wait_ge(yh_stored, 16 * (i - 1))
                stt(yh[:, :, :], rs[:, :, :], norm_c[:, :], sgate[:, :, :], ALU.mult, ALU.mult).then_inc(fin_done, 1)

            def body(i, first, last, second=False):
                base[0] = START + PER * i
                chain[0] = 0
                if first:
                    for _ in range(3):
                        link(nc.vector.memset(kvm[:, 0, 0:1], 0.0))
                else:
                    advance_state(i)
                    pool_out(i, second)
                dve.wait_ge(sig_ready, i + 1)
                for t in range(2):
                    ts(k_s[:, t, :], k_s[:, t, :], omlb[:, t:t + 1], None, ALU.mult)
                for t in range(2):
                    ins = ts(f_s[:, t, :], f_s[:, t, :], omlb[:, t:t + 1], lb[:, t:t + 1], ALU.mult, ALU.add)
                link(ins)
                ts(f_ab[:, 0, :, :], f_s[:, :, :], SPLIT, None, ALU.max)
                ts(f_ab[:, 1, :, :], f_s[:, :, :], MIN_F, SPLIT, ALU.max, ALU.min).then_inc(clipped, 1)
                link(tt(q_s[:, :, :], q_s[:, :, :], in3[:, 0:2, :], ALU.mult))
                dve.wait_ge(logged, i + 1)
                link(tt(f_s[:, :, :], f_ab[:, 0, :, :], f_ab[:, 1, :, :], ALU.add))
                link(nc.vector.tensor_tensor_scan(b_s[:, :, :].rearrange("p n t -> p (n t)"), scan_m[:, :],
                                                  f_s[:, :, :].rearrange("p n t -> p (n t)"), 0.0, ALU.mult, ALU.add))
                nc.vector.tensor_copy(f_s[:, 0, 0:1], b_s[:, 0, 0:1]).then_inc(scanned, 1)
                if not first:
                    dve.wait_ge(r_done, 4 * i)
                for n, m in enumerate(LEVELS):
                    v = b_s[:, :, :].rearrange("p n t -> p (n t)").rearrange("p (n u) -> p n u", u=2 * m)
                    o = X[:, n, :, :].rearrange("p n t -> p (n t)").rearrange("p (n u) -> p n u", u=2 * m)
                    ref = v[:, :, m - 1:m].to_broadcast([P, P // m, 2 * m])
                    ins = tt(o, v, ref, ALU.subtract)
                link(ins)
                flat = X[:, 0:NL - 1, :, :].rearrange("p l n t -> p (l n t)")
                stt(flat, flat, -1.0, flat, ALU.mult, ALU.min).then_inc(spread, 1)
                dve.wait_ge(decayed, i + 1)
                tt(kt[:, :, :], kt[:, :, :], k_s[:, :, :], ALU.mult).then_inc(kt_ready, 1)
                tt(qe[:, :, :], q_s[:, :, :], eb[:, :, :], ALU.mult)
                nc.vector.tensor_copy(QX[:, NL - 1, :, :], q_s[:, :, :])
                nc.vector.tensor_copy(X[:, NL - 1, :, :], k_s[:, :, :])
                dve.wait_ge(xready, i + 1)
                link(tt(QX[:, 0:NL - 1, :, :], X[:, 0:NL - 1, :, :],
                        q_s[:, :, :].unsqueeze(1).to_broadcast([P, NL - 1, 2, P]), ALU.mult))
                tt(X[:, 0:NL - 1, :, :], X[:, 0:NL - 1, :, :],
                   k_s[:, :, :].unsqueeze(1).to_broadcast([P, NL - 1, 2, P]), ALU.mult).then_inc(prep_ready, 1)
                if not first:
                    finish(i, second)
                for r in range(4):
                    dve.wait_ge(r_done, 4 * i + r + 1)
                    m = masks[:, 4 * (r % 2):4 * (r % 2) + 4, :]
                    for h in range(2):
                        ins = tt(picks[:, h, :, :], score[:, h, :, :], m, ALU.mult)
                    ins.then_inc(picked, 1)
                    dve.wait_ge(picked, 4 * i + r + 1)
                    out = AT if r % 2 == 0 else part
                    link(nc.vector.tensor_reduce(out[:, r // 2, :, :].rearrange("p h t -> p (h t)") if r % 2 == 0 else out[:, :, :].rearrange("p h t -> p (h t)"),
                                                 picks[:, :, :, :].rearrange("p h n t -> p h t n"), AX.X, ALU.add))
                    if r % 2:
                        tt(AT[:, r // 2, :, :], AT[:, r // 2, :, :], part[:, :, :], ALU.add).then_inc(attn_ready, 1)
                    if r == 0 and not last:
                        lo(2 * i + 2, 0)
                if not last:
                    lo(2 * i + 3, 1)

            body(0, True, False)
            assert chain[0] == PER
            body(1, False, False, second=True)
            assert chain[0] == PER
            with dve.Fori(2, STEPS - 1) as i:
                body(i, False, False)
            body(STEPS - 1, False, True)
            base[0] = START + PER * STEPS
            chain[0] = 0
            advance_state(STEPS)
            pool_out(STEPS, False)
            finish(STEPS, False)

        @block.scalar
        def _(act):
            chain = [0]
            base = [0]

            def link(ins):
                chain[0] += 1
                ins.then_inc(achain, 1)
                act.wait_ge(achain, base[0] + chain[0])

            a = nc.scalar.activation
            act.wait_ge(dchain, 1)
            a(lb_e[:, :], lb_x[:, :], ACT.Exp).then_inc(lb_exp, 1)

            def hi(tile, j, fresh):
                act.wait_ge(w_loaded, 16 * (tile + 1))
                if not fresh:
                    act.wait_ge(ps_ready, 4 * (tile - 1))
                a(w_hi[j][:, :, :], w_stage[:, :, :], ACT.Copy).then_inc(whi, 1)

            hi(0, 0, True)
            hi(1, 1, True)

            def evacuate(i, s, first):
                act.wait_ge(ps_ready, 8 * i + s + 1)
                if not (first and s < 4):
                    act.wait_ge(stored[s % 4], 16 * (2 * i + s // 4))
                a(g_out[s % 4][:, :], bank[s % 4][:, :], ACT.Copy).then_inc(evac, 1)

            def squares(i):
                act.wait_ge(o_done, i)
                a(osq[:, :, :], b6[:, 0:2, :], ACT.Square).then_inc(osq_ready, 1)

            def gate_sigmoid(i, second):
                act.wait_ge(g_loaded, 16 * i)
                a(sgate[:, :, :], g_in[:, :, :], ACT.Sigmoid).then_inc(sigg_ready, 1)

            def root(i):
                act.wait_ge(n_done, i)
                link(a(rs[:, :, :], b7[:, 2:4, :], ACT.Ln, bias=epsb[:, :]))
                a(rs[:, :, :], rs[:, :, :], ACT.Exp, scale=-0.5).then_inc(rstd_ready, 1)

            def body(i, first, last):
                base[0] = i - 1 if not first else 0
                chain[0] = 0
                if not first:
                    squares(i)
                act.wait_ge(in3_loaded, 16 * (i + 1))
                if not first:
                    act.wait_ge(prep_ready, i)
                a(f_s[:, :, :], in3[:, 2:4, :], ACT.Sigmoid)
                a(k_s[:, :, :], in3[:, 2:4, :], ACT.Sigmoid, scale=-1.0)
                a(q_s[:, :, :], in3[:, 0:2, :], ACT.Sigmoid).then_inc(sig_ready, 1)
                if not first:
                    act.wait_ge(yp_ready, i)
                    gate_sigmoid(i, False)
                act.wait_ge(a_loaded, 32 * (i + 1))
                a(s_ag[:, :, :], ag_in[:, :, :], ACT.Sigmoid)
                act.wait_ge(c_loaded, 16 * (i + 1))
                a(s_cg[:, :, :], c_in[:, 6:8, HALO_C:], ACT.Sigmoid).then_inc(sigac_ready, 1)
                act.preload_act_table_set("natural_log_exp_and_others")
                act.wait_ge(clipped, i + 1)
                a(f_ab[:, 0, :, :], f_ab[:, 0, :, :], ACT.Ln)
                a(f_ab[:, 1, :, :], f_ab[:, 1, :, :], ACT.Ln, scale=1.0 / SPLIT).then_inc(logged, 1)
                evacuate(i, 0, first)
                if not first:
                    root(i)
                act.wait_ge(scanned, i + 1)
                if not first:
                    act.wait_ge(state_done, i)
                a(eb[:, :, :], b_s[:, :, :], ACT.Exp)
                if not first:
                    act.wait_ge(t_done, i)
                for t in range(2):
                    ins = a(kt[:, t, :], b_s[:, t, :], ACT.Exp, bias=b_s[:, t, P - 1:P], scale=-1.0)
                ins.then_inc(decayed, 1)
                evacuate(i, 1, first)
                act.wait_ge(spread, i + 1)
                a(X[:, 0:NL - 1, :, :], X[:, 0:NL - 1, :, :], ACT.Exp).then_inc(xready, 1)
                evacuate(i, 2, first)
                evacuate(i, 3, first)
                if not last:
                    hi(2 * i + 2, 0, False)
                act.wait_ge(t_done, i + 1)
                if not first:
                    act.wait_ge(o_done, i)
                a(tok[:, :, :], b6[:, :, :], ACT.Copy).then_inc(tok_ready, 1)
                for s in range(4, 8):
                    evacuate(i, s, first)
                if not last:
                    hi(2 * i + 3, 1, False)

            loop(act, body)
            base[0] = STEPS - 1
            chain[0] = 0
            squares(STEPS)
            gate_sigmoid(STEPS, False)
            root(STEPS)

        @block.tensor
        def _(pe):
            mm = nc.tensor.matmul
            pe.wait_ge(zeroed_v, 3)
            pe.wait_ge(consts_in, 16 * 18)

            def segment(i, s, first):
                j, g = divmod(s, 4)
                if g == 0:
                    pe.wait_ge(wlo, 2 * i + j + 1)
                if not (first and j == 0):
                    pe.wait_ge(evac, 8 * i + s - 3)
                cols = slice(g * TG, (g + 1) * TG)
                for k in range(KD):
                    mm(bank[g][:, :], w_hi[j][:, k, :], h_hi[:, k, cols], start=(k == 0), stop=False)
                    mm(bank[g][:, :], w_hi[j][:, k, :], h_lo[:, k, cols], start=False, stop=False)
                    last = mm(bank[g][:, :], w_lo[j][:, k, :], h_hi[:, k, cols], start=False, stop=(k == KD - 1))
                last.then_inc(ps_ready, 1)

            def norms(i):
                pe.wait_ge(osq_ready, i)
                pe.wait_ge(state_done, i)
                mm(b7[:, 2:4, :], mean_w[:, :], osq[:, :, :], start=True, stop=True).then_inc(n_done, 1)

            def transposes(i, first):
                pe.wait_ge(kt_ready, i + 1)
                if not first:
                    pe.wait_ge(fin_done, i)
                    pe.wait_ge(yp_ready, i)
                for t in range(2):
                    nc.tensor.transpose(b6[:, t, :], in3[:, 4 + t, :], ident[:, :])
                    last = nc.tensor.transpose(b6[:, 2 + t, :], kt[:, t, :], ident[:, :])
                last.then_inc(t_done, 1)

            def scores(i, r, first):
                if r == 0:
                    pe.wait_ge(prep_ready, i + 1)
                if not (first and r == 0):
                    pe.wait_ge(picked, 4 * i + r)
                t = r // 2
                for n in range(4):
                    for h in range(2):
                        rows = slice(64 * h, 64 * h + 64)
                        last = mm(score[:, h, n, :], X[rows, 4 * (r % 2) + n, t, :], QX[rows, 4 * (r % 2) + n, t, :],
                                  start=True, stop=True)
                last.then_inc(r_done, 1)

            def outputs(i, first):
                pe.wait_ge(attn_ready, 2 * i + 2)
                pe.wait_ge(tok_ready, i + 1)
                pe.wait_ge(pooled, i + 1)
                if not first:
                    pe.wait_ge(state_done, i)
                for t in range(2):
                    mm(b6[:, t, :], S[:, t, :], qe[:, t, :], start=True, stop=False, skip_group_check=True)
                    for h in range(2):
                        mm(b6[64 * h:64 * h + 64, t, :], tok[:, t, 64 * h:64 * h + 64], AT[:, t, h, :], start=False, stop=True,
                           skip_group_check=True)
                for t in range(2):
                    mm(b6[:, 2 + t, :], pool_bd[:, t, :], win[:, t, :], start=True, stop=True, skip_group_check=True)
                for t in range(2):
                    last = mm(b7[:, t, :], tok[:, 2 + t, :], tok[:, t, :], start=True, stop=True)
                last.then_inc(o_done, 1)

            def body(i, first, last):
                segment(i, 0, first)
                if not first:
                    norms(i)
                segment(i, 1, first)
                segment(i, 2, first)
                segment(i, 3, first)
                transposes(i, first)
                scores(i, 0, first)
                segment(i, 4, first)
                scores(i, 1, first)
                segment(i, 5, first)
                scores(i, 2, first)
                segment(i, 6, first)
                scores(i, 3, first)
                segment(i, 7, first)
                outputs(i, first)

            loop(pe, body)
            norms(STEPS)


HEADS = 4
DH = 64
LAM_INIT = 0.8 - 0.6 * float(np.exp(-0.3 * 0))
NEG = -1e30


def differential_attention(nc, pT, yT, consts, diff_lam, diff_norm, c, w_ada, b_ada, g_post, post):
    with ExitStack() as ctx:
        def sb(name, shape, dt=F32):
            return ctx.enter_context(nc.sbuf_tensor("C_" + name, shape, dt))

        def sem(name):
            return ctx.enter_context(nc.semaphore("C_" + name))

        q_in = sb("q_in", [P, 2, T])
        k_in = sb("k_in", [P, 2, T])
        v_in = sb("v_in", [P, T])
        g_in = sb("g_in", [P, T])
        g_sig = sb("g_sig", [P, T])
        ks = sb("ks", [P, 2, T], F32R)
        q_hi = sb("q_hi", [P, 2, T], F32R)
        q_lo = sb("q_lo", [P, 2, T], F32R)
        v_tok = sb("v_tok", [P, NT, P])
        prob = [sb(f"prob{j}", [P, 2, T]) for j in range(3)]
        at = [sb(f"at{j}", [P, NT, P]) for j in range(2)]
        on = sb("on", [P, P])
        junk = sb("junk", [P, P])
        y_out = sb("y_out", [P, 2, P])
        ident = sb("ident", [P, P])
        ident_r = sb("ident_r", [P, P], F32R)
        causal = sb("causal", [P, P])
        causal_r = sb("causal_r", [P, P], F32R)
        lam_in = sb("lam_in", [P, 4, DH])
        lam_p = sb("lam_p", [P, 2, DH])
        lam_s = sb("lam_s", [P, 2])
        nlam = sb("nlam", [P, 1])
        norm_c = sb("norm_c", [P, 1])
        epsb = sb("epsb", [P, 1])
        negm = [sb(f"negm{j}", [P, 2, 4]) for j in range(2)]
        sums = [sb(f"sums{j}", [P, 2, 4]) for j in range(2)]
        nm = sb("nm", [P, 2])
        dist = sb("dist", [P, 2, 4])
        wts = sb("wts", [P, 2, 4])
        wsum = sb("wsum", [P, 2, 4])
        tot = sb("tot", [P, 2])
        inv = sb("inv", [P, 2])
        cf = sb("cf", [P, 2, 4])
        ssq = sb("ssq", [P, 1])
        rstd = sb("rstd", [P, 1])
        c_col = sb("c_col", [P, KD])
        c_act = sb("c_act", [P, KD])
        ada_in = [sb(f"ada_in{j}", [P, D]) for j in range(2)]
        ada_p = sb("ada_p", [P, D])
        ada_sum = sb("ada_sum", [P, D])
        ada_b = sb("ada_b", [P, D])
        g_row = sb("g_row", [P, D])
        ones = sb("ones", [P, P])
        sc = [ctx.enter_context(nc.psum_tensor(f"C_sc{j}", [P, 2, TG], F32)) for j in range(2)]
        tb = [ctx.enter_context(nc.psum_tensor(f"C_tb{j}", [P, 4, P], F32)) for j in range(2)]
        ob = ctx.enter_context(nc.psum_tensor("C_ob", [P, TG], F32))
        otb = ctx.enter_context(nc.psum_tensor("C_otb", [P, TG], F32))

        consts_in, setup, setup_v = sem("consts_in"), sem("setup"), sem("setup_v")
        qk_loaded, v_loaded, g_loaded = sem("qk_loaded"), sem("v_loaded"), sem("g_loaded")
        hi_ready, lo_ready, vt_ready, v_ready = sem("hi_ready"), sem("lo_ready"), sem("vt_ready"), sem("v_ready")
        gsig_ready, gs_ready = sem("gsig_ready"), sem("gs_ready")
        s_ready, max_ready, exp_done = sem("s_ready"), sem("max_ready"), sem("exp_done")
        d_ready, w_ready, a_ready = sem("d_ready"), sem("w_ready"), sem("a_ready")
        t_ready, at_ready = sem("t_ready"), sem("at_ready")
        pv_done, rstd_ready, on_ready, ot_ready, y_ready = (sem(n) for n in ("pv_done", "rstd_ready", "on_ready", "ot_ready", "y_ready"))
        y_stored = [sem(f"y_stored{j}") for j in range(2)]
        dchain, achain, c_done = sem("dchain"), sem("achain"), sem("c_done")
        c_sig, ones_set, pchain = sem("c_sig"), sem("ones_set"), sem("pchain")
        ada_loaded, rows_loaded, ada_used = [sem(f"ada_loaded{j}") for j in range(2)], sem("rows_loaded"), sem("ada_used")
        gate_ready, post_ready = sem("gate_ready"), sem("post_ready")

        block = ctx.enter_context(nc.Block())
        U = NT
        pieces = [(u + 4) // 4 for u in range(U)]
        before = [sum(pieces[:u]) for u in range(U + 1)]
        NP = before[U]
        multi_before = [sum(p > 1 for p in pieces[:u]) for u in range(U + 1)]
        multi = multi_before[U]

        def width(u, p):
            return min(TG, (u + 1) * P - p * TG)

        @block.sync
        def _(sp):
            sp.dma_start(ident[:, :], consts["ident"]).then_inc(consts_in, 16)
            sp.dma_start(causal[:, :], consts["causal"]).then_inc(consts_in, 16)
            sp.dma_start(c_col[:, :], c.rearrange("a (k p) -> p (a k)", p=P), allow_slow_non_contiguous=True).then_inc(consts_in, 16)
            sp.dma_start(lam_in[:, :, :].rearrange("p a d -> p (a d)"),
                         diff_lam.rearrange("a l d -> a (l d)").to_broadcast([P, 4 * DH])).then_inc(consts_in, 16)
            sp.dma_start(norm_c[:, :], diff_norm.rearrange("a p -> p a"), allow_slow_non_contiguous=True).then_inc(consts_in, 16)

            def load(h):
                tiles = [h + 20, h + 24, h + 28, h + 32] if isinstance(h, int) else [sp.snap(h + n) for n in (20, 24, 28, 32)]
                if not isinstance(h, int):
                    sp.wait_ge(lo_ready, 4 * h)
                for m in range(2):
                    for half in range(2):
                        rows = slice(DH * half, DH * half + DH)
                        sp.dma_start(k_in[rows, m, :], pT[bass.ds(tiles[1], 1), DH * m:DH * m + DH, :].rearrange("a p t -> (a p) t")).then_inc(qk_loaded, 16)
                        sp.dma_start(q_in[rows, m, :], pT[bass.ds(tiles[0], 1), DH * m:DH * m + DH, :].rearrange("a p t -> (a p) t")).then_inc(qk_loaded, 16)
                if not isinstance(h, int):
                    sp.wait_ge(vt_ready, 4 * h)
                sp.dma_start(v_in[:, :], pT[bass.ds(tiles[2], 1), :, :].rearrange("a p t -> (a p) t")).then_inc(v_loaded, 16)
                if not isinstance(h, int):
                    sp.wait_ge(gs_ready, h)
                sp.dma_start(g_in[:, :], pT[bass.ds(tiles[3], 1), :, :].rearrange("a p t -> (a p) t")).then_inc(g_loaded, 16)

            def store(h, u, tile):
                sp.wait_ge(y_ready, U * h + u + 1)
                sp.dma_start(yT[bass.ds(tile, 1), :, u * P:(u + 1) * P].rearrange("a p t -> (a p) t"),
                             y_out[:, u % 2, :]).then_inc(y_stored[u % 2], 16)

            load(0)
            sp.dma_start(ada_b[:, :], b_ada[:, 2 * D:3 * D].to_broadcast([P, D])).then_inc(rows_loaded, 16)
            sp.dma_start(g_row[:, :], g_post.to_broadcast([P, D])).then_inc(rows_loaded, 16)
            ada_v = w_ada.rearrange("a (k p) n -> p (a k) n", p=P)
            for k in range(2):
                sp.dma_start(ada_in[k][:, :], ada_v[:, k, 2 * D:3 * D]).then_inc(ada_loaded[k], 16)
            with sp.Fori(0, HEADS - 1) as h:
                tile = sp.snap(h + 6)
                load(sp.snap(h + 1))
                for u in range(U):
                    store(h, u, tile)
            for u in range(U):
                store(HEADS - 1, u, HEADS + 5)
                if 2 <= u + 2 < KD:
                    sp.wait_ge(ada_used, u + 1)
                    sp.dma_start(ada_in[u % 2][:, :], ada_v[:, u + 2, 2 * D:3 * D]).then_inc(ada_loaded[u % 2], 16)
            for j in range(2):
                sp.wait_ge(y_stored[j], 16 * HEADS * U // 2)

        @block.gpsimd
        def _(pool):
            with pool.Fori(0, HEADS) as h:
                pool.wait_ge(gsig_ready, h + 1)
                nc.gpsimd.tensor_tensor(g_sig[:, :], g_sig[:, :], g_in[:, :], ALU.mult).then_inc(gs_ready, 1)
            chain = [0]

            def link(ins):
                chain[0] += 1
                ins.then_inc(pchain, 1)
                pool.wait_ge(pchain, chain[0])

            pool.wait_ge(c_sig, 1)
            link(nc.gpsimd.tensor_tensor(c_act[:, :], c_act[:, :], c_col[:, :], ALU.mult))
            link(nc.gpsimd.memset(ada_sum[:, :], 0.0))
            nc.gpsimd.memset(ones[:, :], 1.0).then_inc(ones_set, 1)
            for k in range(KD):
                pool.wait_ge(ada_loaded[k % 2], 16 * (k // 2 + 1))
                nc.gpsimd.tensor_scalar(ada_p[:, :], ada_in[k % 2][:, :], c_act[:, k:k + 1], None, ALU.mult).then_inc(ada_used, 1)
                pool.wait_ge(ada_used, k + 1)
                link(nc.gpsimd.tensor_tensor(ada_sum[:, :], ada_sum[:, :], ada_p[:, :], ALU.add))

        @block.vector
        def _(dve):
            chain = [0]
            base = [0]
            START = 5
            PER = 5 * sum(p > 1 for p in pieces) + NP

            def link(ins):
                chain[0] += 1
                ins.then_inc(dchain, 1)
                dve.wait_ge(dchain, base[0] + chain[0])

            tt, ts, stt = nc.vector.tensor_tensor, nc.vector.tensor_scalar, nc.vector.scalar_tensor_tensor
            nc.vector.memset(epsb[:, :], EPS).then_inc(setup_v, 1)
            dve.wait_ge(consts_in, 80)
            nc.vector.tensor_copy(ident_r[:, :], ident[:, :]).then_inc(setup_v, 1)
            nc.vector.tensor_copy(causal_r[:, :], causal[:, :]).then_inc(setup_v, 1)
            lv = lam_in[:, :, :].rearrange("p (a b) d -> p a b d", b=2)
            link(tt(lam_p[:, :, :], lv[:, :, 0, :], lv[:, :, 1, :], ALU.mult))
            nc.vector.tensor_reduce(lam_s[:, :], lam_p[:, :, :], AX.X, ALU.add).then_inc(setup_v, 1)
            dve.wait_ge(setup, 1)
            link(tt(nlam[:, :], lam_s[:, 1:2], lam_s[:, 0:1], ALU.subtract))
            link(ts(nlam[:, :], nlam[:, :], -LAM_INIT, None, ALU.add))
            link(ts(norm_c[:, :], norm_c[:, :], 1.0 - LAM_INIT, None, ALU.mult))
            link(nc.vector.memset(junk[:, 0:1], 0.0))
            assert chain[0] == START

            def maximum(h, u, p):
                n = before[u] + p
                w = width(u, p)
                dve.wait_ge(s_ready, NP * h + n + 1)
                nc.vector.tensor_reduce(negm[u % 2][:, :, p:p + 1], sc[n % 2][:, :, 0:w], AX.X, ALU.max,
                                        negate=True).then_inc(max_ready, 1)

            def weights(h, u):
                np_ = pieces[u]
                dve.wait_ge(a_ready, U * h + u)
                sm, ng = sums[u % 2], negm[u % 2]
                if np_ > 1:
                    link(nc.vector.tensor_reduce(nm[:, :], ng[:, :, 0:np_], AX.X, ALU.min))
                    tt(dist[:, :, 0:np_], ng[:, :, 0:np_], nm[:, :].unsqueeze(2).to_broadcast([P, 2, np_]),
                       ALU.subtract).then_inc(d_ready, 1)
                    dve.wait_ge(exp_done, NP * h + before[u] + np_)
                    dve.wait_ge(w_ready, multi * h + multi_before[u] + 1)
                    link(tt(wsum[:, :, 0:np_], wts[:, :, 0:np_], sm[:, :, 0:np_], ALU.mult))
                    link(nc.vector.tensor_reduce(tot[:, :], wsum[:, :, 0:np_], AX.X, ALU.add))
                    link(nc.vector.reciprocal(inv[:, :], tot[:, :]))
                    link(tt(cf[:, :, 0:np_], wts[:, :, 0:np_], inv[:, :].unsqueeze(2).to_broadcast([P, 2, np_]), ALU.mult))
                else:
                    dve.wait_ge(exp_done, NP * h + before[u] + 1)
                    nc.vector.reciprocal(cf[:, :, 0:1], sm[:, :, 0:1]).then_inc(c_done, 1)
                    dve.wait_ge(c_done, 4 * h + u + 1)

            def combine(h, u, p):
                keys = slice(p * TG, p * TG + width(u, p))
                pr = prob[u % 3]
                link(ts(pr[:, 1, keys], pr[:, 1, keys], cf[:, 1, p:p + 1], nlam[:, :], ALU.mult, ALU.mult))
                ins = stt(pr[:, 0, keys], pr[:, 0, keys], cf[:, 0, p:p + 1], pr[:, 1, keys], ALU.mult, ALU.add)
                if p == pieces[u] - 1:
                    ins.then_inc(a_ready, 1)

            def normalise(h, u):
                dve.wait_ge(rstd_ready, U * h + u + 1)
                dve.wait_ge(ot_ready, U * h + u)
                ts(on[:, :], ob[:, 0:P], rstd[:, :], None, ALU.mult).then_inc(on_ready, 1)

            def gate(h, u, wait_store):
                dve.wait_ge(ot_ready, U * h + u + 1)
                if u == 0:
                    dve.wait_ge(gs_ready, h + 1)
                dve.wait_ge(y_stored[u % 2], 16 * (U // 2 * h + u // 2))
                stt(y_out[:, u % 2, :], otb[:, 0:P], norm_c[:, :], g_sig[:, u * P:(u + 1) * P], ALU.mult,
                    ALU.mult).then_inc(y_ready, 1)

            with dve.Fori(0, HEADS) as h:
                base[0] = START + PER * h
                chain[0] = 0
                dve.wait_ge(qk_loaded, 128 * (h + 1))
                for m in range(2):
                    dve.wait_ge(hi_ready, 4 * h + 2 * m + 1)
                    tt(ks[DH:P, m, :], k_in[DH:P, m, :], ks[DH:P, m, :].bitcast(F32), ALU.subtract).then_inc(lo_ready, 1)
                    dve.wait_ge(hi_ready, 4 * h + 2 * m + 2)
                    stt(q_lo[:, m, :], q_in[:, m, :], DH ** -0.5, q_hi[:, m, :].bitcast(F32), ALU.mult,
                        ALU.subtract).then_inc(lo_ready, 1)
                for u in range(U + 5):
                    top = [(maximum, u, p) for p in range(pieces[u])] if u < U else []
                    rest = []
                    if 0 <= u - 1 < U:
                        rest += [(lambda h, u, p: weights(h, u), u - 1, 0)]
                        rest += [(combine, u - 1, p) for p in range(pieces[u - 1])]
                    for step in merged(top, rest):
                        step[0](h, step[1], step[2])
                    if 0 <= u - 3 < U:
                        normalise(h, u - 3)
                    if 0 <= u - 4 < U:
                        gate(h, u - 4, True)
                assert chain[0] == PER, (chain[0], PER)
            dve.wait_ge(gate_ready, 1)
            dve.wait_ge(rows_loaded, 32)
            tt(post[:, :], sc[0][:, :, :].rearrange("p a n -> p (a n)"), ada_b[:, :], ALU.add).then_inc(post_ready, 1)
            dve.wait_ge(post_ready, 1)
            tt(post[:, :], post[:, :], g_row[:, :], ALU.mult).then_inc(post_ready, 1)

        @block.scalar
        def _(act):
            a = nc.scalar.activation
            act.wait_ge(setup_v, 4)
            a(lam_s[:, :], lam_s[:, :], ACT.Exp).then_inc(setup, 1)
            act.wait_ge(consts_in, 80)
            a(c_act[:, :], c_col[:, :], ACT.Sigmoid).then_inc(c_sig, 1)

            def exps(h, u, p):
                n = before[u] + p
                w = width(u, p)
                act.wait_ge(max_ready, NP * h + n + 1)
                if p == 0 and u >= 3:
                    act.wait_ge(t_ready, NP * h + before[u - 2])
                for m in range(2):
                    ins = a(prob[u % 3][:, m, p * TG:p * TG + w], sc[n % 2][:, m, 0:w], ACT.Exp,
                            bias=negm[u % 2][:, m, p:p + 1], accum_out=sums[u % 2][:, m, p:p + 1])
                ins.then_inc(exp_done, 1)

            def wexp(h, u):
                if pieces[u] > 1:
                    act.wait_ge(d_ready, multi * h + multi_before[u] + 1)
                    a(wts[:, :, 0:pieces[u]], dist[:, :, 0:pieces[u]], ACT.Exp, scale=-1.0).then_inc(w_ready, 1)

            def evacuate(h, u, p):
                n = before[u] + p
                nb = width(u, p) // P
                act.wait_ge(t_ready, NP * h + n + 1)
                if p == 0:
                    if u >= 2:
                        act.wait_ge(pv_done, U * h + u - 1)
                a(at[u % 2][:, 4 * p:4 * p + nb, :], tb[n % 2][:, 0:nb, :], ACT.Copy).then_inc(at_ready, 1)

            def root(h, u):
                act.wait_ge(pv_done, U * h + u + 1)
                act.wait_ge(on_ready, U * h + u)
                a(junk[:, :], ob[:, 0:P], ACT.Square, accum_out=ssq[:, :]).then_inc(achain, 1)
                act.wait_ge(achain, 2 * (U * h + u) + 1)
                a(ssq[:, :], ssq[:, :], ACT.Ln, bias=epsb[:, :], scale=1.0 / P).then_inc(achain, 1)
                act.wait_ge(achain, 2 * (U * h + u) + 2)
                a(rstd[:, :], ssq[:, :], ACT.Exp, scale=-0.5).then_inc(rstd_ready, 1)

            with act.Fori(0, HEADS) as h:
                act.wait_ge(qk_loaded, 128 * (h + 1))
                act.wait_ge(s_ready, NP * h)
                for m in range(2):
                    a(ks[:, m, :], k_in[:, m, :], ACT.Copy).then_inc(hi_ready, 1)
                    a(q_hi[:, m, :], q_in[:, m, :], ACT.Copy, scale=DH ** -0.5).then_inc(hi_ready, 1)
                act.wait_ge(g_loaded, 16 * (h + 1))
                act.wait_ge(y_ready, U * h)
                a(g_sig[:, :], g_in[:, :], ACT.Sigmoid).then_inc(gsig_ready, 1)
                act.preload_act_table_set("natural_log_exp_and_others")
                for n in range(4):
                    act.wait_ge(vt_ready, 4 * h + n + 1)
                    a(v_tok[:, 4 * n:4 * n + 4, :], tb[n % 2][:, :, :], ACT.Copy).then_inc(v_ready, 1)
                for u in range(U + 5):
                    top = [(exps, u, p) for p in range(pieces[u])] if u < U else []
                    rest = []
                    if 0 <= u - 1 < U:
                        wexp(h, u - 1)
                    if 0 <= u - 2 < U:
                        rest += [(evacuate, u - 2, p) for p in range(pieces[u - 2])]
                    for step in merged(top, rest):
                        step[0](h, step[1], step[2])
                    if 0 <= u - 3 < U:
                        root(h, u - 3)

        @block.tensor
        def _(pe):
            mm = nc.tensor.matmul
            pe.wait_ge(setup_v, 4)

            def scores(h, u, p):
                n = before[u] + p
                w = width(u, p)
                if n >= 2:
                    pe.wait_ge(exp_done, NP * h + n - 1)
                q = slice(u * P, (u + 1) * P)
                keys = slice(p * TG, p * TG + w)
                last_piece = p == pieces[u] - 1
                for m in range(2):
                    mm(sc[n % 2][:, m, 0:w], q_hi[:, m, q], ks[:, m, keys], start=True, stop=False)
                    last = mm(sc[n % 2][:, m, 0:w], q_lo[:, m, q], ks[:, m, keys], start=False, stop=True)
                    if last_piece:
                        last = mm(sc[n % 2][:, m, w - P:w], ident_r[:, :], causal_r[:, :], start=False, stop=True,
                                  skip_group_check=True)
                last.then_inc(s_ready, 1)

            def turn(h, u, p):
                n = before[u] + p
                if p == 0:
                    pe.wait_ge(a_ready, U * h + u + 1)
                if n >= 2:
                    pe.wait_ge(at_ready, NP * h + n - 1)
                else:
                    pe.wait_ge(v_ready, 4 * h + 4)
                    pe.wait_ge(at_ready, NP * h)
                for b in range(width(u, p) // P):
                    last = nc.tensor.transpose(tb[n % 2][:, b, :], prob[u % 3][:, 0, p * TG + b * P:p * TG + (b + 1) * P],
                                               ident[:, :])
                last.then_inc(t_ready, 1)

            def values(h, u, p):
                if p == 0:
                    pe.wait_ge(on_ready, U * h + u)
                pe.wait_ge(at_ready, NP * h + before[u] + p + 1)
                for b in range(4 * p, min(4 * p + 4, u + 1)):
                    last = mm(ob[:, 0:P], at[u % 2][:, b, :], v_tok[:, b, :], start=(b == 0), stop=(b == u))
                if p == pieces[u] - 1:
                    last.then_inc(pv_done, 1)

            def turn_back(h, u):
                pe.wait_ge(on_ready, U * h + u + 1)
                pe.wait_ge(y_ready, U * h + u)
                nc.tensor.transpose(otb[:, 0:P], on[:, :], ident[:, :]).then_inc(ot_ready, 1)

            with pe.Fori(0, HEADS) as h:
                pe.wait_ge(v_loaded, 16 * (h + 1))
                pe.wait_ge(pv_done, U * h)
                for n in range(4):
                    if n < 2:
                        pe.wait_ge(at_ready, NP * h)
                    else:
                        pe.wait_ge(v_ready, 4 * h + n - 1)
                    for b in range(4):
                        last = nc.tensor.transpose(tb[n % 2][:, b, :], v_in[:, (4 * n + b) * P:(4 * n + b + 1) * P], ident[:, :])
                    last.then_inc(vt_ready, 1)
                pe.wait_ge(lo_ready, 4 * h + 4)
                pe.wait_ge(exp_done, NP * h)
                for u in range(U + 5):
                    top = [(scores, u, p) for p in range(pieces[u])] if u < U else []
                    rest = []
                    if 0 <= u - 2 < U:
                        rest += [(turn, u - 2, p) for p in range(pieces[u - 2])]
                    if 0 <= u - 3 < U:
                        rest += [(values, u - 3, p) for p in range(pieces[u - 3])]
                    for step in merged(top, rest):
                        step[0](h, step[1], step[2])
                    if 0 <= u - 4 < U:
                        turn_back(h, u - 4)
            pe.wait_ge(ones_set, 1)
            pe.wait_ge(pchain, 2 + KD)
            pe.wait_ge(exp_done, NP * HEADS)
            for m in range(2):
                last = mm(sc[0][:, m, :], ones[:, :], ada_sum[:, m * TG:(m + 1) * TG], start=True, stop=True)
            last.then_inc(gate_ready, 1)


def merged(top, rest):
    out, done = [], 0
    for n, step in enumerate(top):
        out.append(step)
        until = len(rest) * (n + 1) // len(top)
        out += rest[done:until]
        done = until
    return out + rest[done:]


BRANCH_CHUNKS = ((0, 2), (2, 4), (4, 6), (6, 10))
YC = 10


def merge_and_output(nc, x, w_merge, w_out, gT, yT, post, out):
    with ExitStack() as ctx:
        def sb(name, shape, dt=F32):
            return ctx.enter_context(nc.sbuf_tensor("D_" + name, shape, dt))

        def sem(name):
            return ctx.enter_context(nc.semaphore("D_" + name))

        GB = 4
        wo_stage = sb("wo_stage", [P, D])
        wo_hi = sb("wo_hi", [P, KD, D], F32R)
        wo_lo = sb("wo_lo", [P, KD, D], F32R)
        wm_stage = [sb(f"wm_stage{j}", [P, YC, P]) for j in range(2)]
        wm_hi = [sb(f"wm_hi{j}", [P, YC, P], F32R) for j in range(2)]
        wm_lo = [sb(f"wm_lo{j}", [P, YC, P], F32R) for j in range(2)]
        y_stage = [sb(f"y_stage{j}", [P, TG]) for j in range(2)]
        y_hi = sb("y_hi", [P, YC, TG], F32R)
        y_lo = sb("y_lo", [P, YC, TG], F32R)
        m_hi = sb("m_hi", [P, KD, TG], F32R)
        m_lo = sb("m_lo", [P, KD, TG], F32R)
        gate = [sb(f"gate{j}", [P, 4, TG]) for j in range(GB)]
        x_in = sb("x_in", [P, D])
        o_buf = [sb(f"o_buf{j}", [P, D]) for j in range(2)]
        ss = sb("ss", [P, 1])
        rstd = sb("rstd", [P, 1])
        epsb = sb("epsb", [P, 1])
        mb = [ctx.enter_context(nc.psum_tensor(f"D_mb{b}", [P, TG], F32)) for b in range(4)]
        pb = [ctx.enter_context(nc.psum_tensor(f"D_pb{j}", [P, D], F32)) for j in range(2)]

        eps_set, wo_loaded, wo_hi_ready, wo_lo_ready = sem("eps_set"), sem("wo_loaded"), sem("wo_hi_ready"), sem("wo_lo_ready")
        wm_loaded, wm_hi_ready, wm_lo_ready = [sem(f"wm_loaded{j}") for j in range(2)], sem("wm_hi_ready"), sem("wm_lo_ready")
        y_loaded, y_hi_ready, y_lo_ready = [sem(f"y_loaded{j}") for j in range(2)], sem("y_hi_ready"), sem("y_lo_ready")
        g_loaded, g_ready, merged_done, mul_done = [sem(f"g_loaded{j}") for j in range(GB)], sem("g_ready"), sem("merged_done"), sem("mul_done")
        paired, added, m_hi_ready, m_lo_ready, p_done, squared, logged, rstd_ready, scaled, out_ready = (
            sem(n) for n in ("paired", "added", "m_hi_ready", "m_lo_ready", "p_done", "squared", "logged", "rstd_ready", "scaled", "out_ready"))
        x_loaded, out_stored = sem("x_loaded"), [sem(f"out_stored{j}") for j in range(2)]
        block = ctx.enter_context(nc.Block())
        wo_v = w_out.rearrange("a (k p) n -> p (a k) n", p=P)
        TB = TG // P

        def groups(eng, body):
            body(0, True, False)
            with eng.Fori(1, NG - 1) as g:
                body(g, False, False)
            body(NG - 1, False, True)

        @block.sync
        def _(sp):
            def fixed(value):
                return value if isinstance(value, int) else sp.snap(value)

            def load_wm(n, d):
                if not (isinstance(n, int) and n < 2):
                    sp.wait_ge(wm_hi_ready, n - 1)
                    sp.wait_ge(wm_lo_ready, n - 1)
                for w, (c0, c1) in zip(w_merge, BRANCH_CHUNKS):
                    sp.dma_start(wm_stage[d % 2][:, c0:c1, :], w[0, :, d * P:(d + 1) * P].rearrange("(k p) n -> p k n", p=P)).then_inc(wm_loaded[d % 2], 16)

            def load_gates(n, d, at):
                if not (isinstance(n, int) and n < GB):
                    sp.wait_ge(m_lo_ready, n - GB + 1)
                sp.dma_start(gate[d % GB][:, :, :], gT[d:d + 3 * KD + 1:KD, :, bass.ds(at, TG)].rearrange("n p t -> p n t")).then_inc(g_loaded[d % GB], 16)

            def load_y(g, k, at):
                if not (isinstance(g, int) and g == 0 and k < 2):
                    sp.wait_ge(y_hi_ready, YC * g + k - 1)
                    sp.wait_ge(y_lo_ready, YC * g + k - 1)
                sp.dma_start(y_stage[k % 2][:, :], yT[k, :, bass.ds(at, TG)]).then_inc(y_loaded[k % 2], 16)

            def load_wo(k):
                if k:
                    sp.wait_ge(wo_hi_ready, k)
                    sp.wait_ge(wo_lo_ready, k)
                sp.dma_start(wo_stage[:, :], wo_v[:, k, :]).then_inc(wo_loaded, 16)

            def store(n, b, row):
                sp.wait_ge(out_ready, n + 1)
                sp.dma_start(out[0, bass.ds(row, P), :], o_buf[b % 2][:, :]).then_inc(out_stored[b % 2], 16)

            def body(g, first, last):
                at = fixed(g * TG)
                at_next = fixed(g * TG + TG)
                rows = [fixed(g * TG + b * P) for b in range(TB)]
                row_before = None if first else fixed(g * TG - P)
                for d in range(KD):
                    n = KD * g + d
                    if not (last and d + 2 >= KD):
                        load_wm(n + 2, (d + 2) % KD)
                        load_gates(n + 2, (d + 2) % KD, at if d + 2 < KD else at_next)
                    if first:
                        load_wo(d)
                    if d == 1 and not first:
                        store(TB * g - 1, TB - 1, row_before)
                for b in range(TB):
                    sp.wait_ge(out_ready, TB * g + b)
                    sp.dma_start(x_in[:, :], x[0, bass.ds(rows[b], P), :]).then_inc(x_loaded, 16)
                    if b == 0 and not last:
                        for k in range(YC):
                            load_y(g + 1, k, at_next)
                    if b:
                        store(TB * g + b - 1, b - 1, rows[b - 1])

            load_wm(0, 0)
            for k in range(2):
                load_y(0, k, 0)
            load_gates(0, 0, 0)
            for k in range(2, YC):
                load_y(0, k, 0)
            load_wm(1, 1)
            load_gates(1, 1, 0)
            groups(sp, body)
            store(NT - 1, TB - 1, (NT - 1) * P)
            for j in range(2):
                sp.wait_ge(out_stored[j], 16 * NT // 2)

        @block.gpsimd
        def _(pool):
            tt = nc.gpsimd.tensor_tensor

            def body(g, first, last):
                for d in range(KD):
                    n = KD * g + d
                    if first:
                        pool.wait_ge(wo_hi_ready, d + 1)
                        tt(wo_lo[:, d, :], wo_stage[:, :], wo_hi[:, d, :].bitcast(F32), ALU.subtract).then_inc(wo_lo_ready, 1)
                    pool.wait_ge(mul_done, 4 * n + 4)
                    s = gate[d % GB]
                    tt(s[:, 0:2, :], s[:, 0:2, :], s[:, 2:4, :], ALU.add).then_inc(paired, 1)
                    pool.wait_ge(paired, n + 1)
                    tt(s[:, 0, :], s[:, 0, :], s[:, 1, :], ALU.add).then_inc(added, 1)
                for b in range(TB):
                    n = TB * g + b
                    pool.wait_ge(scaled, n + 1)
                    pool.wait_ge(x_loaded, 16 * (n + 1))
                    tt(o_buf[b % 2][:, :], o_buf[b % 2][:, :], x_in[:, :], ALU.add).then_inc(out_ready, 1)

            groups(pool, body)

        @block.vector
        def _(dve):
            tt, stt = nc.vector.tensor_tensor, nc.vector.scalar_tensor_tensor
            nc.vector.memset(epsb[:, :], EPS).then_inc(eps_set, 1)

            def split_wm(n, d):
                dve.wait_ge(wm_hi_ready, n + 1)
                tt(wm_lo[d % 2][:, :, :], wm_stage[d % 2][:, :, :], wm_hi[d % 2][:, :, :].bitcast(F32), ALU.subtract).then_inc(wm_lo_ready, 1)

            def split_y(g, k):
                dve.wait_ge(y_hi_ready, YC * g + k + 1)
                tt(y_lo[:, k, :], y_stage[k % 2][:, :], y_hi[:, k, :].bitcast(F32), ALU.subtract).then_inc(y_lo_ready, 1)

            def low(n, d):
                dve.wait_ge(m_hi_ready, n + 1)
                tt(m_lo[:, d, :], gate[d % GB][:, 0, :], m_hi[:, d, :].bitcast(F32), ALU.subtract).then_inc(m_lo_ready, 1)

            def body(g, first, last):
                for d in range(KD):
                    n = KD * g + d
                    if d + 1 < KD:
                        split_wm(n + 1, d + 1)
                    dve.wait_ge(g_ready, n + 1)
                    for b in range(4):
                        dve.wait_ge(merged_done, 4 * n + b + 1)
                        s = gate[d % GB]
                        tt(s[:, b, :], mb[b][:, :], s[:, b, :], ALU.mult).then_inc(mul_done, 1)
                        if b == 1 and d:
                            low(n - 1, d - 1)
                if not last:
                    for k in range(4):
                        split_y(g + 1, k)
                low(KD * g + KD - 1, KD - 1)
                if not last:
                    for k in range(4, YC):
                        split_y(g + 1, k)
                    split_wm(KD * g + KD, 0)
                for b in range(TB):
                    n = TB * g + b
                    dve.wait_ge(rstd_ready, n + 1)
                    dve.wait_ge(out_stored[b % 2], 16 * (TB // 2 * g + b // 2))
                    stt(o_buf[b % 2][:, :], pb[b % 2][:, :], rstd[:, :], post[:, :], ALU.mult, ALU.mult).then_inc(scaled, 1)

            for k in range(2):
                split_y(0, k)
            split_wm(0, 0)
            for k in range(2, YC):
                split_y(0, k)
            groups(dve, body)

        @block.scalar
        def _(act):
            a = nc.scalar.activation

            def split_wm(g, n, d):
                act.wait_ge(wm_loaded[d % 2], 64 * (KD // 2 * g + d // 2 + 1))
                if not (isinstance(n, int) and n < 2):
                    act.wait_ge(merged_done, 4 * (n - 1))
                a(wm_hi[d % 2][:, :, :], wm_stage[d % 2][:, :, :], ACT.Copy).then_inc(wm_hi_ready, 1)

            def split_y(g, k):
                act.wait_ge(y_loaded[k % 2], 16 * (YC // 2 * g + k // 2 + 1))
                if k == 0:
                    act.wait_ge(merged_done, 4 * KD * g)
                a(y_hi[:, k, :], y_stage[k % 2][:, :], ACT.Copy).then_inc(y_hi_ready, 1)

            def sigmoids(g, n, d):
                act.wait_ge(g_loaded[d % GB], 16 * (KD // GB * g + d // GB + 1))
                a(gate[d % GB][:, :, :], gate[d % GB][:, :, :], ACT.Sigmoid).then_inc(g_ready, 1)

            def high(g, d):
                act.wait_ge(added, KD * g + d + 1)
                if d == 0:
                    act.wait_ge(p_done, TB * g)
                a(m_hi[:, d, :], gate[d % GB][:, 0, :], ACT.Copy).then_inc(m_hi_ready, 1)

            def body(g, first, last):
                for d in range(KD):
                    n = KD * g + d
                    if d + 1 < KD:
                        split_wm(g, n + 1, d + 1)
                        sigmoids(g, n + 1, d + 1)
                    if first:
                        act.wait_ge(wo_loaded, 16 * (d + 1))
                        a(wo_hi[:, d, :], wo_stage[:, :], ACT.Copy).then_inc(wo_hi_ready, 1)
                    if d:
                        high(g, d - 1)
                if not last:
                    for k in range(4):
                        split_y(g + 1, k)
                high(g, KD - 1)
                if not last:
                    for k in range(4, YC):
                        split_y(g + 1, k)
                    split_wm(g + 1, KD * g + KD, 0)
                    sigmoids(g + 1, KD * g + KD, 0)
                act.preload_act_table_set("natural_log_exp_and_others")
                for b in range(TB):
                    n = TB * g + b
                    act.wait_ge(p_done, n + 1)
                    act.wait_ge(scaled, n)
                    if first:
                        act.wait_ge(wo_lo_ready, KD)
                    a(wo_stage[:, :], pb[b % 2][:, :], ACT.Square, accum_out=ss[:, :]).then_inc(squared, 1)
                    act.wait_ge(squared, n + 1)
                    a(ss[:, :], ss[:, :], ACT.Ln, bias=epsb[:, :], scale=1.0 / D).then_inc(logged, 1)
                    act.wait_ge(logged, n + 1)
                    a(rstd[:, :], ss[:, :], ACT.Exp, scale=-0.5).then_inc(rstd_ready, 1)

            act.wait_ge(eps_set, 1)
            for k in range(2):
                split_y(0, k)
            split_wm(0, 0, 0)
            for k in range(2, YC):
                split_y(0, k)
                if k == 3:
                    sigmoids(0, 0, 0)
            groups(act, body)

        @block.tensor
        def _(pe):
            mm = nc.tensor.matmul

            def output(g, b, half, k):
                tok = slice(b * P, (b + 1) * P)
                cols = slice(half * TG, (half + 1) * TG)
                mm(pb[b % 2][:, cols], m_hi[:, k, tok], wo_hi[:, k, cols], start=(k == 0), stop=False)
                mm(pb[b % 2][:, cols], m_hi[:, k, tok], wo_lo[:, k, cols], start=False, stop=False)
                return mm(pb[b % 2][:, cols], m_lo[:, k, tok], wo_hi[:, k, cols], start=False, stop=(k == KD - 1))

            def body(g, first, last):
                for d in range(KD):
                    n = KD * g + d
                    pe.wait_ge(wm_lo_ready, n + 1)
                    for b, (c0, c1) in enumerate(BRANCH_CHUNKS):
                        if not (first and d == 0):
                            pe.wait_ge(mul_done, 4 * n + b - 3)
                        if d == 0:
                            pe.wait_ge(y_lo_ready, YC * g + c1)
                        for k in range(c0, c1):
                            mm(mb[b][:, :], wm_hi[d % 2][:, k, :], y_hi[:, k, :], start=(k == c0), stop=False)
                            mm(mb[b][:, :], wm_hi[d % 2][:, k, :], y_lo[:, k, :], start=False, stop=False)
                            done = mm(mb[b][:, :], wm_lo[d % 2][:, k, :], y_hi[:, k, :], start=False, stop=(k == c1 - 1))
                        done.then_inc(merged_done, 1)
                if first:
                    pe.wait_ge(wo_lo_ready, KD)
                for b in range(TB):
                    n = TB * g + b
                    if not (first and b < 2):
                        pe.wait_ge(scaled, n - 1)
                    if b == 0:
                        pe.wait_ge(m_lo_ready, KD * g + KD - 1)
                        for half in range(2):
                            for k in range(KD - 1):
                                output(g, b, half, k)
                        pe.wait_ge(m_lo_ready, KD * g + KD)
                        for half in range(2):
                            done = output(g, b, half, KD - 1)
                    else:
                        for half in range(2):
                            for k in range(KD):
                                done = output(g, b, half, k)
                    done.then_inc(p_done, 1)

            groups(pe, body)


def constants():
    i = np.arange(P)
    same_head = (i[:, None] // 64 == i[None, :] // 64).astype(np.float32)
    masks = np.zeros((P, NL, P), np.float32)
    for n, m in enumerate(LEVELS):
        s, t = i[:, None], i[None, :]
        masks[:, n, :] = (s // (2 * m) == t // (2 * m)) & (s % (2 * m) < m) & (t % (2 * m) >= m)
    masks[:, NL - 1, :] = np.eye(P)
    scan = np.ones((P, 2, P), np.float32)
    scan[:, :, 0] = 0
    windows = np.array([[2, 8], [4, 16]])[i // 64]
    inv_first = 1.0 / np.minimum(i[None, None, :] + 1, windows[:, :, None])
    return {
        "causal": np.where(i[None, :] <= i[:, None], 0.0, NEG).astype(np.float32),
        "ident": np.eye(P, dtype=np.float32),
        "mean_w": same_head / 64,
        "head_m": same_head,
        "masks": masks,
        "scan_m": scan.reshape(P, 2 * P),
        "inv_first": inv_first.astype(np.float32),
        "inv_count": (1.0 / windows).astype(np.float32),
    }


def hybrid_trunk(nc, A, consts, out):
    pT = nc.dram_tensor("pT_scratch", [MIX_TILES, P, T], F32).ap()
    gT = nc.dram_tensor("gT_scratch", [GATE_TILES, P, T], F32).ap()
    yT = nc.dram_tensor("yT_scratch", [YC, P, T], F32).ap()
    with ExitStack() as ctx:
        h_hi = ctx.enter_context(nc.sbuf_tensor("h_hi", [P, KD, T], F32R))
        h_lo = ctx.enter_context(nc.sbuf_tensor("h_lo", [P, KD, T], F32R))
        project_mixer_inputs(nc, A["x"], A["c"], A["w_ada"], A["b_ada"], A["g_pre"], A["w_in"], consts["ident"], h_hi, h_lo, pT)
        gates_and_local_mixers(nc, A["w_in"], h_hi, h_lo, pT, gT, yT, consts, A["hgrn_lb"], A["hgrn_norm"], A["conv_w"],
                               A["pool_w"], A["pool_scale"])
    with ExitStack() as ctx:
        post = ctx.enter_context(nc.sbuf_tensor("post", [P, D], F32))
        differential_attention(nc, pT, yT, consts, A["diff_lam"], A["diff_norm"], A["c"], A["w_ada"], A["b_ada"], A["g_post"], post)
        merge_and_output(nc, A["x"], [A[f"w_merge_{b}"] for b in ("pool", "hgrn", "conv", "diff")], A["w_out"], gT, yT, post, out)


NAMES = ["x", "c", "w_ada", "b_ada", "g_pre", "g_post", "w_in", "pool_w", "pool_scale", "hgrn_lb", "hgrn_norm", "conv_w",
         "diff_lam", "diff_norm", "w_merge_pool", "w_merge_hgrn", "w_merge_conv", "w_merge_diff", "w_out"]


def kernel(**inputs):
    import concourse.bacc as bacc
    from concourse.bass_utils import run_bass_kernel_spmd

    nc = bacc.Bacc("TRN2", target_bir_lowering=False, num_devices=1, dynamic_dma_scratch_size=1024)
    arrays = {}

    def declare(name, array):
        array = np.ascontiguousarray(array)
        arrays[name + "_dram"] = array
        return nc.dram_tensor(name + "_dram", array.shape, mybir.dt.from_np(array.dtype), kind="ExternalInput").ap()

    inputs_ap = {n: declare("in_" + n, np.asarray(inputs[n])) for n in NAMES}
    consts_ap = {n: declare("const_" + n, a) for n, a in constants().items()}
    out = nc.dram_tensor("out_dram", (1, T, D), F32, kind="ExternalOutput").ap()
    hybrid_trunk(nc, inputs_ap, consts_ap, out)
    result = run_bass_kernel_spmd(nc, [arrays], core_ids=[0])
    return result.results[0]["out_dram"]
```

```python
import numpy as np
import concourse.bass as bass
from concourse import mybir
from contextlib import ExitStack

F32 = mybir.dt.float32
F32R = mybir.dt.float32r
ACT = mybir.ActivationFunctionType
ALU = mybir.AluOpType
AX = mybir.AxisListType

P = 128
D = 1024
T = 2048
KD = D // P
TG = 512
NG = T // TG
NT = T // P
D_IN = 8704
MIX_TILES = 36
GATE_TILES = D_IN // P - MIX_TILES
PAIRS = MIX_TILES // 2
EPS = 1e-6


def project_mixer_inputs(nc, x, c, w_ada, b_ada, g_pre, w_in, ident_d, h_hi, h_lo, pT):
    with ExitStack() as ctx:
        def sb(name, shape, dt=F32):
            return ctx.enter_context(nc.sbuf_tensor(name, shape, dt))

        def sem(name):
            return ctx.enter_context(nc.semaphore(name))

        w_stage = sb("w_stage", [P, KD, 2 * P])
        w_hi = [sb(f"w_hi{j}", [P, KD, P], F32R) for j in range(2)]
        w_lo = [sb(f"w_lo{j}", [P, KD, P], F32R) for j in range(2)]
        p_out = [sb(f"p_out{j}", [P, T]) for j in range(2)]
        x_tile = [sb(f"x_tile{j}", [P, D]) for j in range(2)]
        xn_all = sb("xn_all", [P, 8, D])
        xn = [xn_all[:, j, :] for j in range(8)]
        h_tmp = [sb(f"h_tmp{j}", [P, TG]) for j in range(4)]
        ada_acc = [xn_all[:, 4 + 2 * j:6 + 2 * j, :].rearrange("p a n -> p (a n)") for j in range(2)]
        square = sb("square", [P, D])
        ident = sb("ident", [P, P])
        ones = sb("ones", [P, 1])
        epsb = sb("epsb", [P, 1])
        c_col = sb("c_col", [P, KD])
        c_act = sb("c_act", [P, KD])
        c_sig = sb("c_sig", [P, KD])
        g_col = sb("g_col", [P, KD])
        b_col = sb("b_col", [P, 2 * KD])
        mod = sb("mod", [P, 2 * KD])
        sc1 = sb("sc1", [P, KD])
        gs = sb("gs", [P, KD])
        ss = sb("ss", [P, NT])
        rt = sb("rt", [P, NT])
        rstd = sb("rstd", [P, NT])
        bank = [ctx.enter_context(nc.psum_tensor(f"bankA{i}", [P, TG], F32)) for i in range(8)]

        consts_in = sem("A_consts_in")
        ones_set = sem("A_ones_set")
        ada_in = [sem(f"A_ada_in{j}") for j in range(2)]
        ada_used = sem("A_ada_used")
        c_ready = sem("A_c_ready")
        mod_summed = sem("A_mod_summed")
        mod_ready = sem("A_mod_ready")
        x_slot = [t % 2 if t < 4 else (t - 4) % 6 for t in range(NT)]
        x_at = x_tile + [p_out[j][:, half * D:(half + 1) * D] for j in range(2) for half in range(2)]
        x_before = [max([u for u in range(t) if x_slot[u] == x_slot[t]], default=None) for t in range(NT)]
        x_turn = [x_slot[:t + 1].count(x_slot[t]) for t in range(NT)]
        x_in = [sem(f"A_x_in{j}") for j in range(6)]
        squared = sem("A_squared")
        rooted = sem("A_rooted")
        inverted = sem("A_inverted")
        xn_ready = sem("A_xn_ready")
        turned = sem("A_turned")
        h_ready = sem("A_h_ready")
        hi_ready = sem("A_hi_ready")
        lo_ready = sem("A_lo_ready")
        dchain = sem("A_dchain")
        w_in_sem = sem("A_w_loaded")
        whi = sem("A_w_hi_ready")
        wlo = sem("A_w_lo_ready")
        ps_ready = sem("A_ps_ready")
        evac = sem("A_evacuated")
        stored = [sem(f"A_stored{j}") for j in range(2)]

        block = ctx.enter_context(nc.Block())
        NORM_AFTER = (1, 3, 5, 6)
        LAST = KD - 1
        w_v = w_in.rearrange("a (k p) n -> p (a k) n", p=P)
        ada_v = w_ada.rearrange("a (k p) n -> p (a k) n", p=P)

        @block.sync
        def _(sp):
            sp.dma_start(c_col[:, :], c.rearrange("a (k p) -> p (a k)", p=P), allow_slow_non_contiguous=True).then_inc(consts_in, 16)
            sp.dma_start(b_col[:, :], b_ada[:, 0:2 * D].rearrange("a (k p) -> p (a k)", p=P), allow_slow_non_contiguous=True).then_inc(consts_in, 16)
            sp.dma_start(g_col[:, :], g_pre.rearrange("a (k p) -> p (a k)", p=P), allow_slow_non_contiguous=True).then_inc(consts_in, 16)
            sp.dma_start(ident[:, :], ident_d).then_inc(consts_in, 16)
            def load_x(t):
                if x_before[t] is not None:
                    sp.wait_ge(xn_ready, x_before[t] + 1)
                elif t >= 4:
                    sp.wait_ge(ada_used, KD)
                sp.dma_start(x_at[x_slot[t]][:, :], x[0, t * P:(t + 1) * P, :]).then_inc(x_in[x_slot[t]], 16)

            for k in range(KD):
                if k >= 2:
                    sp.wait_ge(ada_used, k - 1)
                sp.dma_start(p_out[k % 2][:, :], ada_v[:, k, 0:2 * D]).then_inc(ada_in[k % 2], 16)
                if k in NORM_AFTER:
                    load_x(NORM_AFTER.index(k))
            for t in range(len(NORM_AFTER), NT):
                load_x(t)

            def load(q):
                sp.dma_start(w_stage[:, :, :], w_v[:, :, bass.ds(q * 2 * P, 2 * P)]).then_inc(w_in_sem, 16)

            def store(q, j):
                sp.wait_ge(evac, 8 * q + 4 * j + 4)
                sp.dma_start(pT[bass.ds(2 * q + j, 1), :, :].rearrange("a p t -> (a p) t"), p_out[j][:, :]).then_inc(stored[j], 16)

            load(0)
            with sp.Fori(1, PAIRS) as q:
                sp.wait_ge(whi, 2 * q)
                sp.wait_ge(wlo, 2 * q)
                load(q)
                store(q - 1, 0)
                store(q - 1, 1)
            store(PAIRS - 1, 0)
            store(PAIRS - 1, 1)
            for j in range(2):
                sp.wait_ge(stored[j], 16 * PAIRS)

        @block.gpsimd
        def _(pool):
            nc.gpsimd.memset(ones[:, :], 1.0).then_inc(ones_set, 1)
            nc.gpsimd.memset(epsb[:, :], EPS).then_inc(ones_set, 1)
            for n in range(NG * KD):
                g, k = divmod(n, KD)
                pool.wait_ge(hi_ready, n + 1)
                nc.gpsimd.tensor_tensor(h_lo[:, k, g * TG:(g + 1) * TG], h_tmp[n % 4][:, :],
                                        h_hi[:, k, g * TG:(g + 1) * TG].bitcast(F32), ALU.subtract).then_inc(lo_ready, 1)

        @block.vector
        def _(dve):
            chain = [0]

            def link(ins):
                chain[0] += 1
                ins.then_inc(dchain, 1)
                dve.wait_ge(dchain, chain[0])

            def norm(t):
                dve.wait_ge(rooted, t + 1)
                nc.vector.reciprocal(rstd[:, t:t + 1], rt[:, t:t + 1]).then_inc(inverted, 1)
                dve.wait_ge(inverted, t + 1)
                if t >= 8:
                    dve.wait_ge(turned, (t // 4 - 1) * KD)
                elif t >= 4:
                    dve.wait_ge(mod_ready, 1)
                nc.vector.tensor_scalar(xn[t % 8], x_at[x_slot[t]][:, :], rstd[:, t:t + 1], None,
                                        ALU.mult).then_inc(xn_ready, 1)

            dve.wait_ge(c_ready, 1)
            link(nc.vector.tensor_tensor(c_act[:, :], c_col[:, :], c_sig[:, :], ALU.mult))
            for k in range(KD):
                dve.wait_ge(ada_in[k % 2], 16 * (k // 2 + 1))
                if k == 0:
                    ins = nc.vector.tensor_scalar(ada_acc[0], p_out[0][:, :], c_act[:, 0:1], None, ALU.mult)
                else:
                    ins = nc.vector.scalar_tensor_tensor(ada_acc[k % 2], p_out[k % 2][:, :], c_act[:, k:k + 1],
                                                         ada_acc[(k - 1) % 2], ALU.mult, ALU.add)
                ins.then_inc(ada_used, 1)
                if k in NORM_AFTER:
                    norm(NORM_AFTER.index(k))
                dve.wait_ge(ada_used, k + 1)
            dve.wait_ge(mod_summed, 1)
            link(nc.vector.tensor_tensor(mod[:, :], bank[LAST][:, 0:2 * KD], b_col[:, :], ALU.add))
            link(nc.vector.tensor_scalar(sc1[:, :], mod[:, KD:2 * KD], 1.0, None, ALU.add))
            nc.vector.tensor_tensor(gs[:, :], sc1[:, :], g_col[:, :], ALU.mult).then_inc(mod_ready, 1)
            dve.wait_ge(mod_ready, 1)

            def split(q, j):
                dve.wait_ge(whi, 2 * q + j + 1)
                nc.vector.tensor_tensor(w_lo[j][:, :, :], w_stage[:, :, j * P:(j + 1) * P],
                                        w_hi[j][:, :, :].bitcast(F32), ALU.subtract).then_inc(wlo, 1)

            for g in range(NG):
                if g == NG - 1:
                    split(0, 0)
                    split(0, 1)
                for k in range(KD):
                    n = g * KD + k
                    dve.wait_ge(turned, n + 1)
                    if n >= 4:
                        dve.wait_ge(lo_ready, n - 3)
                    nc.vector.tensor_scalar(h_tmp[n % 4][:, :], bank[k][:, :], gs[:, k:k + 1], mod[:, k:k + 1],
                                            ALU.mult, ALU.add).then_inc(h_ready, 1)
                    if g + 1 < NG and k % 2:
                        norm(4 * (g + 1) + k // 2)

            with dve.Fori(1, PAIRS) as q:
                for j in range(2):
                    split(q, j)

        @block.scalar
        def _(act):
            act.wait_ge(consts_in, 64)
            nc.scalar.activation(c_sig[:, :], c_col[:, :], ACT.Sigmoid).then_inc(c_ready, 1)
            act.wait_ge(ones_set, 2)

            def root(t):
                act.wait_ge(x_in[x_slot[t]], 16 * x_turn[t])
                nc.scalar.activation(square[:, :], x_at[x_slot[t]][:, :], ACT.Square,
                                     accum_out=ss[:, t:t + 1]).then_inc(squared, 1)
                act.wait_ge(squared, t + 1)
                nc.scalar.activation(rt[:, t:t + 1], ss[:, t:t + 1], ACT.Sqrt, bias=epsb[:, :],
                                     scale=1.0 / D).then_inc(rooted, 1)

            def split(q, j, first):
                act.wait_ge(w_in_sem, 16 * (q + 1))
                if not first:
                    act.wait_ge(ps_ready, 4 * (2 * q + j - 1))
                nc.scalar.activation(w_hi[j][:, :, :], w_stage[:, :, j * P:(j + 1) * P], ACT.Copy).then_inc(whi, 1)

            ahead = 6
            for t in range(ahead):
                root(t)
            for g in range(NG):
                if g == NG - 1:
                    split(0, 0, True)
                    split(0, 1, True)
                for k in range(KD):
                    n = g * KD + k
                    act.wait_ge(h_ready, n + 1)
                    nc.scalar.activation(h_hi[:, k, g * TG:(g + 1) * TG], h_tmp[n % 4][:, :], ACT.Copy).then_inc(hi_ready, 1)
                    if k % 2 == 0 and 4 * g + ahead + k // 2 < NT:
                        root(4 * g + ahead + k // 2)

            def evacuate(q, j, first):
                for g in range(NG):
                    act.wait_ge(ps_ready, 8 * q + 4 * j + g + 1)
                    if not first and g == 0:
                        act.wait_ge(stored[j], 16 * q)
                    nc.scalar.activation(p_out[j][:, g * TG:(g + 1) * TG], bank[4 * j + g][:, :], ACT.Copy).then_inc(evac, 1)

            def body(q, first, last=False):
                evacuate(q, 0, first)
                if not last:
                    split(q + 1, 0, False)
                evacuate(q, 1, first)
                if not last:
                    split(q + 1, 1, False)

            body(0, True)
            with act.Fori(1, PAIRS - 1) as q:
                body(q, False)
            body(PAIRS - 1, False, last=True)

        @block.tensor
        def _(pe):
            pe.wait_ge(ones_set, 2)

            def turn(g, k):
                for i in range(4):
                    last = nc.tensor.transpose(bank[k][:, i * P:(i + 1) * P], xn[(4 * g + i) % 8][:, k * P:(k + 1) * P], ident[:, :])
                last.then_inc(turned, 1)

            pe.wait_ge(xn_ready, 4)
            for k in range(LAST):
                turn(0, k)
            pe.wait_ge(ada_used, KD)
            for j in range(2 * KD):
                last = nc.tensor.matmul(bank[LAST][:, j:j + 1], ada_acc[(KD - 1) % 2][:, j * P:(j + 1) * P], ones[:, :],
                                        start=True, stop=True)
            last.then_inc(mod_summed, 1)
            pe.wait_ge(mod_ready, 1)
            turn(0, LAST)
            for g in range(1, NG):
                pe.wait_ge(xn_ready, 4 * (g + 1))
                for k in range(KD):
                    pe.wait_ge(h_ready, (g - 1) * KD + k + 1)
                    turn(g, k)

            def tile(q, j, first):
                pe.wait_ge(wlo, 2 * q + j + 1)
                for g in range(NG):
                    if first:
                        pe.wait_ge(h_ready, (NG - 1) * KD + 4 * j + g + 1)
                        pe.wait_ge(hi_ready, (g + 1) * KD)
                        pe.wait_ge(lo_ready, (g + 1) * KD)
                    else:
                        pe.wait_ge(evac, 8 * (q - 1) + 4 * j + g + 1)
                    cols = slice(g * TG, (g + 1) * TG)
                    for k in range(KD):
                        nc.tensor.matmul(bank[4 * j + g][:, :], w_hi[j][:, k, :], h_hi[:, k, cols], start=(k == 0), stop=False)
                        nc.tensor.matmul(bank[4 * j + g][:, :], w_hi[j][:, k, :], h_lo[:, k, cols], start=False, stop=False)
                        last = nc.tensor.matmul(bank[4 * j + g][:, :], w_lo[j][:, k, :], h_hi[:, k, cols], start=False,
                                                stop=(k == KD - 1))
                    last.then_inc(ps_ready, 1)

            tile(0, 0, True)
            tile(0, 1, True)
            with pe.Fori(1, PAIRS) as q:
                for j in range(2):
                    tile(q, j, False)


LEVELS = (64, 32, 16, 8, 4, 2, 1)
NL = len(LEVELS) + 1
SPLIT = 2.0 ** -30
MIN_F = 1e-20
HALO_P, HALO_C = 16, 2


def gates_and_local_mixers(nc, w_in, h_hi, h_lo, pT, gT, yT, consts, hgrn_lb, hgrn_norm, conv_w, pool_w, pool_scale):
    with ExitStack() as ctx:
        def sb(name, shape, dt=F32):
            return ctx.enter_context(nc.sbuf_tensor("B_" + name, shape, dt))

        def sem(name):
            return ctx.enter_context(nc.semaphore("B_" + name))

        w_stage = sb("w_stage", [P, KD, P])
        w_hi = [sb(f"w_hi{j}", [P, KD, P], F32R) for j in range(2)]
        w_lo = [sb(f"w_lo{j}", [P, KD, P], F32R) for j in range(2)]
        g_out = [sb(f"g_out{j}", [P, TG]) for j in range(4)]
        ident = sb("ident", [P, P])
        mean_w = sb("mean_w", [P, P])
        head_m = sb("head_m", [P, P])
        masks = sb("masks", [P, NL, P], mybir.dt.uint8)
        scan_m = sb("scan_m", [P, 2 * P])
        inv_first = sb("inv_first", [P, 2, P])
        inv_count = sb("inv_count", [P, 2])
        pool_bd = sb("pool_bd", [P, 2, P])
        pool_sc = sb("pool_sc", [P, 2])
        conv_c = sb("conv_c", [P, 3, 2])
        lb_x = sb("lb_x", [P, 2])
        lb_e = sb("lb_e", [P, 2])
        lb = sb("lb", [P, 2])
        omlb = sb("omlb", [P, 2])
        norm_c = sb("norm_c", [P, 1])
        epsb = sb("epsb", [P, 1])
        in3 = sb("in3", [P, 6, P])
        g_in = sb("g_in", [P, 2, P])
        f_s = sb("f_s", [P, 2, P])
        k_s = sb("k_s", [P, 2, P])
        q_s = sb("q_s", [P, 2, P])
        f_ab = sb("f_ab", [P, 2, 2, P])
        b_s = sb("b_s", [P, 2, P])
        eb = sb("eb", [P, 2, P])
        qe = sb("qe", [P, 2, P])
        kt = sb("kt", [P, 2, P])
        X = sb("X", [P, NL, 2, P])
        QX = sb("QX", [P, NL, 2, P])
        tok = sb("tok", [P, 4, P])
        AT = sb("AT", [P, 2, 2, P])
        picks = sb("picks", [P, 2, 4, P])
        part = sb("part", [P, 2, P])
        S = sb("S", [P, 2, P])
        kvm = sb("kvm", [P, 2, P])
        osq = sb("osq", [P, 2, P])
        rs = sb("rs", [P, 2, P])
        sgate = sb("sgate", [P, 2, P])
        yh = sb("yh", [P, 2, P])
        a_in = sb("a_in", [P, 2, HALO_P + P])
        ag_in = sb("ag_in", [P, 2, P])
        s_ag = sb("s_ag", [P, 2, P])
        sum2 = sb("sum2", [P, 2, HALO_P + P])
        sum4 = sb("sum4", [P, 2, HALO_P + P])
        sum8 = sb("sum8", [P, HALO_P + P])
        win = sb("win", [P, 2, P])
        yp = sb("yp", [P, 2, P])
        c_in = sb("c_in", [P, 8, HALO_C + P])
        s_cg = sb("s_cg", [P, 2, P])
        z_s = sb("z_s", [P, 2, HALO_C + P])
        tap = sb("tap", [P, 2, P])
        acc = sb("acc", [P, 2, P])
        yc = sb("yc", [P, 2, P])
        bank = [ctx.enter_context(nc.psum_tensor(f"bankB{i}", [P, TG], F32)) for i in range(4)]
        score = ctx.enter_context(nc.psum_tensor("B_score", [P, 2, 4, P], F32))
        b6 = ctx.enter_context(nc.psum_tensor("B_b6", [P, 4, P], F32))
        b7 = ctx.enter_context(nc.psum_tensor("B_b7", [P, 4, P], F32))

        consts_in = sem("consts_in")
        zeroed = sem("zeroed")
        zeroed_v = sem("zeroed_v")
        lb_exp = sem("lb_exp")
        w_loaded = sem("w_loaded")
        whi, wlo = sem("w_hi_ready"), sem("w_lo_ready")
        ps_ready, evac = sem("ps_ready"), sem("evacuated")
        stored = [sem(f"stored{j}") for j in range(4)]
        in3_loaded, g_loaded, a_loaded, c_loaded = sem("in3_loaded"), sem("g_loaded"), sem("a_loaded"), sem("c_loaded")
        sig_ready, sigg_ready, sigac_ready = sem("sig_ready"), sem("sigg_ready"), sem("sigac_ready")
        clipped, logged, scanned, decayed, spread, xready = (sem(n) for n in ("clipped", "logged", "scanned", "decayed", "spread", "x_ready"))
        kt_ready, prep_ready = sem("kt_ready"), sem("prep_ready")
        t_done, r_done, o_done, n_done = sem("t_done"), sem("r_done"), sem("o_done"), sem("n_done")
        tok_ready, picked = sem("tok_ready"), sem("picked")
        attn_ready = sem("attn_ready")
        state_done, osq_ready, rstd_ready, fin_done = sem("state_done"), sem("osq_ready"), sem("rstd_ready"), sem("fin_done")
        pooled, sag_ready, yp_ready, yc_ready = sem("pooled"), sem("sag_ready"), sem("yp_ready"), sem("yc_ready")
        yh_stored, yp_stored, yc_stored = sem("yh_stored"), sem("yp_stored"), sem("yc_stored")
        dchain, pchain, achain = sem("dchain"), sem("pchain"), sem("achain")

        block = ctx.enter_context(nc.Block())
        w_v = w_in.rearrange("a (k p) n -> p (a k) n", p=P)
        STEPS = NT
        assert GATE_TILES == 2 * STEPS

        def loop(eng, body):
            body(0, True, False)
            with eng.Fori(1, STEPS - 1) as i:
                body(i, False, False)
            body(STEPS - 1, False, True)

        @block.sync
        def _(sp):
            sp.dma_start(w_stage[:, :, :], w_v[:, :, MIX_TILES * P:(MIX_TILES + 1) * P]).then_inc(w_loaded, 16)
            for dst, src in ((ident, consts["ident"]), (mean_w, consts["mean_w"]), (head_m, consts["head_m"]),
                             (scan_m, consts["scan_m"])):
                sp.dma_start(dst[:, :], src).then_inc(consts_in, 16)
            sp.dma_start(QX[:, :, 0, :], consts["masks"]).then_inc(consts_in, 16)
            sp.dma_start(inv_first[:, :, :], consts["inv_first"]).then_inc(consts_in, 16)
            sp.dma_start(inv_count[:, :], consts["inv_count"]).then_inc(consts_in, 16)
            sp.dma_start(pool_sc[:, :], pool_scale.rearrange("a (n p) -> p (a n)", p=P), allow_slow_non_contiguous=True).then_inc(consts_in, 16)
            for k in range(3):
                sp.dma_start(conv_c[:, k, :], conv_w[0, k:k + 1, :].rearrange("a (n p) -> p (a n)", p=P),
                             allow_slow_non_contiguous=True).then_inc(consts_in, 16)
            sp.dma_start(lb_x[:, :], hgrn_lb.rearrange("a (n p) -> p (a n)", p=P), allow_slow_non_contiguous=True).then_inc(consts_in, 16)
            for h in range(2):
                sp.dma_start(norm_c[64 * h:64 * h + 64, :], hgrn_norm.rearrange("a p -> p a"), allow_slow_non_contiguous=True).then_inc(consts_in, 16)
            sp.wait_ge(zeroed, 1)
            for g in range(4):
                sp.dma_start(pool_bd[64 * (g % 2):64 * (g % 2) + 64, g // 2, 64 * (g % 2):64 * (g % 2) + 64],
                             pool_w[0, g, :, :]).then_inc(consts_in, 16)

            def fixed(value):
                return value if isinstance(value, int) else sp.snap(value)

            def load_w(col):
                sp.dma_start(w_stage[:, :, :], w_v[:, :, bass.ds(col, P)]).then_inc(w_loaded, 16)

            def load_hgrn(at):
                sp.dma_start(in3[:, :, :], pT[4:10, :, bass.ds(at, P)].rearrange("n p t -> p n t")).then_inc(in3_loaded, 16)

            def load_gate(at):
                sp.dma_start(g_in[:, :, :], pT[10:12, :, bass.ds(at, P)].rearrange("n p t -> p n t")).then_inc(g_loaded, 16)

            def load_pool_conv(at, at_p, at_c):
                if at_p is None:
                    sp.wait_ge(zeroed, 3)
                    sp.dma_start(a_in[:, :, HALO_P:], pT[0:2, :, 0:P].rearrange("n p t -> p n t")).then_inc(a_loaded, 16)
                    sp.dma_start(c_in[:, :, HALO_C:], pT[12:20, :, 0:P].rearrange("n p t -> p n t")).then_inc(c_loaded, 16)
                else:
                    sp.dma_start(a_in[:, :, :], pT[0:2, :, bass.ds(at_p, HALO_P + P)].rearrange("n p t -> p n t")).then_inc(a_loaded, 16)
                    sp.dma_start(c_in[:, :, :], pT[12:20, :, bass.ds(at_c, HALO_C + P)].rearrange("n p t -> p n t")).then_inc(c_loaded, 16)
                sp.dma_start(ag_in[:, :, :], pT[2:4, :, bass.ds(at, P)].rearrange("n p t -> p n t")).then_inc(a_loaded, 16)

            def store_gate(i, s, tile):
                sp.wait_ge(evac, 8 * i + s + 1)
                sp.dma_start(gT[bass.ds(tile, 1), :, (s % 4) * TG:(s % 4 + 1) * TG].rearrange("a p t -> (a p) t"),
                             g_out[s % 4][:, :]).then_inc(stored[s % 4], 16)

            def store_y(at, first_chunk, src, done):
                sp.dma_start(yT[first_chunk:first_chunk + 2, :, bass.ds(at, P)].rearrange("n p t -> p n t"),
                             src[:, :, :]).then_inc(done, 16)

            load_hgrn(0)
            load_pool_conv(0, None, None)
            sp.wait_ge(whi, 1)
            sp.wait_ge(wlo, 1)
            load_w((MIX_TILES + 1) * P)

            def finish_last(i, at):
                sp.wait_ge(fin_done, i)
                store_y(at, 2, yh, yh_stored)
                sp.wait_ge(yp_ready, i)
                store_y(at, 0, yp, yp_stored)

            def body(i, first, last):
                here = fixed(i * P)
                before = None if first else fixed(i * P - P)
                tiles = [fixed(2 * i), fixed(2 * i + 1)]
                if not last:
                    cols = [fixed(i * (2 * P) + (MIX_TILES + 2 + j) * P) for j in range(2)]
                    after, after_p, after_c = (fixed(i * P + (P - halo)) for halo in (0, HALO_P, HALO_C))
                    sp.wait_ge(whi, 2 * i + 2)
                    sp.wait_ge(wlo, 2 * i + 2)
                    load_w(cols[0])
                store_gate(i, 0, tiles[0])
                store_gate(i, 1, tiles[0])
                if not first:
                    finish_last(i, before)
                load_gate(here)
                store_gate(i, 2, tiles[0])
                store_gate(i, 3, tiles[0])
                if not last:
                    sp.wait_ge(whi, 2 * i + 3)
                    sp.wait_ge(wlo, 2 * i + 3)
                    load_w(cols[1])
                    sp.wait_ge(prep_ready, i + 1)
                    sp.wait_ge(t_done, i + 1)
                    load_hgrn(after)
                store_gate(i, 4, tiles[1])
                store_gate(i, 5, tiles[1])
                store_gate(i, 6, tiles[1])
                sp.wait_ge(yc_ready, i + 1)
                store_y(here, 4, yc, yc_stored)
                if not last:
                    load_pool_conv(after, after_p, after_c)
                store_gate(i, 7, tiles[1])

            loop(sp, body)
            finish_last(STEPS, (STEPS - 1) * P)
            for j in range(4):
                sp.wait_ge(stored[j], 16 * 2 * STEPS)
            sp.wait_ge(yh_stored, 16 * STEPS)
            sp.wait_ge(yp_stored, 16 * STEPS)
            sp.wait_ge(yc_stored, 16 * STEPS)

        @block.gpsimd
        def _(pool):
            chain = [0]
            base = [0]
            PER = 13

            def link(ins):
                chain[0] += 1
                ins.then_inc(pchain, 1)
                pool.wait_ge(pchain, base[0] + chain[0])

            tt = nc.gpsimd.tensor_tensor
            nc.gpsimd.memset(pool_bd[:, :, :], 0.0).then_inc(zeroed, 1)
            nc.gpsimd.memset(a_in[:, :, 0:HALO_P], 0.0).then_inc(zeroed, 1)
            nc.gpsimd.memset(c_in[:, :, 0:HALO_C], 0.0).then_inc(zeroed, 1)
            pool.wait_ge(consts_in, 16 * 18)

            def body(i, first, last):
                base[0] = PER * i
                chain[0] = 0
                pool.wait_ge(a_loaded, 32 * (i + 1))
                link(tt(sum2[:, :, 1:], a_in[:, :, 1:], a_in[:, :, :-1], ALU.add))
                link(tt(sum4[:, :, 3:], sum2[:, :, 3:], sum2[:, :, 1:-2], ALU.add))
                link(tt(sum8[:, 7:], sum4[:, 1, 7:], sum4[:, 1, 3:-4], ALU.add))
                if not first:
                    pool.wait_ge(o_done, i)
                tt(win[64:128, 1, :], sum8[64:128, HALO_P:], sum8[64:128, 8:-8], ALU.add)
                nc.gpsimd.tensor_copy(win[0:64, 0, :], sum2[0:64, 0, HALO_P:])
                nc.gpsimd.tensor_copy(win[64:128, 0, :], sum4[64:128, 0, HALO_P:])
                link(nc.gpsimd.tensor_copy(win[0:64, 1, :], sum8[0:64, HALO_P:]))
                inv = inv_first[:, :, :] if first else inv_count[:, :].unsqueeze(2).to_broadcast([P, 2, P])
                link(tt(win[:, :, :], win[:, :, :], inv, ALU.mult))
                tt(win[:, :, :], win[:, :, :], a_in[:, :, HALO_P:], ALU.subtract).then_inc(pooled, 1)
                pool.wait_ge(sigac_ready, i + 1)
                tt(s_ag[:, :, :], s_ag[:, :, :], ag_in[:, :, :], ALU.mult).then_inc(sag_ready, 1)
                pool.wait_ge(c_loaded, 16 * (i + 1))
                link(tt(z_s[:, :, :], c_in[:, 0:2, :], c_in[:, 4:6, :], ALU.mult))
                w = [conv_c[:, k, :].unsqueeze(2).to_broadcast([P, 2, P]) for k in range(3)]
                link(tt(acc[:, :, :], z_s[:, :, 2:], w[2], ALU.mult))
                link(tt(tap[:, :, :], z_s[:, :, 1:-1], w[1], ALU.mult))
                link(tt(acc[:, :, :], acc[:, :, :], tap[:, :, :], ALU.add))
                link(tt(tap[:, :, :], z_s[:, :, :-2], w[0], ALU.mult))
                link(tt(acc[:, :, :], acc[:, :, :], tap[:, :, :], ALU.add))
                link(tt(acc[:, :, :], acc[:, :, :], c_in[:, 2:4, HALO_C:], ALU.mult))
                link(tt(s_cg[:, :, :], s_cg[:, :, :], c_in[:, 6:8, HALO_C:], ALU.mult))
                if not first:
                    pool.wait_ge(yc_stored, 16 * i)
                tt(yc[:, :, :], acc[:, :, :], s_cg[:, :, :], ALU.mult).then_inc(yc_ready, 1)
                assert chain[0] == PER, chain[0]

            loop(pool, body)

        @block.vector
        def _(dve):
            chain = [0]
            base = [0]
            START, PER = 5, 13

            def link(ins):
                chain[0] += 1
                ins.then_inc(dchain, 1)
                dve.wait_ge(dchain, base[0] + chain[0])

            tt, ts, stt = nc.vector.tensor_tensor, nc.vector.tensor_scalar, nc.vector.scalar_tensor_tensor
            def lo(tile, j):
                dve.wait_ge(whi, tile + 1)
                tt(w_lo[j][:, :, :], w_stage[:, :, :], w_hi[j][:, :, :].bitcast(F32), ALU.subtract).then_inc(wlo, 1)

            nc.vector.memset(S[:, :, :], 0.0).then_inc(zeroed_v, 1)
            nc.vector.memset(epsb[:, :], EPS).then_inc(zeroed_v, 1)
            nc.vector.memset(AT[:, :, :, :], 0.0).then_inc(zeroed_v, 1)
            lo(0, 0)
            dve.wait_ge(zeroed_v, 3)
            dve.wait_ge(consts_in, 16 * 18)
            nc.vector.tensor_copy(masks[:, :, :], QX[:, :, 0, :])
            link(tt(lb_x[:, :], lb_x[:, :], lb_x[:, :], ALU.subtract))
            dve.wait_ge(lb_exp, 1)
            link(nc.vector.reciprocal(lb[:, :], lb_e[:, :]))
            link(tt(lb[:, :], lb[:, :], lb_e[:, :], ALU.mult))
            link(tt(lb[:, :], lb[:, :], lb[:, :], ALU.subtract))
            link(ts(omlb[:, :], lb[:, :], -1.0, 1.0, ALU.mult, ALU.add))
            assert chain[0] == START

            lo(1, 1)

            def advance_state(i):
                dve.wait_ge(o_done, i)
                tt(kvm[:, :, :], b7[:, 0:2, :], head_m[:, :].unsqueeze(1).to_broadcast([P, 2, P]), ALU.mult).then_inc(dchain, 1)
                chain[0] += 1
                dve.wait_ge(dchain, base[0] + chain[0])
                for t in range(2):
                    last = stt(S[:, t, :], S[:, t, :], eb[:, t, P - 1:P], kvm[:, t, :], ALU.mult, ALU.add)
                last.then_inc(state_done, 1)
                dve.wait_ge(sag_ready, i)

            def pool_out(i, second):
                dve.wait_ge(osq_ready, i)
                if not second:
                    dve.wait_ge(yp_stored, 16 * (i - 1))
                for t in range(2):
                    last = stt(yp[:, t, :], b6[:, 2 + t, :], pool_sc[:, t:t + 1], s_ag[:, t, :], ALU.mult, ALU.mult)
                last.then_inc(yp_ready, 1)

            def finish(i, second):
                dve.wait_ge(sigg_ready, i)
                link(tt(sgate[:, :, :], sgate[:, :, :], g_in[:, :, :], ALU.mult))
                dve.wait_ge(rstd_ready, i)
                link(tt(rs[:, :, :], b6[:, 0:2, :], rs[:, :, :], ALU.mult))
                if not second:
                    dve.wait_ge(yh_stored, 16 * (i - 1))
                stt(yh[:, :, :], rs[:, :, :], norm_c[:, :], sgate[:, :, :], ALU.mult, ALU.mult).then_inc(fin_done, 1)

            def body(i, first, last, second=False):
                base[0] = START + PER * i
                chain[0] = 0
                if first:
                    for _ in range(3):
                        link(nc.vector.memset(kvm[:, 0, 0:1], 0.0))
                else:
                    advance_state(i)
                    pool_out(i, second)
                dve.wait_ge(sig_ready, i + 1)
                for t in range(2):
                    ts(k_s[:, t, :], k_s[:, t, :], omlb[:, t:t + 1], None, ALU.mult)
                for t in range(2):
                    ins = ts(f_s[:, t, :], f_s[:, t, :], omlb[:, t:t + 1], lb[:, t:t + 1], ALU.mult, ALU.add)
                link(ins)
                ts(f_ab[:, 0, :, :], f_s[:, :, :], SPLIT, None, ALU.max)
                ts(f_ab[:, 1, :, :], f_s[:, :, :], MIN_F, SPLIT, ALU.max, ALU.min).then_inc(clipped, 1)
                link(tt(q_s[:, :, :], q_s[:, :, :], in3[:, 0:2, :], ALU.mult))
                dve.wait_ge(logged, i + 1)
                link(tt(f_s[:, :, :], f_ab[:, 0, :, :], f_ab[:, 1, :, :], ALU.add))
                link(nc.vector.tensor_tensor_scan(b_s[:, :, :].rearrange("p n t -> p (n t)"), scan_m[:, :],
                                                  f_s[:, :, :].rearrange("p n t -> p (n t)"), 0.0, ALU.mult, ALU.add))
                nc.vector.tensor_copy(f_s[:, 0, 0:1], b_s[:, 0, 0:1]).then_inc(scanned, 1)
                if not first:
                    dve.wait_ge(r_done, 4 * i)
                for n, m in enumerate(LEVELS):
                    v = b_s[:, :, :].rearrange("p n t -> p (n t)").rearrange("p (n u) -> p n u", u=2 * m)
                    o = X[:, n, :, :].rearrange("p n t -> p (n t)").rearrange("p (n u) -> p n u", u=2 * m)
                    ref = v[:, :, m - 1:m].to_broadcast([P, P // m, 2 * m])
                    ins = tt(o, v, ref, ALU.subtract)
                link(ins)
                flat = X[:, 0:NL - 1, :, :].rearrange("p l n t -> p (l n t)")
                stt(flat, flat, -1.0, flat, ALU.mult, ALU.min).then_inc(spread, 1)
                dve.wait_ge(decayed, i + 1)
                tt(kt[:, :, :], kt[:, :, :], k_s[:, :, :], ALU.mult).then_inc(kt_ready, 1)
                tt(qe[:, :, :], q_s[:, :, :], eb[:, :, :], ALU.mult)
                nc.vector.tensor_copy(QX[:, NL - 1, :, :], q_s[:, :, :])
                nc.vector.tensor_copy(X[:, NL - 1, :, :], k_s[:, :, :])
                dve.wait_ge(xready, i + 1)
                link(tt(QX[:, 0:NL - 1, :, :], X[:, 0:NL - 1, :, :],
                        q_s[:, :, :].unsqueeze(1).to_broadcast([P, NL - 1, 2, P]), ALU.mult))
                tt(X[:, 0:NL - 1, :, :], X[:, 0:NL - 1, :, :],
                   k_s[:, :, :].unsqueeze(1).to_broadcast([P, NL - 1, 2, P]), ALU.mult).then_inc(prep_ready, 1)
                if not first:
                    finish(i, second)
                for r in range(4):
                    dve.wait_ge(r_done, 4 * i + r + 1)
                    m = masks[:, 4 * (r % 2):4 * (r % 2) + 4, :]
                    for h in range(2):
                        ins = tt(picks[:, h, :, :], score[:, h, :, :], m, ALU.mult)
                    ins.then_inc(picked, 1)
                    dve.wait_ge(picked, 4 * i + r + 1)
                    out = AT if r % 2 == 0 else part
                    link(nc.vector.tensor_reduce(out[:, r // 2, :, :].rearrange("p h t -> p (h t)") if r % 2 == 0 else out[:, :, :].rearrange("p h t -> p (h t)"),
                                                 picks[:, :, :, :].rearrange("p h n t -> p h t n"), AX.X, ALU.add))
                    if r % 2:
                        tt(AT[:, r // 2, :, :], AT[:, r // 2, :, :], part[:, :, :], ALU.add).then_inc(attn_ready, 1)
                    if r == 0 and not last:
                        lo(2 * i + 2, 0)
                if not last:
                    lo(2 * i + 3, 1)

            body(0, True, False)
            assert chain[0] == PER
            body(1, False, False, second=True)
            assert chain[0] == PER
            with dve.Fori(2, STEPS - 1) as i:
                body(i, False, False)
            body(STEPS - 1, False, True)
            base[0] = START + PER * STEPS
            chain[0] = 0
            advance_state(STEPS)
            pool_out(STEPS, False)
            finish(STEPS, False)

        @block.scalar
        def _(act):
            chain = [0]
            base = [0]

            def link(ins):
                chain[0] += 1
                ins.then_inc(achain, 1)
                act.wait_ge(achain, base[0] + chain[0])

            a = nc.scalar.activation

            def hi(tile, j, fresh):
                act.wait_ge(w_loaded, 16 * (tile + 1))
                if not fresh:
                    act.wait_ge(ps_ready, 4 * (tile - 1))
                a(w_hi[j][:, :, :], w_stage[:, :, :], ACT.Copy).then_inc(whi, 1)

            hi(0, 0, True)
            act.wait_ge(dchain, 1)
            a(lb_e[:, :], lb_x[:, :], ACT.Exp).then_inc(lb_exp, 1)
            hi(1, 1, True)

            def evacuate(i, s, first):
                act.wait_ge(ps_ready, 8 * i + s + 1)
                if not (first and s < 4):
                    act.wait_ge(stored[s % 4], 16 * (2 * i + s // 4))
                a(g_out[s % 4][:, :], bank[s % 4][:, :], ACT.Copy).then_inc(evac, 1)

            def squares(i):
                act.wait_ge(o_done, i)
                a(osq[:, :, :], b6[:, 0:2, :], ACT.Square).then_inc(osq_ready, 1)

            def gate_sigmoid(i):
                act.wait_ge(g_loaded, 16 * i)
                a(sgate[:, :, :], g_in[:, :, :], ACT.Sigmoid).then_inc(sigg_ready, 1)

            def root(i):
                act.wait_ge(n_done, i)
                link(a(rs[:, :, :], b7[:, 2:4, :], ACT.Ln, bias=epsb[:, :]))
                a(rs[:, :, :], rs[:, :, :], ACT.Exp, scale=-0.5).then_inc(rstd_ready, 1)

            def body(i, first, last):
                base[0] = i - 1 if not first else 0
                chain[0] = 0
                if not first:
                    squares(i)
                act.wait_ge(in3_loaded, 16 * (i + 1))
                if not first:
                    act.wait_ge(prep_ready, i)
                a(f_s[:, :, :], in3[:, 2:4, :], ACT.Sigmoid)
                a(k_s[:, :, :], in3[:, 2:4, :], ACT.Sigmoid, scale=-1.0)
                a(q_s[:, :, :], in3[:, 0:2, :], ACT.Sigmoid).then_inc(sig_ready, 1)
                if not first:
                    act.wait_ge(yp_ready, i)
                    gate_sigmoid(i)
                act.wait_ge(a_loaded, 32 * (i + 1))
                a(s_ag[:, :, :], ag_in[:, :, :], ACT.Sigmoid)
                act.wait_ge(c_loaded, 16 * (i + 1))
                a(s_cg[:, :, :], c_in[:, 6:8, HALO_C:], ACT.Sigmoid).then_inc(sigac_ready, 1)
                act.preload_act_table_set("natural_log_exp_and_others")
                act.wait_ge(clipped, i + 1)
                a(f_ab[:, 0, :, :], f_ab[:, 0, :, :], ACT.Ln)
                a(f_ab[:, 1, :, :], f_ab[:, 1, :, :], ACT.Ln, scale=1.0 / SPLIT).then_inc(logged, 1)
                evacuate(i, 0, first)
                if not first:
                    root(i)
                act.wait_ge(scanned, i + 1)
                if not first:
                    act.wait_ge(state_done, i)
                a(eb[:, :, :], b_s[:, :, :], ACT.Exp)
                if not first:
                    act.wait_ge(t_done, i)
                for t in range(2):
                    ins = a(kt[:, t, :], b_s[:, t, :], ACT.Exp, bias=b_s[:, t, P - 1:P], scale=-1.0)
                ins.then_inc(decayed, 1)
                evacuate(i, 1, first)
                act.wait_ge(spread, i + 1)
                a(X[:, 0:NL - 1, :, :], X[:, 0:NL - 1, :, :], ACT.Exp).then_inc(xready, 1)
                evacuate(i, 2, first)
                evacuate(i, 3, first)
                if not last:
                    hi(2 * i + 2, 0, False)
                act.wait_ge(t_done, i + 1)
                if not first:
                    act.wait_ge(o_done, i)
                a(tok[:, :, :], b6[:, :, :], ACT.Copy).then_inc(tok_ready, 1)
                for s in range(4, 8):
                    evacuate(i, s, first)
                if not last:
                    hi(2 * i + 3, 1, False)

            loop(act, body)
            base[0] = STEPS - 1
            chain[0] = 0
            squares(STEPS)
            gate_sigmoid(STEPS)
            root(STEPS)

        @block.tensor
        def _(pe):
            mm = nc.tensor.matmul

            def segment(i, s, first):
                j, g = divmod(s, 4)
                if g == 0:
                    pe.wait_ge(wlo, 2 * i + j + 1)
                if not (first and j == 0):
                    pe.wait_ge(evac, 8 * i + s - 3)
                cols = slice(g * TG, (g + 1) * TG)
                for k in range(KD):
                    mm(bank[g][:, :], w_hi[j][:, k, :], h_hi[:, k, cols], start=(k == 0), stop=False)
                    mm(bank[g][:, :], w_hi[j][:, k, :], h_lo[:, k, cols], start=False, stop=False)
                    last = mm(bank[g][:, :], w_lo[j][:, k, :], h_hi[:, k, cols], start=False, stop=(k == KD - 1))
                last.then_inc(ps_ready, 1)

            def norms(i):
                pe.wait_ge(osq_ready, i)
                pe.wait_ge(state_done, i)
                mm(b7[:, 2:4, :], mean_w[:, :], osq[:, :, :], start=True, stop=True).then_inc(n_done, 1)

            def transposes(i, first):
                pe.wait_ge(kt_ready, i + 1)
                if not first:
                    pe.wait_ge(fin_done, i)
                    pe.wait_ge(yp_ready, i)
                for t in range(2):
                    nc.tensor.transpose(b6[:, t, :], in3[:, 4 + t, :], ident[:, :])
                    last = nc.tensor.transpose(b6[:, 2 + t, :], kt[:, t, :], ident[:, :])
                last.then_inc(t_done, 1)

            def scores(i, r, first):
                if r == 0:
                    pe.wait_ge(prep_ready, i + 1)
                if not (first and r == 0):
                    pe.wait_ge(picked, 4 * i + r)
                t = r // 2
                for n in range(4):
                    for h in range(2):
                        rows = slice(64 * h, 64 * h + 64)
                        last = mm(score[:, h, n, :], X[rows, 4 * (r % 2) + n, t, :], QX[rows, 4 * (r % 2) + n, t, :],
                                  start=True, stop=True)
                last.then_inc(r_done, 1)

            def outputs(i, first):
                pe.wait_ge(attn_ready, 2 * i + 2)
                pe.wait_ge(tok_ready, i + 1)
                pe.wait_ge(pooled, i + 1)
                if not first:
                    pe.wait_ge(state_done, i)
                for t in range(2):
                    mm(b6[:, t, :], S[:, t, :], qe[:, t, :], start=True, stop=False, skip_group_check=True)
                    for h in range(2):
                        mm(b6[64 * h:64 * h + 64, t, :], tok[:, t, 64 * h:64 * h + 64], AT[:, t, h, :], start=False, stop=True,
                           skip_group_check=True)
                for t in range(2):
                    mm(b6[:, 2 + t, :], pool_bd[:, t, :], win[:, t, :], start=True, stop=True, skip_group_check=True)
                for t in range(2):
                    last = mm(b7[:, t, :], tok[:, 2 + t, :], tok[:, t, :], start=True, stop=True)
                last.then_inc(o_done, 1)

            def body(i, first, last):
                segment(i, 0, first)
                if not first:
                    norms(i)
                segment(i, 1, first)
                segment(i, 2, first)
                segment(i, 3, first)
                if first:
                    pe.wait_ge(zeroed_v, 3)
                    pe.wait_ge(consts_in, 16 * 18)
                transposes(i, first)
                scores(i, 0, first)
                segment(i, 4, first)
                scores(i, 1, first)
                segment(i, 5, first)
                scores(i, 2, first)
                segment(i, 6, first)
                scores(i, 3, first)
                segment(i, 7, first)
                outputs(i, first)

            loop(pe, body)
            norms(STEPS)


HEADS = 4
DH = 64
LAM_INIT = 0.8 - 0.6 * float(np.exp(-0.3 * 0))
NEG = -1e30


def differential_attention(nc, pT, yT, consts, diff_lam, diff_norm, c, w_ada, b_ada, g_post, post):
    with ExitStack() as ctx:
        def sb(name, shape, dt=F32):
            return ctx.enter_context(nc.sbuf_tensor("C_" + name, shape, dt))

        def sem(name):
            return ctx.enter_context(nc.semaphore("C_" + name))

        U = NT
        NQ = T // TG
        pieces = [(u + 4) // 4 for u in range(U)]
        before = [sum(pieces[:u]) for u in range(U + 1)]
        NP = before[U]
        multi_before = [sum(p > 1 for p in pieces[:u]) for u in range(U + 1)]
        multi = multi_before[U]
        LAGS = 6
        SPLIT_STEP = (0, 3, 7, 11)
        V_STEP = 3
        G_STEP = 2
        QB = 4

        q_in = sb("q_in", [P, 2, T])
        k_in = sb("k_in", [P, 2, T])
        v_in = sb("v_in", [P, T])
        g_in = sb("g_in", [P, T])
        g_sig = sb("g_sig", [P, T])
        silu = sb("silu", [P, T])
        ks = sb("ks", [P, 2, T], F32R)
        q_hi = sb("q_hi", [P, 2, T], F32R)
        q_lo = sb("q_lo", [P, 2, T], F32R)
        v_tok = sb("v_tok", [P, NT, P])
        prob = [sb(f"prob{j}", [P, 2, (U - QB + j + 1) * P]) for j in range(QB)]
        at = [sb(f"at{j}", [P, NT, P]) for j in range(2)]
        on = sb("on", [P, P])
        junk = sb("junk", [P, P])
        y_out = sb("y_out", [P, 2, P])
        ident = sb("ident", [P, P])
        ident_r = sb("ident_r", [P, P], F32R)
        causal = sb("causal", [P, P])
        causal_r = sb("causal_r", [P, P], F32R)
        lam_in = sb("lam_in", [P, 4, DH])
        lam_p = sb("lam_p", [P, 2, DH])
        lam_s = sb("lam_s", [P, 2])
        nlam = sb("nlam", [P, 1])
        norm_c = sb("norm_c", [P, 1])
        epsb = sb("epsb", [P, 1])
        negm = [sb(f"negm{j}", [P, 2, 4]) for j in range(2)]
        sums = [sb(f"sums{j}", [P, 2, 4]) for j in range(2)]
        cf = [sb(f"cf{j}", [P, 2, 4]) for j in range(2)]
        nm = sb("nm", [P, 2])
        dist = sb("dist", [P, 2, 4])
        wts = sb("wts", [P, 2, 4])
        wsum = sb("wsum", [P, 2, 4])
        tot = sb("tot", [P, 2])
        inv = sb("inv", [P, 2])
        ssq = sb("ssq", [P, 1])
        rstd = sb("rstd", [P, 1])
        c_col = sb("c_col", [P, KD])
        c_act = sb("c_act", [P, KD])
        ada_in = [sb(f"ada_in{j}", [P, D]) for j in range(2)]
        ada_sum = sb("ada_sum", [P, D])
        ones = sb("ones", [P, P])
        sc = [ctx.enter_context(nc.psum_tensor(f"C_sc{j}", [P, 2, TG], F32)) for j in range(2)]
        tb = [ctx.enter_context(nc.psum_tensor(f"C_tb{j}", [P, 4, P], F32)) for j in range(2)]
        ob = [ctx.enter_context(nc.psum_tensor(f"C_ob{j}", [P, 4, P], F32)) for j in range(2)]

        consts_in, setup, setup_v = sem("consts_in"), sem("setup"), sem("setup_v")
        qk_loaded, v_loaded, g_loaded = [sem(f"qk_loaded{n}") for n in range(NQ)], sem("v_loaded"), sem("g_loaded")
        hi_ready, lo_ready, vt_ready, v_ready = sem("hi_ready"), sem("lo_ready"), sem("vt_ready"), sem("v_ready")
        gsig_ready, silu_ready = sem("gsig_ready"), sem("silu_ready")
        s_ready, max_ready, exp_done = sem("s_ready"), sem("max_ready"), sem("exp_done")
        d_ready, w_ready, cf_ready, scaled, a_ready = sem("d_ready"), sem("w_ready"), sem("cf_ready"), sem("scaled"), sem("a_ready")
        t_ready, at_ready = sem("t_ready"), sem("at_ready")
        pv_done, rstd_ready, on_ready, ot_ready, y_ready = (sem(n) for n in ("pv_done", "rstd_ready", "on_ready", "ot_ready", "y_ready"))
        y_stored = [sem(f"y_stored{j}") for j in range(2)]
        dchain, achain = sem("dchain"), sem("achain")
        c_sig, c_ready, ones_set = sem("c_sig"), sem("c_ready"), sem("ones_set")
        ada_loaded, rows_loaded, ada_used = [sem(f"ada_loaded{j}") for j in range(2)], sem("rows_loaded"), sem("ada_used")
        gate_ready, post_ready = sem("gate_ready"), sem("post_ready")

        block = ctx.enter_context(nc.Block())

        def unit(h, u):
            return U * h + u

        def piece(h, u, p=0):
            return NP * h + (before[u % U] + NP * (u // U) + p)

        def several(h, u):
            return multi * h + (multi_before[u % U] + multi * (u // U))

        def no_less(count):
            return max(count, 0) if isinstance(count, int) else count

        def width(u, p):
            return min(TG, (u % U + 1) * P - p * TG)

        def keys(u, p):
            return slice(p * TG, p * TG + width(u, p))

        def in_flight(first, last, u):
            return (u < 0 and not first) or (u >= 0 and not last)

        def heads(eng, body):
            body(0, True, False)
            with eng.Fori(1, HEADS) as h:
                body(h, False, False)
            body(HEADS, False, True)

        def each(stage, first, last, u):
            return [(stage, u, p) for p in range(pieces[u % U])] if in_flight(first, last, u) else []

        @block.sync
        def _(sp):
            sp.dma_start(ident[:, :], consts["ident"]).then_inc(consts_in, 16)
            sp.dma_start(causal[:, :], consts["causal"]).then_inc(consts_in, 16)
            sp.dma_start(c_col[:, :], c.rearrange("a (k p) -> p (a k)", p=P), allow_slow_non_contiguous=True).then_inc(consts_in, 16)
            sp.dma_start(lam_in[:, :, :].rearrange("p a d -> p (a d)"),
                         diff_lam.rearrange("a l d -> a (l d)").to_broadcast([P, 4 * DH])).then_inc(consts_in, 16)
            sp.dma_start(norm_c[:, :], diff_norm.rearrange("a p -> p a"), allow_slow_non_contiguous=True).then_inc(consts_in, 16)

            def load_qk(h, tiles, n):
                sp.wait_ge(lo_ready, 2 * NQ * h)
                cols = slice(n * TG, (n + 1) * TG)
                for m in range(2):
                    for half in range(2):
                        rows = slice(DH * half, DH * half + DH)
                        sp.dma_start(k_in[rows, m, cols], pT[bass.ds(tiles[1], 1), DH * m:DH * m + DH, cols].rearrange("a p t -> (a p) t")).then_inc(qk_loaded[n], 16)
                        sp.dma_start(q_in[rows, m, cols], pT[bass.ds(tiles[0], 1), DH * m:DH * m + DH, cols].rearrange("a p t -> (a p) t")).then_inc(qk_loaded[n], 16)

            def load_g(h, tiles):
                sp.wait_ge(silu_ready, 2 * h)
                sp.dma_start(g_in[:, :], pT[bass.ds(tiles[3], 1), :, :].rearrange("a p t -> (a p) t")).then_inc(g_loaded, 16)

            def load_v(h, tiles):
                sp.wait_ge(vt_ready, NQ * h)
                sp.dma_start(v_in[:, :], pT[bass.ds(tiles[2], 1), :, :].rearrange("a p t -> (a p) t")).then_inc(v_loaded, 16)

            def fixed(value):
                return value if isinstance(value, int) else sp.snap(value)

            def tiles_of(h):
                return [fixed(h + n) for n in (20, 24, 28, 32)]

            ada_v = w_ada.rearrange("a (k p) n -> p (a k) n", p=P)

            def body(h, first, last):
                tile, before_tile = fixed(h + 6), fixed(h + 5)
                tiles = None if last else tiles_of(h)
                for s in range(LAGS if last else U):
                    u = s - LAGS
                    k = s - (U - KD - 2)
                    if first and 0 <= k < KD:
                        if k >= 2:
                            sp.wait_ge(ada_used, k - 1)
                        sp.dma_start(ada_in[k % 2][:, :], ada_v[:, k, 2 * D:3 * D]).then_inc(ada_loaded[k % 2], 16)
                    if s == 0 and not (first or last):
                        for n in range(NQ):
                            load_qk(h, tiles, n)
                        load_g(h, tiles)
                        load_v(h, tiles)
                    if in_flight(first, last, u):
                        sp.wait_ge(y_ready, unit(h, u) + 1)
                        sp.dma_start(yT[bass.ds(tile if u >= 0 else before_tile, 1), :, u % U * P:u % U * P + P].rearrange("a p t -> (a p) t"),
                                     y_out[:, u % 2, :]).then_inc(y_stored[u % 2], 16)

            tiles = tiles_of(0)
            load_qk(0, tiles, 0)
            load_g(0, tiles)
            load_v(0, tiles)
            for n in range(1, NQ):
                load_qk(0, tiles, n)
            heads(sp, body)
            sp.wait_ge(vt_ready, NQ * HEADS)
            sp.dma_start(v_in[:, 0:D], b_ada[:, 2 * D:3 * D].to_broadcast([P, D])).then_inc(rows_loaded, 16)
            sp.dma_start(v_in[:, D:2 * D], g_post.to_broadcast([P, D])).then_inc(rows_loaded, 16)
            for j in range(2):
                sp.wait_ge(y_stored[j], 16 * HEADS * U // 2)

        @block.gpsimd
        def _(pool):
            tt = nc.gpsimd.tensor_tensor
            pool.wait_ge(c_sig, 1)
            tt(c_act[:, :], c_act[:, :], c_col[:, :], ALU.mult).then_inc(c_ready, 1)
            nc.gpsimd.memset(ones[:, :], 1.0).then_inc(ones_set, 1)

            def scale(h, u, p):
                if p == 0:
                    pool.wait_ge(cf_ready, unit(h, u) + 1)
                second = prob[u % QB][:, 1, keys(u, p)]
                tt(second, second, cf[u % 2][:, 1, p:p + 1].to_broadcast([P, width(u, p)]), ALU.mult).then_inc(scaled, 1)

            def gates(h, tokens):
                tt(silu[:, tokens], g_sig[:, tokens], g_in[:, tokens], ALU.mult).then_inc(silu_ready, 1)

            def body(h, first, last):
                for s in range(LAGS if last else U):
                    for step in each(scale, first, last, s - 2):
                        step[0](h, step[1], step[2])
                    if s == G_STEP + 2 and not last:
                        pool.wait_ge(gsig_ready, h + 1)
                        pool.wait_ge(y_ready, no_less(unit(h, -4)))
                        gates(h, slice(0, 12 * P))
                    if s == LAGS + 1:
                        pool.wait_ge(y_ready, unit(h, 0))
                        gates(h, slice(12 * P, T))

            heads(pool, body)

        @block.vector
        def _(dve):
            chain = [0]
            base = [0]
            START = 4
            SKIPPED = 5
            PER = sum(5 if p > 1 else 1 for p in pieces)

            def link(ins):
                chain[0] += 1
                ins.then_inc(dchain, 1)

            def linked():
                dve.wait_ge(dchain, base[0] + chain[0])

            tt, ts, stt = nc.vector.tensor_tensor, nc.vector.tensor_scalar, nc.vector.scalar_tensor_tensor
            nc.vector.memset(epsb[:, :], EPS).then_inc(setup_v, 1)
            dve.wait_ge(consts_in, 80)
            nc.vector.tensor_copy(ident_r[:, :], ident[:, :]).then_inc(setup_v, 1)
            nc.vector.tensor_copy(causal_r[:, :], causal[:, :]).then_inc(setup_v, 1)
            lv = lam_in[:, :, :].rearrange("p (a b) d -> p a b d", b=2)
            link(tt(lam_p[:, :, :], lv[:, :, 0, :], lv[:, :, 1, :], ALU.mult))
            linked()
            nc.vector.tensor_reduce(lam_s[:, :], lam_p[:, :, :], AX.X, ALU.add).then_inc(setup_v, 1)
            dve.wait_ge(setup, 1)
            link(tt(nlam[:, :], lam_s[:, 1:2], lam_s[:, 0:1], ALU.subtract))
            linked()
            link(ts(nlam[:, :], nlam[:, :], -LAM_INIT, None, ALU.add))
            link(ts(norm_c[:, :], norm_c[:, :], 1.0 - LAM_INIT, None, ALU.mult))
            linked()
            assert chain[0] == START

            def split(h, n):
                cols = slice(n * TG, (n + 1) * TG)
                dve.wait_ge(hi_ready, 2 * (NQ * h + n) + 1)
                tt(ks[DH:P, :, cols], k_in[DH:P, :, cols], ks[DH:P, :, cols].bitcast(F32), ALU.subtract).then_inc(lo_ready, 1)
                dve.wait_ge(hi_ready, 2 * (NQ * h + n) + 2)
                stt(q_lo[:, :, cols], q_in[:, :, cols], DH ** -0.5, q_hi[:, :, cols].bitcast(F32), ALU.mult,
                    ALU.subtract).then_inc(lo_ready, 1)

            def add_ada(k):
                dve.wait_ge(c_ready, 1)
                dve.wait_ge(ada_loaded[k % 2], 16 * (k // 2 + 1))
                if k == 0:
                    ts(ada_sum[:, :], ada_in[0][:, :], c_act[:, 0:1], None, ALU.mult).then_inc(ada_used, 1)
                else:
                    dve.wait_ge(ada_used, k)
                    stt(ada_sum[:, :], ada_in[k % 2][:, :], c_act[:, k:k + 1], ada_sum[:, :], ALU.mult,
                        ALU.add).then_inc(ada_used, 1)

            def maximum(h, u, p):
                n = before[u] + p
                dve.wait_ge(s_ready, piece(h, u, p) + 1)
                nc.vector.tensor_reduce(negm[u % 2][:, :, p:p + 1], sc[n % 2][:, :, 0:width(u, p)], AX.X, ALU.max,
                                        negate=True).then_inc(max_ready, 1)

            def factors(h, u):
                np_ = pieces[u % U]
                sm, ng, f = sums[u % 2], negm[u % 2], cf[u % 2]

                def largest(h):
                    dve.wait_ge(max_ready, piece(h, u + 1))
                    linked()
                    link(nc.vector.tensor_reduce(nm[:, :], ng[:, :, 0:np_], AX.X, ALU.min))

                def distances(h):
                    linked()
                    tt(dist[:, :, 0:np_], ng[:, :, 0:np_], nm[:, :].unsqueeze(2).to_broadcast([P, 2, np_]),
                       ALU.subtract).then_inc(d_ready, 1)

                def weighted(h):
                    dve.wait_ge(exp_done, 2 * piece(h, u + 1))
                    dve.wait_ge(w_ready, several(h, u) + 1)
                    link(tt(wsum[:, :, 0:np_], wts[:, :, 0:np_], sm[:, :, 0:np_], ALU.mult))

                def total(h):
                    linked()
                    link(nc.vector.tensor_reduce(tot[:, :], wsum[:, :, 0:np_], AX.X, ALU.add))

                def inverse(h):
                    linked()
                    link(nc.vector.reciprocal(inv[:, :], tot[:, :]))

                def with_lambda(h):
                    linked()
                    link(ts(inv[:, 1:2], inv[:, 1:2], nlam[:, :], None, ALU.mult))

                def spread(h):
                    linked()
                    dve.wait_ge(a_ready, no_less(unit(h, u - 1)))
                    tt(f[:, :, 0:np_], wts[:, :, 0:np_], inv[:, :].unsqueeze(2).to_broadcast([P, 2, np_]),
                       ALU.mult).then_inc(cf_ready, 1)

                def single(h):
                    dve.wait_ge(a_ready, no_less(unit(h, u - 1)))
                    dve.wait_ge(exp_done, 2 * piece(h, u + 1))
                    link(nc.vector.reciprocal(f[:, :, 0:1], sm[:, :, 0:1]))

                def single_lambda(h):
                    linked()
                    ts(f[:, 1, 0:1], f[:, 1, 0:1], nlam[:, :], None, ALU.mult).then_inc(cf_ready, 1)

                if np_ == 1:
                    return [single, single_lambda]
                return [largest, distances, weighted, total, inverse, with_lambda, spread]

            def combine(h, u, p):
                dve.wait_ge(scaled, piece(h, u, p) + 1)
                if p == 0:
                    dve.wait_ge(cf_ready, unit(h, u) + 1)
                pr = prob[u % QB]
                ins = stt(pr[:, 0, keys(u, p)], pr[:, 0, keys(u, p)], cf[u % 2][:, 0, p:p + 1], pr[:, 1, keys(u, p)], ALU.mult, ALU.add)
                if p == pieces[u % U] - 1:
                    ins.then_inc(a_ready, 1)

            def normalise(h, u):
                dve.wait_ge(rstd_ready, unit(h, u) + 1)
                dve.wait_ge(ot_ready, unit(h, u))
                ts(on[:, :], ob[u % 2][:, 0, :], rstd[:, :], None, ALU.mult).then_inc(on_ready, 1)

            def gate(h, u):
                dve.wait_ge(ot_ready, unit(h, u) + 1)
                if u % U in (0, 12):
                    dve.wait_ge(silu_ready, 2 * (h + u // U) + 1 + u % U // 12)
                dve.wait_ge(y_stored[u % 2], no_less(16 * (U // 2 * h + u // 2)))
                uu = u % U
                stt(y_out[:, u % 2, :], ob[u % 2][:, 1, :], norm_c[:, :], silu[:, uu * P:(uu + 1) * P], ALU.mult,
                    ALU.mult).then_inc(y_ready, 1)

            def body(h, first, last):
                base[0] = START - SKIPPED + PER * h
                chain[0] = SKIPPED if first else 0
                for s in range(LAGS if last else U):
                    if in_flight(first, last, s - 6):
                        gate(h, s - 6)
                    if s in SPLIT_STEP and not last:
                        split(h, SPLIT_STEP.index(s))
                    large = merged(each(maximum, first, last, s), each(combine, first, last, s - 2))
                    small = [(f,) for f in factors(h, s - 1)] if in_flight(first, last, s - 1) else []
                    if in_flight(first, last, s - 5):
                        small.insert(len(small) // 2, (normalise, s - 5))
                    for step in merged(large, small):
                        step[0](h, *step[1:])
                    if first and s >= U - KD:
                        add_ada(s - (U - KD))
                assert last or chain[0] == PER, (chain[0], PER)

            heads(dve, body)
            dve.wait_ge(gate_ready, 1)
            dve.wait_ge(rows_loaded, 32)
            tt(post[:, :], sc[0][:, :, :].rearrange("p a n -> p (a n)"), v_in[:, 0:D], ALU.add).then_inc(post_ready, 1)
            dve.wait_ge(post_ready, 1)
            tt(post[:, :], post[:, :], v_in[:, D:2 * D], ALU.mult).then_inc(post_ready, 1)

        @block.scalar
        def _(act):
            a = nc.scalar.activation
            act.wait_ge(setup_v, 4)
            a(lam_s[:, :], lam_s[:, :], ACT.Exp).then_inc(setup, 1)
            act.wait_ge(consts_in, 80)
            a(c_act[:, :], c_col[:, :], ACT.Sigmoid).then_inc(c_sig, 1)
            act.preload_act_table_set("natural_log_exp_and_others")

            def split(h, n):
                act.wait_ge(qk_loaded[n], 128 * (h + 1))
                act.wait_ge(s_ready, NP * h)
                cols = slice(n * TG, (n + 1) * TG)
                a(ks[:, :, cols], k_in[:, :, cols], ACT.Copy).then_inc(hi_ready, 1)
                a(q_hi[:, :, cols], q_in[:, :, cols], ACT.Copy, scale=DH ** -0.5).then_inc(hi_ready, 1)

            def exps(h, u, p):
                n = before[u] + p
                act.wait_ge(max_ready, piece(h, u, p) + 1)
                if p == 0:
                    act.wait_ge(t_ready, no_less(piece(h, u - QB + 1)))
                for m in range(2):
                    a(prob[u % QB][:, m, keys(u, p)], sc[n % 2][:, m, 0:width(u, p)], ACT.Exp,
                      bias=negm[u % 2][:, m, p:p + 1], accum_out=sums[u % 2][:, m, p:p + 1]).then_inc(exp_done, 1)

            def weights(h, u):
                np_ = pieces[u % U]
                act.wait_ge(d_ready, several(h, u) + 1)
                a(wts[:, :, 0:np_], dist[:, :, 0:np_], ACT.Exp, scale=-1.0).then_inc(w_ready, 1)

            def evacuate(h, u, p):
                nb = width(u, p) // P
                act.wait_ge(t_ready, piece(h, u, p) + 1)
                if p == 0:
                    act.wait_ge(pv_done, no_less(unit(h, u - 1)))
                a(at[u % 2][:, 4 * p:4 * p + nb, :], tb[(before[u % U] + p) % 2][:, 0:nb, :], ACT.Copy).then_inc(at_ready, 1)

            def root(h, u):
                n = unit(h, u)
                act.wait_ge(pv_done, n + 1)
                act.wait_ge(on_ready, n)
                a(junk[:, :], ob[u % 2][:, 0, :], ACT.Square, accum_out=ssq[:, :]).then_inc(achain, 1)
                act.wait_ge(achain, 2 * n + 1)
                a(ssq[:, :], ssq[:, :], ACT.Ln, bias=epsb[:, :], scale=1.0 / P).then_inc(achain, 1)
                act.wait_ge(achain, 2 * n + 2)
                a(rstd[:, :], ssq[:, :], ACT.Exp, scale=-0.5).then_inc(rstd_ready, 1)

            def body(h, first, last):
                for s in range(LAGS if last else U):
                    if s in SPLIT_STEP and not last:
                        split(h, SPLIT_STEP.index(s))
                    if in_flight(first, last, s - 5):
                        root(h, s - 5)
                    steps = merged(each(exps, first, last, s), each(evacuate, first, last, s - 3))
                    if in_flight(first, last, s - 1) and pieces[(s - 1) % U] > 1:
                        steps.insert(1, (lambda h, u, p: weights(h, u), s - 1, 0))
                    for step in steps:
                        step[0](h, step[1], step[2])
                    if s == G_STEP and not last:
                        act.wait_ge(g_loaded, 16 * (h + 1))
                        act.wait_ge(silu_ready, 2 * h)
                        a(g_sig[:, :], g_in[:, :], ACT.Sigmoid).then_inc(gsig_ready, 1)
                        act.preload_act_table_set("natural_log_exp_and_others")
                    if s == V_STEP and not last:
                        act.wait_ge(pv_done, unit(h, 0))
                        for n in range(NQ):
                            act.wait_ge(vt_ready, NQ * h + n + 1)
                            a(v_tok[:, 4 * n:4 * n + 4, :], tb[n % 2][:, :, :], ACT.Copy).then_inc(v_ready, 1)

            heads(act, body)

        @block.tensor
        def _(pe):
            mm = nc.tensor.matmul
            pe.wait_ge(setup_v, 4)

            def scores(h, u, p):
                n = before[u] + p
                w = width(u, p)
                if p == 0 and u % 4 == 0:
                    pe.wait_ge(lo_ready, 2 * (NQ * h + u // 4 + 1))
                q = slice(u * P, (u + 1) * P)
                for m in range(2):
                    pe.wait_ge(exp_done, no_less(2 * piece(h, u, p) + m - 3))
                    mm(sc[n % 2][:, m, 0:w], q_hi[:, m, q], ks[:, m, keys(u, p)], start=True, stop=False)
                    done = mm(sc[n % 2][:, m, 0:w], q_lo[:, m, q], ks[:, m, keys(u, p)], start=False, stop=True)
                    if p == pieces[u] - 1:
                        done = mm(sc[n % 2][:, m, w - P:w], ident_r[:, :], causal_r[:, :], start=False, stop=True,
                                  skip_group_check=True)
                done.then_inc(s_ready, 1)

            def turn(h, u, p):
                n = before[u % U] + p
                if p == 0:
                    pe.wait_ge(a_ready, unit(h, u) + 1)
                if u == 1:
                    pe.wait_ge(v_ready, NQ * h + NQ)
                pe.wait_ge(at_ready, no_less(piece(h, u, p) - 1))
                for b in range(width(u, p) // P):
                    done = nc.tensor.transpose(tb[n % 2][:, b, :], prob[u % QB][:, 0, p * TG + b * P:p * TG + (b + 1) * P],
                                               ident[:, :])
                done.then_inc(t_ready, 1)

            def values(h, u, p):
                uu = u % U
                if p == 0:
                    pe.wait_ge(y_ready, no_less(unit(h, u - 1)))
                if u == 0:
                    pe.wait_ge(v_ready, NQ * h + NQ)
                pe.wait_ge(at_ready, piece(h, u, p) + 1)
                for b in range(4 * p, min(4 * p + 4, uu + 1)):
                    done = mm(ob[u % 2][:, 0, :], at[u % 2][:, b, :], v_tok[:, b, :], start=(b == 0), stop=(b == uu))
                if p == pieces[uu] - 1:
                    done.then_inc(pv_done, 1)

            def turn_back(h, u):
                pe.wait_ge(on_ready, unit(h, u) + 1)
                nc.tensor.transpose(ob[u % 2][:, 1, :], on[:, :], ident[:, :]).then_inc(ot_ready, 1)

            def body(h, first, last):
                for s in range(LAGS if last else U):
                    for step in merged(each(scores, first, last, s),
                                       merged(each(turn, first, last, s - 3), each(values, first, last, s - 4))):
                        step[0](h, step[1], step[2])
                    if in_flight(first, last, s - 5):
                        turn_back(h, s - 5)
                    if s == V_STEP and not last:
                        pe.wait_ge(v_loaded, 16 * (h + 1))
                        for n in range(NQ):
                            if n < 2:
                                pe.wait_ge(at_ready, piece(h, 1))
                            else:
                                pe.wait_ge(v_ready, NQ * h + n - 1)
                            for b in range(4):
                                done = nc.tensor.transpose(tb[n % 2][:, b, :], v_in[:, (4 * n + b) * P:(4 * n + b + 1) * P], ident[:, :])
                            done.then_inc(vt_ready, 1)

            heads(pe, body)
            pe.wait_ge(ones_set, 1)
            pe.wait_ge(ada_used, KD)
            pe.wait_ge(exp_done, 2 * NP * HEADS)
            for m in range(2):
                done = mm(sc[0][:, m, :], ones[:, :], ada_sum[:, m * TG:(m + 1) * TG], start=True, stop=True)
            done.then_inc(gate_ready, 1)


def merged(top, rest):
    out, done = [], 0
    for n, step in enumerate(top):
        out.append(step)
        until = len(rest) * (n + 1) // len(top)
        out += rest[done:until]
        done = until
    return out + rest[done:]


BRANCH_CHUNKS = ((0, 2), (2, 4), (4, 6), (6, 10))
YC = 10


def merge_and_output(nc, x, w_merge, w_out, gT, yT, post, out):
    with ExitStack() as ctx:
        def sb(name, shape, dt=F32):
            return ctx.enter_context(nc.sbuf_tensor("D_" + name, shape, dt))

        def sem(name):
            return ctx.enter_context(nc.semaphore("D_" + name))

        GB = 4
        wo_stage = sb("wo_stage", [P, D])
        wo_hi = sb("wo_hi", [P, KD, D], F32R)
        wo_lo = sb("wo_lo", [P, KD, D], F32R)
        wm_stage = [sb(f"wm_stage{j}", [P, YC, P]) for j in range(2)]
        wm_hi = [sb(f"wm_hi{j}", [P, YC, P], F32R) for j in range(2)]
        wm_lo = [sb(f"wm_lo{j}", [P, YC, P], F32R) for j in range(2)]
        y_stage = [sb(f"y_stage{j}", [P, TG]) for j in range(2)]
        y_hi = sb("y_hi", [P, YC, TG], F32R)
        y_lo = sb("y_lo", [P, YC, TG], F32R)
        m_hi = sb("m_hi", [P, KD, TG], F32R)
        m_lo = sb("m_lo", [P, KD, TG], F32R)
        gate = [sb(f"gate{j}", [P, 4, TG]) for j in range(GB)]
        x_in = sb("x_in", [P, D])
        o_buf = [sb(f"o_buf{j}", [P, D]) for j in range(2)]
        ss = sb("ss", [P, 1])
        rstd = sb("rstd", [P, 1])
        epsb = sb("epsb", [P, 1])
        mb = [ctx.enter_context(nc.psum_tensor(f"D_mb{b}", [P, TG], F32)) for b in range(4)]
        pb = [ctx.enter_context(nc.psum_tensor(f"D_pb{j}", [P, D], F32)) for j in range(2)]

        y_first = [y_stage[k] if k < 2 else gate[2 + (k - 2) // 4][:, (k - 2) % 4, :] for k in range(YC)]
        y_first_loaded = [sem(f"y_first_loaded{j}") for j in range(2)]
        eps_set, wo_loaded, wo_hi_ready, wo_lo_ready = sem("eps_set"), sem("wo_loaded"), sem("wo_hi_ready"), sem("wo_lo_ready")
        wm_loaded, wm_hi_ready, wm_lo_ready = [sem(f"wm_loaded{j}") for j in range(2)], sem("wm_hi_ready"), sem("wm_lo_ready")
        y_loaded, y_hi_ready, y_lo_ready = [sem(f"y_loaded{j}") for j in range(2)], sem("y_hi_ready"), sem("y_lo_ready")
        g_loaded, g_ready, merged_done, mul_done = [sem(f"g_loaded{j}") for j in range(GB)], sem("g_ready"), sem("merged_done"), sem("mul_done")
        paired, added, m_hi_ready, m_lo_ready, p_done, squared, logged, rstd_ready, scaled, out_ready = (
            sem(n) for n in ("paired", "added", "m_hi_ready", "m_lo_ready", "p_done", "squared", "logged", "rstd_ready", "scaled", "out_ready"))
        x_loaded, out_stored = sem("x_loaded"), [sem(f"out_stored{j}") for j in range(2)]
        block = ctx.enter_context(nc.Block())
        wo_v = w_out.rearrange("a (k p) n -> p (a k) n", p=P)
        TB = TG // P
        Y_SPLITS = ((4,), (5, 6), (7, 8), (9,))

        def groups(eng, body):
            body(0, True, False)
            with eng.Fori(1, NG - 1) as g:
                body(g, False, False)
            body(NG - 1, False, True)

        @block.sync
        def _(sp):
            def fixed(value):
                return value if isinstance(value, int) else sp.snap(value)

            def load_wm(n, d):
                if not (isinstance(n, int) and n < 2):
                    sp.wait_ge(wm_hi_ready, n - 1)
                    sp.wait_ge(wm_lo_ready, n - 1)
                for w, (c0, c1) in zip(w_merge, BRANCH_CHUNKS):
                    sp.dma_start(wm_stage[d % 2][:, c0:c1, :], w[0, :, d * P:(d + 1) * P].rearrange("(k p) n -> p k n", p=P)).then_inc(wm_loaded[d % 2], 16)

            def load_gates(n, d, at):
                if not (isinstance(n, int) and n < GB):
                    sp.wait_ge(m_lo_ready, n - GB + 1)
                elif n >= 2:
                    sp.wait_ge(y_lo_ready, 4 * n - 2)
                    sp.wait_ge(y_hi_ready, 4 * n - 2)
                sp.dma_start(gate[d % GB][:, :, :], gT[d:d + 3 * KD + 1:KD, :, bass.ds(at, TG)].rearrange("n p t -> p n t")).then_inc(g_loaded[d % GB], 16)

            def load_y(g, k, at):
                if not (isinstance(g, int) and g == 0):
                    sp.wait_ge(y_hi_ready, YC * g + k - 1)
                    sp.wait_ge(y_lo_ready, YC * g + k - 1)
                sp.dma_start(y_stage[k % 2][:, :], yT[k, :, bass.ds(at, TG)]).then_inc(y_loaded[k % 2], 16)

            def load_wo(k):
                if k:
                    sp.wait_ge(wo_hi_ready, k)
                    sp.wait_ge(wo_lo_ready, k)
                sp.dma_start(wo_stage[:, :], wo_v[:, k, :]).then_inc(wo_loaded, 16)

            def store(n, b, row):
                sp.wait_ge(out_ready, n + 1)
                sp.dma_start(out[0, bass.ds(row, P), :], o_buf[b % 2][:, :]).then_inc(out_stored[b % 2], 16)

            def body(g, first, last):
                at = fixed(g * TG)
                at_next = fixed(g * TG + TG)
                rows = [fixed(g * TG + b * P) for b in range(TB)]
                row_before = None if first else fixed(g * TG - P)
                for d in range(KD):
                    n = KD * g + d
                    if not (last and d + 2 >= KD):
                        load_wm(n + 2, (d + 2) % KD)
                        load_gates(n + 2, (d + 2) % KD, at if d + 2 < KD else at_next)
                    if first:
                        load_wo(d)
                    if d == 1 and not first:
                        store(TB * g - 1, TB - 1, row_before)
                for b in range(TB):
                    sp.wait_ge(out_ready, TB * g + b)
                    sp.dma_start(x_in[:, :], x[0, bass.ds(rows[b], P), :]).then_inc(x_loaded, 16)
                    if b == 0 and not last:
                        for k in range(YC):
                            load_y(g + 1, k, at_next)
                    if b:
                        store(TB * g + b - 1, b - 1, rows[b - 1])

            for k in range(2):
                load_y(0, k, 0)
            load_wm(0, 0)
            for j in range(2):
                sp.dma_start(gate[2 + j][:, :, :], yT[4 * j + 2:4 * j + 6, :, 0:TG].rearrange("n p t -> p n t")).then_inc(y_first_loaded[j], 16)
            load_gates(0, 0, 0)
            load_wm(1, 1)
            load_gates(1, 1, 0)
            groups(sp, body)
            store(NT - 1, TB - 1, (NT - 1) * P)
            for j in range(2):
                sp.wait_ge(out_stored[j], 16 * NT // 2)

        @block.gpsimd
        def _(pool):
            tt = nc.gpsimd.tensor_tensor

            def body(g, first, last):
                for d in range(KD):
                    n = KD * g + d
                    if first:
                        pool.wait_ge(wo_hi_ready, d + 1)
                        tt(wo_lo[:, d, :], wo_stage[:, :], wo_hi[:, d, :].bitcast(F32), ALU.subtract).then_inc(wo_lo_ready, 1)
                    pool.wait_ge(mul_done, 4 * n + 4)
                    s = gate[d % GB]
                    tt(s[:, 0:2, :], s[:, 0:2, :], s[:, 2:4, :], ALU.add).then_inc(paired, 1)
                    pool.wait_ge(paired, n + 1)
                    tt(s[:, 0, :], s[:, 0, :], s[:, 1, :], ALU.add).then_inc(added, 1)
                for b in range(TB):
                    n = TB * g + b
                    pool.wait_ge(scaled, n + 1)
                    pool.wait_ge(x_loaded, 16 * (n + 1))
                    tt(o_buf[b % 2][:, :], o_buf[b % 2][:, :], x_in[:, :], ALU.add).then_inc(out_ready, 1)

            groups(pool, body)

        @block.vector
        def _(dve):
            tt, stt = nc.vector.tensor_tensor, nc.vector.scalar_tensor_tensor
            nc.vector.memset(epsb[:, :], EPS).then_inc(eps_set, 1)

            def split_wm(n, d):
                dve.wait_ge(wm_hi_ready, n + 1)
                tt(wm_lo[d % 2][:, :, :], wm_stage[d % 2][:, :, :], wm_hi[d % 2][:, :, :].bitcast(F32), ALU.subtract).then_inc(wm_lo_ready, 1)

            def split_y(g, k):
                dve.wait_ge(y_hi_ready, YC * g + k + 1)
                stage = y_first[k] if isinstance(g, int) and g == 0 else y_stage[k % 2]
                tt(y_lo[:, k, :], stage[:, :], y_hi[:, k, :].bitcast(F32), ALU.subtract).then_inc(y_lo_ready, 1)

            def low(n, d):
                dve.wait_ge(m_hi_ready, n + 1)
                tt(m_lo[:, d, :], gate[d % GB][:, 0, :], m_hi[:, d, :].bitcast(F32), ALU.subtract).then_inc(m_lo_ready, 1)

            def body(g, first, last):
                for d in range(KD):
                    n = KD * g + d
                    if d + 1 < KD:
                        split_wm(n + 1, d + 1)
                    dve.wait_ge(g_ready, n + 1)
                    for b in range(4):
                        dve.wait_ge(merged_done, 4 * n + b + 1)
                        s = gate[d % GB]
                        tt(s[:, b, :], mb[b][:, :], s[:, b, :], ALU.mult).then_inc(mul_done, 1)
                        if b == 1 and d:
                            low(n - 1, d - 1)
                if not last:
                    for k in range(4):
                        split_y(g + 1, k)
                low(KD * g + KD - 1, KD - 1)
                for b in range(TB):
                    if not last:
                        for k in Y_SPLITS[b]:
                            split_y(g + 1, k)
                        if b == TB - 1:
                            split_wm(KD * g + KD, 0)
                    n = TB * g + b
                    dve.wait_ge(rstd_ready, n + 1)
                    dve.wait_ge(out_stored[b % 2], 16 * (TB // 2 * g + b // 2))
                    stt(o_buf[b % 2][:, :], pb[b % 2][:, :], rstd[:, :], post[:, :], ALU.mult, ALU.mult).then_inc(scaled, 1)

            for k in range(2):
                split_y(0, k)
            split_wm(0, 0)
            for k in range(2, YC):
                split_y(0, k)
            groups(dve, body)

        @block.scalar
        def _(act):
            a = nc.scalar.activation

            def split_wm(g, n, d):
                act.wait_ge(wm_loaded[d % 2], 64 * (KD // 2 * g + d // 2 + 1))
                if not (isinstance(n, int) and n < 2):
                    act.wait_ge(merged_done, 4 * (n - 1))
                a(wm_hi[d % 2][:, :, :], wm_stage[d % 2][:, :, :], ACT.Copy).then_inc(wm_hi_ready, 1)

            def split_y(g, k):
                start = isinstance(g, int) and g == 0
                if start and k >= 2:
                    act.wait_ge(y_first_loaded[(k - 2) // 4], 16)
                elif start:
                    act.wait_ge(y_loaded[k], 16)
                else:
                    act.wait_ge(y_loaded[k % 2], 16 * (YC // 2 * g + k // 2 + 2 - YC // 2))
                if k == 0:
                    act.wait_ge(merged_done, 4 * KD * g)
                stage = y_first[k] if start else y_stage[k % 2]
                a(y_hi[:, k, :], stage[:, :], ACT.Copy).then_inc(y_hi_ready, 1)

            def sigmoids(g, n, d):
                act.wait_ge(g_loaded[d % GB], 16 * (KD // GB * g + d // GB + 1))
                a(gate[d % GB][:, :, :], gate[d % GB][:, :, :], ACT.Sigmoid).then_inc(g_ready, 1)

            def high(g, d):
                act.wait_ge(added, KD * g + d + 1)
                if d == 0:
                    act.wait_ge(p_done, TB * g)
                a(m_hi[:, d, :], gate[d % GB][:, 0, :], ACT.Copy).then_inc(m_hi_ready, 1)

            def body(g, first, last):
                for d in range(KD):
                    n = KD * g + d
                    if d + 1 < KD:
                        split_wm(g, n + 1, d + 1)
                        sigmoids(g, n + 1, d + 1)
                    if first:
                        act.wait_ge(wo_loaded, 16 * (d + 1))
                        a(wo_hi[:, d, :], wo_stage[:, :], ACT.Copy).then_inc(wo_hi_ready, 1)
                    if d:
                        high(g, d - 1)
                if not last:
                    for k in range(4):
                        split_y(g + 1, k)
                high(g, KD - 1)
                act.preload_act_table_set("natural_log_exp_and_others")
                for b in range(TB):
                    if not last:
                        for k in Y_SPLITS[b]:
                            split_y(g + 1, k)
                        if b == TB - 1:
                            split_wm(g + 1, KD * g + KD, 0)
                    n = TB * g + b
                    act.wait_ge(p_done, n + 1)
                    act.wait_ge(scaled, n)
                    if first:
                        act.wait_ge(wo_lo_ready, KD)
                    a(wo_stage[:, :], pb[b % 2][:, :], ACT.Square, accum_out=ss[:, :]).then_inc(squared, 1)
                    act.wait_ge(squared, n + 1)
                    a(ss[:, :], ss[:, :], ACT.Ln, bias=epsb[:, :], scale=1.0 / D).then_inc(logged, 1)
                    act.wait_ge(logged, n + 1)
                    a(rstd[:, :], ss[:, :], ACT.Exp, scale=-0.5).then_inc(rstd_ready, 1)
                if not last:
                    sigmoids(g + 1, KD * g + KD, 0)

            act.wait_ge(eps_set, 1)
            for k in range(2):
                split_y(0, k)
            split_wm(0, 0, 0)
            for k in range(2, YC):
                split_y(0, k)
                if k == 3:
                    sigmoids(0, 0, 0)
            groups(act, body)

        @block.tensor
        def _(pe):
            mm = nc.tensor.matmul

            def output(g, b, half, k):
                tok = slice(b * P, (b + 1) * P)
                cols = slice(half * TG, (half + 1) * TG)
                mm(pb[b % 2][:, cols], m_hi[:, k, tok], wo_hi[:, k, cols], start=(k == 0), stop=False)
                mm(pb[b % 2][:, cols], m_hi[:, k, tok], wo_lo[:, k, cols], start=False, stop=False)
                return mm(pb[b % 2][:, cols], m_lo[:, k, tok], wo_hi[:, k, cols], start=False, stop=(k == KD - 1))

            def body(g, first, last):
                for d in range(KD):
                    n = KD * g + d
                    pe.wait_ge(wm_lo_ready, n + 1)
                    for b, (c0, c1) in enumerate(BRANCH_CHUNKS):
                        if not (first and d == 0):
                            pe.wait_ge(mul_done, 4 * n + b - 3)
                        if d == 0:
                            pe.wait_ge(y_lo_ready, YC * g + c1)
                        for k in range(c0, c1):
                            mm(mb[b][:, :], wm_hi[d % 2][:, k, :], y_hi[:, k, :], start=(k == c0), stop=False)
                            mm(mb[b][:, :], wm_hi[d % 2][:, k, :], y_lo[:, k, :], start=False, stop=False)
                            done = mm(mb[b][:, :], wm_lo[d % 2][:, k, :], y_hi[:, k, :], start=False, stop=(k == c1 - 1))
                        done.then_inc(merged_done, 1)
                if first:
                    pe.wait_ge(wo_lo_ready, KD)
                for b in range(TB):
                    n = TB * g + b
                    if not (first and b < 2):
                        pe.wait_ge(scaled, n - 1)
                    if b == 0:
                        pe.wait_ge(m_lo_ready, KD * g + KD - 2)
                        for half in range(2):
                            for k in range(KD - 2):
                                output(g, b, half, k)
                        pe.wait_ge(m_lo_ready, KD * g + KD)
                        for half in range(2):
                            for k in range(KD - 2, KD):
                                done = output(g, b, half, k)
                    else:
                        for half in range(2):
                            for k in range(KD):
                                done = output(g, b, half, k)
                    done.then_inc(p_done, 1)

            groups(pe, body)


def constants():
    i = np.arange(P)
    same_head = (i[:, None] // 64 == i[None, :] // 64).astype(np.float32)
    masks = np.zeros((P, NL, P), np.float32)
    for n, m in enumerate(LEVELS):
        s, t = i[:, None], i[None, :]
        masks[:, n, :] = (s // (2 * m) == t // (2 * m)) & (s % (2 * m) < m) & (t % (2 * m) >= m)
    masks[:, NL - 1, :] = np.eye(P)
    scan = np.ones((P, 2, P), np.float32)
    scan[:, :, 0] = 0
    windows = np.array([[2, 8], [4, 16]])[i // 64]
    inv_first = 1.0 / np.minimum(i[None, None, :] + 1, windows[:, :, None])
    return {
        "causal": np.where(i[None, :] <= i[:, None], 0.0, NEG).astype(np.float32),
        "ident": np.eye(P, dtype=np.float32),
        "mean_w": same_head / 64,
        "head_m": same_head,
        "masks": masks,
        "scan_m": scan.reshape(P, 2 * P),
        "inv_first": inv_first.astype(np.float32),
        "inv_count": (1.0 / windows).astype(np.float32),
    }


def hybrid_trunk(nc, A, consts, out):
    pT = nc.dram_tensor("pT_scratch", [MIX_TILES, P, T], F32).ap()
    gT = nc.dram_tensor("gT_scratch", [GATE_TILES, P, T], F32).ap()
    yT = nc.dram_tensor("yT_scratch", [YC, P, T], F32).ap()
    with ExitStack() as ctx:
        h_hi = ctx.enter_context(nc.sbuf_tensor("h_hi", [P, KD, T], F32R))
        h_lo = ctx.enter_context(nc.sbuf_tensor("h_lo", [P, KD, T], F32R))
        project_mixer_inputs(nc, A["x"], A["c"], A["w_ada"], A["b_ada"], A["g_pre"], A["w_in"], consts["ident"], h_hi, h_lo, pT)
        gates_and_local_mixers(nc, A["w_in"], h_hi, h_lo, pT, gT, yT, consts, A["hgrn_lb"], A["hgrn_norm"], A["conv_w"],
                               A["pool_w"], A["pool_scale"])
    with ExitStack() as ctx:
        post = ctx.enter_context(nc.sbuf_tensor("post", [P, D], F32))
        differential_attention(nc, pT, yT, consts, A["diff_lam"], A["diff_norm"], A["c"], A["w_ada"], A["b_ada"], A["g_post"], post)
        merge_and_output(nc, A["x"], [A[f"w_merge_{b}"] for b in ("pool", "hgrn", "conv", "diff")], A["w_out"], gT, yT, post, out)


NAMES = ["x", "c", "w_ada", "b_ada", "g_pre", "g_post", "w_in", "pool_w", "pool_scale", "hgrn_lb", "hgrn_norm", "conv_w",
         "diff_lam", "diff_norm", "w_merge_pool", "w_merge_hgrn", "w_merge_conv", "w_merge_diff", "w_out"]


def kernel(**inputs):
    import concourse.bacc as bacc
    from concourse.bass_utils import run_bass_kernel_spmd

    nc = bacc.Bacc("TRN2", target_bir_lowering=False, num_devices=1, dynamic_dma_scratch_size=1024)
    arrays = {}

    def declare(name, array):
        array = np.ascontiguousarray(array)
        arrays[name + "_dram"] = array
        return nc.dram_tensor(name + "_dram", array.shape, mybir.dt.from_np(array.dtype), kind="ExternalInput").ap()

    inputs_ap = {n: declare("in_" + n, np.asarray(inputs[n])) for n in NAMES}
    consts_ap = {n: declare("const_" + n, a) for n, a in constants().items()}
    out = nc.dram_tensor("out_dram", (1, T, D), F32, kind="ExternalOutput").ap()
    hybrid_trunk(nc, inputs_ap, consts_ap, out)
    result = run_bass_kernel_spmd(nc, [arrays], core_ids=[0])
    return result.results[0]["out_dram"]
```
